# Optimizing a Trainium2 kernel written in Bass

```python
import jax, jax.numpy as jnp
from jax import lax
import numpy as np

D_MODEL = 1024
BATCH = 1
SEQ = 1024
DEPTH = 1
DEC_BATCH = 8
DEC_SEQ = 16
PAST_LEN = 512

CHUNK = 64
Q_BLOCK = 128
EPS = 1e-6
M_HEAD_DIM = 64
M_INNER = D_MODEL
M_HEADS = M_INNER // M_HEAD_DIM
M_GROUPS = 4
M_HPG = M_HEADS // M_GROUPS
M_STATE = 128
CONV_W = 4
CONV_DIM = M_INNER + 2 * M_GROUPS * M_STATE
SB_HEAD_DIM = 64
SB_HEADS = D_MODEL // SB_HEAD_DIM
SB_WIDTH = SB_HEADS * SB_HEAD_DIM
SB_SCALE = SB_HEAD_DIM ** -0.5
D_FF = -(-8 * D_MODEL // (3 * 256)) * 256
PLE_DIM = 256
OFF_Z = 0
OFF_XBC = OFF_Z + M_INNER
OFF_DT = OFF_XBC + CONV_DIM
OFF_Q = OFF_DT + M_HEADS
OFF_K = OFF_Q + SB_WIDTH
OFF_V = OFF_K + SB_WIDTH
OFF_GA = OFF_V + SB_WIDTH
OFF_GB = OFF_GA + D_MODEL
IN_COLS = OFF_GB + D_MODEL

kernel_name = "ssd_stickbreaking_gated_hybrid_step"

def rmsnorm(x, g):
    xf = x.astype(jnp.float32)
    xf = xf * lax.rsqrt(jnp.mean(xf * xf, axis=-1, keepdims=True) + EPS)
    return (xf * g.astype(jnp.float32)).astype(x.dtype)

def ssd_scan(x, dt, a_head, b_mat, c_mat, h0):
    bsz, L = x.shape[0], x.shape[1]
    q = L if L <= CHUNK else CHUNK
    nc = L // q
    x = x.reshape(bsz, nc, q, M_GROUPS, M_HPG, M_HEAD_DIM)
    dt = dt.reshape(bsz, nc, q, M_GROUPS, M_HPG)
    bm = b_mat.reshape(bsz, nc, q, M_GROUPS, M_STATE)
    cm = c_mat.reshape(bsz, nc, q, M_GROUPS, M_STATE)
    acum = jnp.cumsum(dt * a_head, axis=2)
    causal = jnp.tril(jnp.ones((q, q), dtype=bool))[None, None, :, :, None, None]
    seg = acum[:, :, :, None] - acum[:, :, None, :]
    decay = jnp.exp(jnp.where(causal, seg, -jnp.inf))
    cb = jnp.einsum('bclgn,bcsgn->bclsg', cm, bm)
    y_diag = jnp.einsum('bclsg,bclsgr,bcsgr,bcsgrp->bclgrp', cb, decay, dt, x)
    decay_end = jnp.exp(acum[:, :, -1:] - acum)
    states = jnp.einsum('bclgn,bclgr,bclgrp->bcgrpn', bm, decay_end * dt, x)
    chunk_decay = jnp.exp(acum[:, :, -1])

    def step(h, inp):
        s_c, d_c = inp
        return d_c[..., None, None] * h + s_c, h

    h_last, h_in = lax.scan(step, h0, (jnp.moveaxis(states, 1, 0), jnp.moveaxis(chunk_decay, 1, 0)))
    h_in = jnp.moveaxis(h_in, 0, 1)
    y_off = jnp.einsum('bclgn,bcgrpn,bclgr->bclgrp', cm, h_in, jnp.exp(acum))
    y = (y_diag + y_off).reshape(bsz, L, M_GROUPS, M_HPG, M_HEAD_DIM)
    return y, h_last

def sb_block(qb, qpos, k, v):
    kpos = jnp.arange(k.shape[2])
    z = jnp.einsum('bhtd,bhsd->bhts', qb, k) * SB_SCALE
    mask = (kpos[None, :] < qpos[:, None])[None, None]
    log_keep = jnp.where(mask, jax.nn.log_sigmoid(-z), 0.0)
    after = lax.cumsum(log_keep, axis=3, reverse=True) - log_keep
    w = jnp.where(mask, jnp.exp(jax.nn.log_sigmoid(z) + after), 0.0)
    return jnp.einsum('bhts,bhsd->bhtd', w, v)

def sb_attention(q, k, v, q_offset):
    bsz, nh, lq, hd = q.shape
    qpos = q_offset + jnp.arange(lq)
    if lq <= Q_BLOCK:
        return sb_block(q, qpos, k, v)
    nb = lq // Q_BLOCK
    qb = jnp.moveaxis(q.reshape(bsz, nh, nb, Q_BLOCK, hd), 2, 0)
    out = lax.map(lambda a: sb_block(a[0], a[1], k, v), (qb, qpos.reshape(nb, Q_BLOCK)))
    return jnp.moveaxis(out, 0, 2).reshape(bsz, nh, lq, hd)

def hybrid_layer(x, p, past_k, past_v, conv_hist, h0, norm_mix_g, w_in, conv_w, conv_b, dt_bias,
                 a_log, d_skip, mnorm_g, w_a, w_b, w_out, norm_ffn_g, w_gate, w_up, w_down,
                 norm_ple_g, w_ple_gate, w_ple):
    f32 = jnp.float32
    bsz, L, _ = x.shape
    h = rmsnorm(x, norm_mix_g)
    proj = h @ w_in
    z = proj[..., OFF_Z:OFF_XBC]
    xbc_raw = proj[..., OFF_XBC:OFF_DT]
    dt_raw = proj[..., OFF_DT:OFF_Q]
    q = proj[..., OFF_Q:OFF_K].reshape(bsz, L, SB_HEADS, SB_HEAD_DIM).transpose(0, 2, 1, 3)
    k = proj[..., OFF_K:OFF_V].reshape(bsz, L, SB_HEADS, SB_HEAD_DIM).transpose(0, 2, 1, 3)
    v = proj[..., OFF_V:OFF_GA].reshape(bsz, L, SB_HEADS, SB_HEAD_DIM).transpose(0, 2, 1, 3)
    gate_a = proj[..., OFF_GA:OFF_GB]
    gate_b = proj[..., OFF_GB:IN_COLS]

    xpad = jnp.concatenate([conv_hist.astype(xbc_raw.dtype), xbc_raw], axis=1)
    new_conv = xpad[:, xpad.shape[1] - (CONV_W - 1):]
    xbc = lax.conv_general_dilated(xpad, conv_w[:, None, :].astype(xpad.dtype), (1,), 'VALID',
                                   dimension_numbers=('NWC', 'WIO', 'NWC'),
                                   feature_group_count=CONV_DIM) + conv_b
    xbc = jax.nn.silu(xbc.astype(f32))
    xs = xbc[..., :M_INNER].reshape(bsz, L, M_GROUPS, M_HPG, M_HEAD_DIM)
    bm = xbc[..., M_INNER:M_INNER + M_GROUPS * M_STATE].reshape(bsz, L, M_GROUPS, M_STATE)
    cm = xbc[..., M_INNER + M_GROUPS * M_STATE:].reshape(bsz, L, M_GROUPS, M_STATE)
    dt = jax.nn.softplus(dt_raw.astype(f32) + dt_bias.astype(f32)).reshape(bsz, L, M_GROUPS, M_HPG)
    a_head = -jnp.exp(a_log.astype(f32)).reshape(M_GROUPS, M_HPG)
    h0g = h0.astype(f32).reshape(bsz, M_GROUPS, M_HPG, M_HEAD_DIM, M_STATE)
    y, h_last = ssd_scan(xs, dt, a_head, bm, cm, h0g)
    y = y + d_skip.astype(f32).reshape(M_GROUPS, M_HPG)[:, :, None] * xs
    y = (y.reshape(bsz, L, M_INNER) * jax.nn.silu(z.astype(f32))).reshape(bsz, L, M_GROUPS, M_INNER // M_GROUPS)
    y = y * lax.rsqrt(jnp.mean(y * y, axis=-1, keepdims=True) + EPS)
    y = y.reshape(bsz, L, M_INNER) * mnorm_g.astype(f32)
    branch_a = y.astype(x.dtype) @ w_a
    new_ssm = h_last.reshape(bsz, M_HEADS, M_HEAD_DIM, M_STATE)

    k_all = jnp.concatenate([past_k.astype(k.dtype), k], axis=2)
    v_all = jnp.concatenate([past_v.astype(v.dtype), v], axis=2)
    o = sb_attention(q.astype(f32), k_all.astype(f32), v_all.astype(f32), past_k.shape[2])
    o = o.transpose(0, 2, 1, 3).reshape(bsz, L, SB_WIDTH).astype(x.dtype)
    branch_b = o @ w_b

    merged = jax.nn.sigmoid(gate_a) * branch_a + jax.nn.sigmoid(gate_b) * branch_b
    x = x + merged @ w_out

    hf = rmsnorm(x, norm_ffn_g)
    x = x + (jax.nn.silu(hf @ w_gate) * (hf @ w_up)) @ w_down

    g = jax.nn.sigmoid(rmsnorm(x, norm_ple_g) @ w_ple_gate)
    x = x + g * (p.astype(x.dtype) @ w_ple)
    return x, k, v, new_conv, new_ssm

def setup_inputs(seed: int = 0) -> dict:
    key = jax.random.key(seed)
    ks = jax.random.split(key, 32)
    nrm = lambda k, s, sc: jax.random.normal(k, s, jnp.float32) * sc
    dt0 = jnp.exp(jax.random.uniform(ks[12], (DEPTH, M_HEADS), jnp.float32, np.log(1e-3), np.log(1e-1)))
    return {
        "x_prompt": nrm(ks[0], (BATCH, SEQ, D_MODEL), 1.0),
        "x_sample": nrm(ks[1], (DEC_BATCH, DEC_SEQ, D_MODEL), 1.0),
        "cache_k": nrm(ks[2], (DEPTH, DEC_BATCH, SB_HEADS, PAST_LEN, SB_HEAD_DIM), 1.0),
        "cache_v": nrm(ks[3], (DEPTH, DEC_BATCH, SB_HEADS, PAST_LEN, SB_HEAD_DIM), 1.0),
        "state_conv": nrm(ks[4], (DEPTH, DEC_BATCH, CONV_W - 1, CONV_DIM), 1.0),
        "state_ssm": nrm(ks[5], (DEPTH, DEC_BATCH, M_HEADS, M_HEAD_DIM, M_STATE), 0.1),
        "p_prompt": nrm(ks[6], (DEPTH, BATCH, SEQ, PLE_DIM), 1.0),
        "p_sample": nrm(ks[7], (DEPTH, DEC_BATCH, DEC_SEQ, PLE_DIM), 1.0),
        "norm_mix_g": 1.0 + nrm(ks[8], (DEPTH, D_MODEL), 0.02),
        "w_in": nrm(ks[9], (DEPTH, D_MODEL, IN_COLS), D_MODEL ** -0.5),
        "conv_w": nrm(ks[10], (DEPTH, CONV_W, CONV_DIM), CONV_W ** -0.5),
        "conv_b": nrm(ks[11], (DEPTH, CONV_DIM), 0.02),
        "dt_bias": dt0 + jnp.log(-jnp.expm1(-dt0)),
        "a_log": jnp.log(jax.random.uniform(ks[13], (DEPTH, M_HEADS), jnp.float32, 1.0, 16.0)),
        "d_skip": 1.0 + nrm(ks[14], (DEPTH, M_HEADS), 0.1),
        "mnorm_g": 1.0 + nrm(ks[15], (DEPTH, M_INNER), 0.02),
        "w_a": nrm(ks[16], (DEPTH, M_INNER, D_MODEL), M_INNER ** -0.5),
        "w_b": nrm(ks[17], (DEPTH, SB_WIDTH, D_MODEL), SB_WIDTH ** -0.5),
        "w_out": nrm(ks[18], (DEPTH, D_MODEL, D_MODEL), D_MODEL ** -0.5),
        "norm_ffn_g": 1.0 + nrm(ks[19], (DEPTH, D_MODEL), 0.02),
        "w_gate": nrm(ks[20], (DEPTH, D_MODEL, D_FF), D_MODEL ** -0.5),
        "w_up": nrm(ks[21], (DEPTH, D_MODEL, D_FF), D_MODEL ** -0.5),
        "w_down": nrm(ks[22], (DEPTH, D_FF, D_MODEL), D_FF ** -0.5),
        "norm_ple_g": 1.0 + nrm(ks[23], (DEPTH, D_MODEL), 0.02),
        "w_ple_gate": nrm(ks[24], (DEPTH, D_MODEL, D_MODEL), D_MODEL ** -0.5),
        "w_ple": nrm(ks[25], (DEPTH, PLE_DIM, D_MODEL), PLE_DIM ** -0.5),
        "final_norm_g": 1.0 + nrm(ks[26], (D_MODEL,), 0.02),
    }

def reference(x_prompt, x_sample, cache_k, cache_v, state_conv, state_ssm, p_prompt, p_sample,
              norm_mix_g, w_in, conv_w, conv_b, dt_bias, a_log, d_skip, mnorm_g, w_a, w_b, w_out,
              norm_ffn_g, w_gate, w_up, w_down, norm_ple_g, w_ple_gate, w_ple, final_norm_g):
    bp = x_prompt.shape[0]
    xp, xs = x_prompt, x_sample
    kp_l, vp_l, cp_l, sp_l = [], [], [], []
    ks_l, vs_l, cs_l, ss_l = [], [], [], []
    for i in range(DEPTH):
        w = (norm_mix_g[i], w_in[i], conv_w[i], conv_b[i], dt_bias[i], a_log[i], d_skip[i], mnorm_g[i],
             w_a[i], w_b[i], w_out[i], norm_ffn_g[i], w_gate[i], w_up[i], w_down[i],
             norm_ple_g[i], w_ple_gate[i], w_ple[i])
        empty_kv = jnp.zeros((bp, SB_HEADS, 0, SB_HEAD_DIM), xp.dtype)
        zero_conv = jnp.zeros((bp, CONV_W - 1, CONV_DIM), xp.dtype)
        zero_ssm = jnp.zeros((bp, M_HEADS, M_HEAD_DIM, M_STATE), jnp.float32)
        xp, kp, vp, cp, sp = hybrid_layer(xp, p_prompt[i], empty_kv, empty_kv, zero_conv, zero_ssm, *w)
        xs, k_s, v_s, c_s, s_s = hybrid_layer(xs, p_sample[i], cache_k[i], cache_v[i], state_conv[i], state_ssm[i], *w)
        kp_l.append(kp); vp_l.append(vp); cp_l.append(cp); sp_l.append(sp)
        ks_l.append(k_s); vs_l.append(v_s); cs_l.append(c_s); ss_l.append(s_s)
    y_prompt = rmsnorm(xp, final_norm_g)
    y_sample = rmsnorm(xs, final_norm_g)
    return (y_prompt, y_sample,
            jnp.stack(kp_l), jnp.stack(vp_l), jnp.stack(cp_l), jnp.stack(sp_l),
            jnp.stack(ks_l), jnp.stack(vs_l), jnp.stack(cs_l), jnp.stack(ss_l))


_drawn_inputs = setup_inputs


def setup_inputs(seed=0):
    import zlib

    import numpy as np

    out = dict(_drawn_inputs(seed))
    spreads = {}
    factors = {'mnorm_g': 5.996,
     'norm_ffn_g': 4.679,
     'norm_ple_g': 64.0,
     'final_norm_g': 7.829,
     'cache_k': 2.865}
    for name, (base, spread) in spreads.items():
        noise = np.random.default_rng([zlib.crc32(name.encode()), seed]).standard_normal(out[name].shape)
        drawn = base * np.exp(spread * noise) if base else spread * noise
        out[name] = __import__('jax').numpy.asarray(drawn.astype(out[name].dtype))
    for name, factor in factors.items():
        out[name] = (out[name] * factor).astype(out[name].dtype)
    return out
```

```python
import numpy as np
from contextlib import ExitStack

import concourse.bass as bass
from concourse import mybir
from concourse.alu_op_type import AluOpType as ALU

F32 = mybir.dt.float32
F32R = mybir.dt.float32r
BF16 = mybir.dt.bfloat16
ACT = mybir.ActivationFunctionType
ds = bass.ds

D, SEQ, NB, TD, PAST = 1024, 1024, 8, 16, 512
EPS = 1e-6
NEG = -1e30
P = 128
KT = D // P
ROWS = SEQ + NB * TD
RT = ROWS // P
RBN = 384
NRB = ROWS // RBN
PT = SEQ // P
HD, NH, NG, HPG, NS = 64, 16, 4, 4, 128
XBC = D + 2 * NG * NS
DFF = 2816
FT = DFF // P
PLE = 256
OFF_Z = 0
OFF_XBC = OFF_Z + D
OFF_DT = OFF_XBC + XBC
OFF_Q = OFF_DT + NH
OFF_K = OFF_Q + D
OFF_V = OFF_K + D
OFF_GA = OFF_V + D
OFF_GB = OFF_GA + D
SB_SCALE = HD ** -0.5
CT = XBC // P
HEAD = 4

V_MIX, V_CW, V_CB, V_MN, V_FFN, V_PLE, V_ALL = 0, 8, 72, 88, 96, 104, 112


class Store:
    pass


class Steps:

    def __init__(self, sem):
        self.sem, self.base = sem, HEAD

    def body(self, i, per):
        self.i, self.per, self.pos = i, per, 0

    def mark(self, ins):
        ins.then_inc(self.sem, 1)
        self.pos += 1
        return self.pos

    def value(self, pos):
        return self.base + self.i * self.per + pos

    def end(self, passes):
        assert self.pos == self.per, (self.pos, self.per)
        self.base += passes * self.per


def rev(t, c0, c1):
    return t[:, c1 - 1::-1] if c0 == 0 else t[:, c1 - 1:c0 - 1:-1]


def turn_columns(u):
    kind, t, h, s0, n, first = UNITS[u][:6]
    end = SEQ
    if not first:
        end -= P if kind == "old" else (t + 1) * P - n
    return end - n, end


def wsrc(w, col, n=P):
    return w.rearrange("(k p) c -> p k c", p=P)[:, :, ds(col, n)]


class WeightStream:

    def __init__(self, S):
        self.S = S

    def load(self, sp, u0, per, i, src):
        S = self.S
        sp.wait_ge(S.lo_done, HEAD + u0 - 1 + i * per)
        dst = S.raw[u0 % 2][:, 0:src.shape[1] * src.shape[2]].rearrange("p (k c) -> p k c", k=src.shape[1])
        sp.dma_start(dst, src).then_inc(S.raw_in[u0 % 2], 16)

    def split_hi(self, act, u0, per, i, last_block):
        S = self.S
        act.wait_ge(S.raw_in[u0 % 2], (u0 // 2 + 1) * 16 + i * (per // 2 * 16))
        act.wait_ge(S.acc_done, last_block)
        act.activation(S.w_hi[u0 % 2][:, :], S.raw[u0 % 2][:, :], ACT.Copy).then_inc(S.hi_done, 1)

    def split_lo(self, dve, u0, per, i, last_block):
        S = self.S
        dve.wait_ge(S.hi_done, HEAD + u0 + 1 + i * per)
        dve.wait_ge(S.acc_done, last_block)
        dve.tensor_tensor(S.w_lo[u0 % 2][:, :], S.raw[u0 % 2][:, :], S.w_hi[u0 % 2][:, :].bitcast(F32),
                          ALU.subtract).then_inc(S.lo_done, 1)


def product_block(S, pe, u, slot, acc, rhs, rb, ready, free, kts=KT, more=None):
    if ready is not None:
        pe.wait_ge(S.lo_done, ready)
    pe.wait_ge(*free)
    hi = S.w_hi[slot][:, 0:kts * P].rearrange("p (k c) -> p k c", k=kts)
    lo = S.w_lo[slot][:, 0:kts * P].rearrange("p (k c) -> p k c", k=kts)
    a_hi, a_lo = rhs
    rows = slice(rb * RBN, (rb + 1) * RBN)
    n = 0
    for k in range(kts):
        for w, a in ((hi, a_hi), (hi, a_lo), (lo, a_hi)):
            last = pe.matmul(acc[:, 0:RBN], w[:, k, :], a[:, k, rows],
                             start=(n == 0), stop=(n == 3 * kts - 1 and more is None))
            n += 1
    if more is not None:
        last = more()
    last.then_inc(S.acc_done, 1)


def stage_prologue(nc, S, A, first_tiles):
    with ExitStack() as ctx:
        def sb(name, shape, dt=F32):
            return ctx.enter_context(nc.sbuf_tensor(name, shape, dt))

        sem = S.sem

        x_rows = [sb(f"x_rows{n}", [P, D]) for n in range(3)]
        x_sq = sb("x_sq", [P, D])
        gain = sb("mix_gain", [P, D])
        vec_rows = sb("vec_rows", [V_ALL, P])
        mean_sq = sb("mean_sq", [P, RT])
        root = sb("root", [P, RT])
        rstd = sb("rstd", [P, RT])
        mask_f = sb("mask_f", [P, 64])
        mask_g = sb("mask_g", [P, 64])
        pt = [ctx.enter_context(nc.psum_tensor(f"x_t{n}", [P, KT, P], F32)) for n in range(2)]
        pv = ctx.enter_context(nc.psum_tensor("vec_t", [P, V_ALL], F32))
        vec_in, par_in, gain_in = sem("vec_in"), sem("par_in"), sem("gain_in")
        x_in = [sem(f"x_in{n}") for n in range(3)]
        made, sq_done, root_done, h_done = sem("made"), sem("sq_done"), sem("root_done"), sem("h_rows_done")
        x_t, vec_t, hi_ev, lo_ev = sem("x_tdone"), sem("vec_tdone"), sem("h_hi_done"), sem("h_lo_done")
        rstd_done, started = sem("rstd_done"), sem("par_done")

        with nc.Block() as block:
            @block.sync
            def _(sp):
                for r in range(3):
                    src = A.x_prompt[0, r * P:(r + 1) * P, :]
                    sp.dma_start(x_rows[r][:, :], src).then_inc(x_in[r], 16)
                sp.dma_start(gain[:, :], A.norm_mix_g[0:1, :].to_broadcast([P, D])).then_inc(gain_in, 16)
                table = [(A.norm_mix_g[0], V_MIX), (A.conv_b[0], V_CB), (A.mnorm_g[0], V_MN),
                         (A.norm_ffn_g[0], V_FFN), (A.norm_ple_g[0], V_PLE)]
                for v, at in table:
                    n = v.shape[0] // P
                    sp.dma_start(vec_rows[at:at + n, :], v.rearrange("(k p) -> k p", p=P)).then_inc(vec_in, 16)
                sp.dma_start(vec_rows[V_CW:V_CB, :],
                             A.conv_w[0].rearrange("t (c p) -> (t c) p", p=P)).then_inc(vec_in, 16)
                for v, dst in ((A.dt_bias, S.dt_bias), (A.a_log, S.a_log), (A.d_skip, S.d_heads)):
                    sp.dma_start(dst[:, :], v[0:1, :].to_broadcast([P, NH])).then_inc(par_in, 16)
                S.W.load(sp, 0, 2, 0, first_tiles[0])
                S.W.load(sp, 1, 2, 0, first_tiles[1])
                for r in range(3, RT):
                    sp.wait_ge(x_t, r - 2)
                    src = A.x_prompt[0, r * P:(r + 1) * P, :] if r < PT else \
                        A.x_sample.rearrange("b t d -> (b t) d")
                    sp.dma_start(x_rows[r % 3][:, :], src).then_inc(x_in[r % 3], 16)
                S.W.load(sp, 2, 2, 0, first_tiles[2])
                S.W.load(sp, 3, 2, 0, first_tiles[3])

            @block.gpsimd
            def _(pool):
                count = [0]

                def link(ins):
                    count[0] += 1
                    ins.then_inc(made, 1)
                    pool.wait_ge(made, count[0])

                def fill(t, v):
                    link(pool.memset(t, v))

                def sel(out, in_, op, fill_, base, pattern, cm):
                    link(pool.affine_select(out=out, in_=in_, compare_op=op, fill=fill_, base=base,
                                            pattern=pattern, channel_multiplier=cm))

                fill(S.ident[:, :], 0.0)
                sel(S.ident[:, :], S.ident[:, :], ALU.not_equal, 1.0, 0, [[-1, P]], 1)
                fill(S.ones[:, :], 1.0)
                sel(S.tri[:, :], S.ones[:, :], ALU.is_ge, 0.0, 0, [[1, P]], -1)
                blocks = S.same_batch[:, :].rearrange("p (b t) -> p b t", t=TD)
                sel(blocks, S.ones[:, :].rearrange("p (b t) -> p b t", t=TD), ALU.is_ge, 0.0, 0,
                    [[-TD, NB], [0, TD]], 1)
                sel(blocks, blocks, ALU.is_ge, 0.0, TD - 1, [[TD, NB], [0, TD]], -1)
                link(pool.tensor_tensor(S.tri_s[:, :], S.tri[:, :], S.same_batch[:, :], ALU.mult))
                fill(S.tmp[:, :], 0.0)
                sel(S.tmp[:, :], S.tmp[:, :], ALU.is_gt, NEG, 0, [[-1, P]], 1)
                link(pool.tensor_copy(S.mask_p[:, :], S.tmp[:, :]))
                link(pool.tensor_copy(S.ident_b[:, :], S.ident[:, :]))
                for h, m in ((0, mask_f), (1, mask_g)):
                    v = m[:, :].rearrange("p (b s) -> p b s", s=TD)
                    fill(m[:, :], 1.0)
                    sel(v, v, ALU.is_gt, 0.0, -TD * h, [[-2 * TD, 4], [-1, TD]], 1)
                    sel(v, v, ALU.is_ge, 0.0, TD * h + TD - 1, [[2 * TD, 4], [0, TD]], -1)
                link(pool.tensor_tensor(mask_f[:, :], mask_f[:, :], mask_g[:, :], ALU.add))
                link(pool.tensor_scalar(mask_f[:, :], mask_f[:, :], 1.0, -NEG, ALU.subtract, ALU.mult))
                for j in range(2):
                    fill(S.mask_s[j][:, :], NEG)
                    link(pool.tensor_copy(S.mask_s[j][:, 64 * j:64 * j + 64], mask_f[:, :]))
                pool.nop().then_inc(S.pw_done, HEAD)

            @block.scalar
            def _(act):
                act.nop().then_inc(S.hi_done, HEAD)
                act.nop().then_inc(S.acc_read_a, HEAD)
                act.nop().then_inc(S.kk_done, HEAD)
                act.nop().then_inc(S.gg_done, HEAD)
                act.nop().then_inc(S.o_read, HEAD)
                for r in range(RT + 1):
                    if r < RT:
                        act.wait_ge(x_in[r % 3], 16 * (r // 3 + 1))
                        if r >= 1:
                            act.wait_ge(sq_done, r)
                        act.activation(x_sq[:, :], x_rows[r % 3][:, :], ACT.Square,
                                       accum_out=mean_sq[:, r:r + 1]).then_inc(sq_done, 1)
                        act.wait_ge(rstd_done, r + 1)
                        act.activation(root[:, r:r + 1], rstd[:, r:r + 1], ACT.Sqrt).then_inc(root_done, 1)
                    if r >= 1:
                        act.wait_ge(x_t, r)
                        act.activation(S.R0_hi[:, :, (r - 1) * P:r * P], pt[(r - 1) % 2][:, :, :],
                                       ACT.Copy).then_inc(hi_ev, 1)
                S.W.split_hi(act, 0, 2, 0, HEAD)
                S.W.split_hi(act, 1, 2, 0, HEAD)

            @block.vector
            def _(dve):
                for s in (S.lo_done, S.acc_read_v, S.tp_drained, S.p_done, S.dve_steps.sem):
                    dve.nop().then_inc(s, HEAD)
                dve.wait_ge(gain_in, 16)
                for r in range(RT + 1):
                    if r < RT:
                        dve.wait_ge(sq_done, r + 1)
                        dve.tensor_scalar(rstd[:, r:r + 1], mean_sq[:, r:r + 1], 1.0 / D, EPS,
                                          ALU.mult, ALU.add).then_inc(rstd_done, 1)
                        dve.wait_ge(root_done, r + 1)
                        dve.reciprocal(rstd[:, r:r + 1], root[:, r:r + 1]).then_inc(started, 1)
                        dve.wait_ge(started, r + 1)
                        dve.scalar_tensor_tensor(x_rows[r % 3][:, :], x_rows[r % 3][:, :], rstd[:, r:r + 1],
                                                 gain[:, :], ALU.mult, ALU.mult).then_inc(h_done, 1)
                    if r >= 1:
                        dve.wait_ge(hi_ev, r)
                        cols = slice((r - 1) * P, r * P)
                        dve.tensor_tensor(S.R0_lo[:, :, cols], pt[(r - 1) % 2][:, :, :],
                                          S.R0_hi[:, :, cols].bitcast(F32), ALU.subtract).then_inc(lo_ev, 1)
                S.W.split_lo(dve, 0, 2, 0, HEAD)
                S.W.split_lo(dve, 1, 2, 0, HEAD)
                dve.wait_ge(vec_t, 1)
                dve.tensor_copy(S.vec[:, :], pv[:, :])
                dve.wait_ge(par_in, 48)
                for h in range(2):
                    dve.tensor_copy(S.d_chan[64 * h:64 * h + 64, :],
                                    S.d_heads[64 * h:64 * h + 64, :].rearrange("p (k h) -> p k h", h=2)[:, :, h])

            @block.tensor
            def _(pe):
                for s in (S.acc_done, S.z_done, S.tp_done, S.av_done):
                    pe.nop().then_inc(s, HEAD)
                pe.wait_ge(made, 2)
                for r in range(RT):
                    pe.wait_ge(h_done, r + 1)
                    if r >= 2:
                        pe.wait_ge(lo_ev, r - 1)
                    for k in range(KT):
                        last = pe.transpose(pt[r % 2][:, k, :], x_rows[r % 3][:, k * P:(k + 1) * P], S.ident[:, :])
                    last.then_inc(x_t, 1)
                pe.wait_ge(vec_in, 6 * 16)
                pe.transpose(pv[:, :], vec_rows[:, :], S.ident[0:V_ALL, 0:V_ALL]).then_inc(vec_t, 1)


def score_units():
    rows = []
    for t in range(PT):
        for h in range(2):
            n = (t + 1) * P
            top = max(0, n - n % 512 if n % 512 else n - 512)
            row = [("p", t, h, top, n - top)]
            if top:
                row.append(("p", t, h, 0, top))
            rows.append([u + (m == 0, m == len(row) - 1) for m, u in enumerate(row)])
    sample = [[("new", j, 0, 0, P, True, False), ("old", j, 0, 0, PAST, False, True)] for j in range(2)]
    rows = rows[:10] + [sample[0]] + rows[10:] + [sample[1]]
    return [u + (n,) for n, row in enumerate(rows) for u in row]


UNITS = score_units()
NU = len(UNITS)
N_ROWS_SB = UNITS[-1][-1] + 1
LAG_T, LAG_A = 3, 5
STEPS = NU + LAG_A + 1
U_OLD0 = [n for n, u in enumerate(UNITS) if u[0] == "old"]
CACHE_AT = {0: 2, 1: 3, 2: 4, 3: 5, 4: U_OLD0[0] + 1, 5: U_OLD0[0] + 2, 6: U_OLD0[0] + 3, 7: U_OLD0[0] + 4}
GATE_AT = {3: 0, 12: 1, 22: 2}
O_BANKS = [("p", t) for t in range(5)] + [("s", 0)] + [("p", t) for t in range(5, PT)] + [("s", 1)]


def o_bank(u):
    kind, n = ("p" if UNITS[u][0] == "p" else "s"), UNITS[u][1]
    return O_BANKS.index((kind, n))


def o_last(u):
    return u == max(m for m in range(NU) if o_bank(m) == o_bank(u))


def o_first(u):
    return u == min(m for m in range(NU) if o_bank(m) == o_bank(u))


def tp_events():
    ev = [("k", 0), ("k", 1), ("k", 2), ("v", 0), ("v", 1), ("v", 2)]
    for s in range(STEPS):
        ev += [("cache", b) for b in range(NB) if CACHE_AT[b] == s]
        if 0 <= s - LAG_T < NU:
            ev.append(("w", s - LAG_T))
        if 0 <= s - LAG_A - 1 < NU and UNITS[s - LAG_A - 1][0] == "old":
            ev.append(("o", UNITS[s - LAG_A - 1][1]))
    return ev


TP = tp_events()
NTP = len(TP)
NO = len(O_BANKS)


def stage_pairs(nc, S, A, b0, u0, tiles, next_tiles):
    N = NH // 2
    BPI, PER = 12, 4
    assert NTP % 2 == 0 and NO % 2 == 0 and NU % 2 == 0 and NU % 4 == 0, (NTP, NO, NU)
    with ExitStack() as ctx:
        def sb(name, shape, dt=F32):
            return ctx.enter_context(nc.sbuf_tensor(name, shape, dt))

        sem = S.sem

        q_pack = [sb(f"q_pack{h}", [P, ROWS], F32R) for h in range(2)]
        k_hi = [sb(f"k_hi{h}", [P, ROWS], F32R) for h in range(2)]
        k_lo = [sb(f"k_lo{h}", [P, ROWS], F32R) for h in range(2)]
        k_new = sb("k_new", [P, P])
        q_diag = sb("q_diag", [P, NB, 2, TD])
        stage = [sb(f"qkv_stage{n}", [P, RBN]) for n in range(2)]
        kv_out = [sb(f"kv_out{n}", [P, 3, P]) for n in range(2)]
        v_rows = sb("v_rows", [P, RT, P])
        keep = [sb(f"keep{n}", [P, 512]) for n in range(2)]
        wgt = [sb(f"wgt{n}", [P, 512]) for n in range(4)]
        left = [sb(f"left{n}", [P, SEQ + 1]) for n in range(2)]
        w_t = [sb(f"w_t{n}", [P, 4, P]) for n in range(4)]
        kc = sb("k_cache", [P, 4, 4, 2, HD])
        vc = sb("v_cache", [P, 4, 2, 4, HD])
        kc_t = sb("k_cache_t", [P, 4, PAST])
        o_t = sb("o_t", [P, ROWS])
        o_s = sb("o_sample", [P, P])
        gate = [sb(f"gate{n}", [P, RBN]) for n in range(2)]

        def bank(name):
            return ctx.enter_context(nc.psum_tensor(name, [P, 512], F32))

        acc = [bank("acc0"), bank("acc1")]
        zb = [bank("z0"), bank("z1")]
        tp = [bank("tp0"), bank("tp1")]
        ob = [bank("o0"), bank("o1")]

        kc_in, vc_in, o_stored = sem("kc_in"), sem("vc_in"), sem("o_st")
        kv_stored = [sem(f"kv_st{n}") for n in range(2)]
        gate_stored = [sem(f"gt_st{n}") for n in range(3)]
        q_diag_done, packed, zeroed = sem("q_diag_done"), sem("packed"), sem("zeroed")
        k_out = A.new_k_prompt[0, 0], A.new_k_sample[0]
        v_out = A.new_v_prompt[0, 0], A.new_v_sample[0]
        tiles_now = tiles

        def b_end(i, n):
            return HEAD + b0 + BPI * i + n + 1

        def tpv(i, ev):
            return HEAD + NTP * i + TP.index(ev) + 1

        def uv(i, u):
            return HEAD + NU * i + u + 1

        per_m = [3, 3, 2 + NB] * 2
        KV0 = 16 * sum(per_m[m] for m in range(6) if m % 2 == 0)
        KV1 = 16 * sum(per_m[m] for m in range(6) if m % 2 == 1)

        def kv_before(i, m):
            return (KV1 if m % 2 else KV0) * i + 16 * sum(per_m[n] for n in range(m) if n % 2 == m % 2)

        with nc.Block() as block:
            @block.sync
            def _(sp):
                def body(i, last):
                    def weight(j):
                        src = next_tiles[j] if last else tiles_now(i + 1, j)
                        S.W.load(sp, u0 + PER + j, PER, i, src)


                    def cache_k(j):
                        sp.wait_ge(S.tp_done, tpv(i, ("cache", 3)) if j else HEAD + NTP * i)
                        for n in range(4):
                            for s in range(4):
                                src = A.cache_k[0, 4 * j + n, ds(2 * i, 2)].rearrange("h (p s) d -> s p h d", s=4)[s]
                                sp.dma_start(kc[:, n, s, :, :], src).then_inc(kc_in, 16)

                    def cache_v(j):
                        sp.wait_ge(S.av_done, uv(i, U_OLD0[0]) if j else HEAD + NU * i)
                        for n in range(4):
                            sp.dma_start(vc[:, n, :, :, :].rearrange("p h s d -> p h (s d)"),
                                         A.cache_v[0, 4 * j + n, ds(2 * i, 2)].rearrange("h (p s) d -> p h (s d)", s=4))\
                              .then_inc(vc_in, 16)

                    def store_rows(out, m):
                        sp.wait_ge(S.tp_drained, tpv(i, ("kv"[m // 3], m % 3)))
                        src = kv_out[m % 2]
                        prompt, sample = out
                        n = 3 if m % 3 < 2 else 2
                        for r in range(n):
                            s0 = (m % 3) * RBN + r * P
                            sp.dma_start(prompt[ds(2 * i, 2), s0:s0 + P, :].rearrange("h p d -> p h d"),
                                         src[:, r, :].rearrange("p (h d) -> p h d", h=2)).then_inc(kv_stored[m % 2], 16)
                        if n == 2:
                            for b in range(NB):
                                sp.dma_start(sample[b, ds(2 * i, 2)].rearrange("h p d -> p h d"),
                                             src[TD * b:TD * (b + 1), 2, :].rearrange("p (h d) -> p h d", h=2))\
                                  .then_inc(kv_stored[m % 2], 16)

                    cache_k(0)
                    cache_v(0)
                    weight(0)
                    for m in range(3):
                        store_rows(k_out, m)
                    weight(1)
                    for m in range(3, 6):
                        store_rows(v_out, m)
                    weight(2)

                    def store_gate(rb):
                        sp.wait_ge(S.acc_read_a, b_end(i, 9 + rb))
                        sp.dma_start(S.d_gate_a[ds(i, 1), :, rb * RBN:(rb + 1) * RBN].rearrange("a p n -> (a p) n"),
                                     gate[rb % 2][:, :]).then_inc(gate_stored[rb], 16)
                    store_gate(0)
                    cache_k(1)
                    store_gate(1)
                    cache_v(1)
                    store_gate(2)
                    weight(3)
                    sp.wait_ge(S.tp_drained, tpv(i, ("o", 1)))
                    sp.dma_start(S.d_o[ds(i, 1)].rearrange("a p n -> (a p) n"), o_t[:, :]).then_inc(o_stored, 16)

                with sp.Fori(0, N - 1) as i:
                    body(i, False)
                body(N - 1, True)
                for s, n in ((kv_stored[0], KV0), (kv_stored[1], KV1), (o_stored, 16), *((g, 16) for g in gate_stored)):
                    sp.wait_ge(s, N * n)

            @block.tensor
            def _(pe):
                rhs = (S.R0_hi, S.R0_lo)

                def product(i, n):
                    b = b0 + n
                    product_block(S, pe, None, (u0 + n // 3) % 2, acc[b % 2], rhs, n % 3,
                                  HEAD + u0 + PER * i + n // 3 + 1,
                                  (S.acc_read_a, HEAD + b0 - 1 + BPI * i + n))

                def open_tp(i, ev):
                    n = TP.index(ev)
                    pe.wait_ge(S.tp_drained, HEAD + NTP * i + n - 1)
                    return tp[n % 2]

                def rows_of(i, ev):
                    kind, rb = ev
                    n = (3 if kind == "k" else 6) + rb
                    pe.wait_ge(S.acc_read_a, b_end(i, n))
                    out = open_tp(i, ev)
                    for r in range(3):
                        last = pe.transpose(out[:, r * P:(r + 1) * P], stage[n % 2][:, r * P:(r + 1) * P], S.ident[:, :])
                    last.then_inc(S.tp_done, 1)

                def cache_t(i, b):
                    pe.wait_ge(kc_in, 512 * i + 256 * (b // 4 + 1))
                    out = open_tp(i, ("cache", b))
                    for s in range(4):
                        last = pe.transpose(out[:, s * P:(s + 1) * P], kc[:, b % 4, s, :, :].rearrange("p h d -> p (h d)"), S.ident[:, :])
                    last.then_inc(S.tp_done, 1)

                def scores(i, u):
                    kind, t, h, s0, n = UNITS[u][:5]
                    z = zb[u % 2]
                    pe.wait_ge(S.gg_done, HEAD + NU * i + u - 1)
                    if u == 0:
                        pe.wait_ge(packed, 6 * i + 6)
                    if kind == "p":
                        q = q_pack[h][:, t * P:(t + 1) * P]
                        pe.matmul(z[:, 0:n], q, k_hi[h][:, s0:s0 + n], start=True, stop=False)
                        last = pe.matmul(z[:, 0:n], q, k_lo[h][:, s0:s0 + n], start=False, stop=(s0 + n <= t * P))
                        if s0 + n > t * P:
                            last = pe.matmul(z[:, n - P:n], S.ident_b[:, :], S.mask_p[:, :], start=False, stop=True)
                    elif kind == "new":
                        if t == 0:
                            pe.wait_ge(q_diag_done, 3 * i + 3)
                        q = q_diag[:, 4 * t:4 * t + 4, :, :].rearrange("p b h t -> p (b h t)")
                        pe.matmul(z[:, 0:P], q, k_new[:, :], start=True, stop=False)
                        last = pe.matmul(z[:, 0:P], S.ident_b[:, :], S.mask_s[t][:, :], start=False, stop=True)
                    else:
                        pe.wait_ge(S.tp_drained, tpv(i, ("cache", 4 * t + 3)))
                        for b in range(4):
                            last = pe.matmul(z[32 * b:32 * b + 32, :],
                                             q_diag[:, 4 * t + b, :, :].rearrange("p h t -> p (h t)"),
                                             kc_t[:, b, :], start=True, stop=True)
                    last.then_inc(S.z_done, 1)

                def transposes(i, u):
                    kind, t, h, s0, n = UNITS[u][:5]
                    pe.wait_ge(S.pw_done, uv(i, u))
                    out = open_tp(i, ("w", u))
                    w = wgt[u % 4]
                    for c in range(n // P):
                        src = w[:, c:PAST:4] if kind == "old" else w[:, c * P:(c + 1) * P]
                        last = pe.transpose(out[:, c * P:(c + 1) * P], src, S.ident[:, :])
                    last.then_inc(S.tp_done, 1)

                def values(i, u):
                    kind, t, h, s0, n, first, final = UNITS[u][:7]
                    pe.wait_ge(S.tp_drained, tpv(i, ("w", u)))
                    o = ob[o_bank(u) % 2]
                    if o_first(u):
                        pe.wait_ge(S.o_read, HEAD + NO * i + o_bank(u) - 1)
                    wt = w_t[u % 4]
                    if kind == "p":
                        for c in range(n // P):
                            last = pe.matmul(o[64 * h:64 * h + 64, 0:P], v_rows[:, s0 // P + c, 64 * h:64 * h + 64],
                                             wt[:, c, :], start=(first and c == 0), stop=(final and c == n // P - 1))
                    elif kind == "new":
                        last = pe.matmul(o[:, 0:P], wt[:, 0, :], v_rows[:, PT, :], start=True, stop=False)
                    else:
                        pe.wait_ge(vc_in, 128 * i + 64 * (t + 1))
                        for c in range(4):
                            for b in range(4):
                                last = pe.matmul(o[32 * b:32 * b + 32, 0:P], wt[:, c, 32 * b:32 * b + 32],
                                                 vc[:, b, :, c, :], start=False, stop=(c == 3))
                    last.then_inc(S.av_done, 1)

                def turn_o(i, j):
                    pe.wait_ge(S.o_read, HEAD + NO * i + O_BANKS.index(("s", j)) + 1)
                    out = open_tp(i, ("o", j))
                    pe.transpose(out[:, 0:P], o_s[:, :], S.ident[:, :]).then_inc(S.tp_done, 1)

                with pe.Fori(0, N) as i:
                    for n in range(9):
                        product(i, n)
                        if n >= 4:
                            rows_of(i, TP[n - 4])
                    rows_of(i, ("v", 2))
                    for s in range(STEPS):
                        if s in GATE_AT:
                            product(i, 9 + GATE_AT[s])
                        for b in range(NB):
                            if CACHE_AT[b] == s:
                                cache_t(i, b)
                        if s < NU:
                            scores(i, s)
                        if 0 <= s - LAG_T < NU:
                            transposes(i, s - LAG_T)
                        if 0 <= s - LAG_A < NU:
                            values(i, s - LAG_A)
                        if 0 <= s - LAG_A - 1 < NU and UNITS[s - LAG_A - 1][0] == "old":
                            turn_o(i, UNITS[s - LAG_A - 1][1])

            @block.scalar
            def _(act):
                def copy_block(i, n):
                    act.wait_ge(S.acc_done, b_end(i, n))
                    if n < 2:
                        act.wait_ge(S.tp_done, HEAD + NTP * i)
                    elif n < 8:
                        m = n - 2
                        act.wait_ge(packed, 6 * i + min(m, 5) + 1)
                        if n == 4 or n == 7:
                            act.wait_ge(q_diag_done, 3 * i + (2 if n == 4 else 3))
                        if m >= 3:
                            act.wait_ge(S.tp_done, tpv(i, ("k", m - 3)))
                    else:
                        act.wait_ge(S.tp_done, tpv(i, ("v", 0)))
                    act.activation(stage[n % 2][:, :], acc[(b0 + n) % 2][:, 0:RBN], ACT.Copy)\
                       .then_inc(S.acc_read_a, 1)

                def diag(i, h):
                    act.wait_ge(S.acc_read_a, b_end(i, 2))
                    act.wait_ge(zeroed, 1)
                    act.activation(q_diag[64 * h:64 * h + 64, :, h, :],
                                   stage[0][64 * h:64 * h + 64, 2 * P:3 * P].rearrange("p (b t) -> p b t", t=TD),
                                   ACT.Copy).then_inc(q_diag_done, 1)

                def split(i, j):
                    S.W.split_hi(act, u0 + j + 2, PER, i, b_end(i, 3 * j + 2))

                with act.Fori(0, N) as i:
                    for n in range(9):
                        copy_block(i, n)
                        if n == 2:
                            diag(i, 0)
                            diag(i, 1)
                        if n == 5:
                            act.wait_ge(S.acc_read_a, b_end(i, 5))
                            act.activation(k_new[:, :], stage[1][:, 2 * P:3 * P], ACT.Copy).then_inc(q_diag_done, 1)
                        if n % 3 == 2:
                            split(i, n // 3)
                    for s in range(STEPS):
                        if s in GATE_AT:
                            rb = GATE_AT[s]
                            act.wait_ge(S.acc_done, b_end(i, 9 + rb))
                            if rb == 2:
                                act.wait_ge(gate_stored[0], 16 * i + 16)
                            else:
                                act.wait_ge(gate_stored[rb], 16 * i)
                                if rb == 0:
                                    act.wait_ge(gate_stored[2], 16 * i)
                            act.activation(gate[rb % 2][:, :], acc[(b0 + 9 + rb) % 2][:, 0:RBN], ACT.Sigmoid)\
                               .then_inc(S.acc_read_a, 1)
                            if rb == 2:
                                split(i, 3)
                        if s < NU:
                            n = UNITS[s][4]
                            act.wait_ge(S.z_done, uv(i, s))
                            act.wait_ge(S.p_done, HEAD + NU * i + s - 1)
                            act.activation(keep[s % 2][:, 0:n], zb[s % 2][:, 0:n], ACT.Sigmoid, scale=-SB_SCALE)\
                               .then_inc(S.kk_done, 1)
                            if s >= 4:
                                act.wait_ge(S.tp_done, tpv(i, ("w", s - 4)))
                            act.activation(wgt[s % 4][:, 0:n], zb[s % 2][:, 0:n], ACT.Sigmoid, scale=SB_SCALE)\
                               .then_inc(S.gg_done, 1)
                        u = s - LAG_A
                        if 0 <= u < NU and o_last(u):
                            act.wait_ge(S.av_done, uv(i, u))
                            if u == min(m for m in range(NU) if o_last(m)):
                                act.wait_ge(o_stored, 16 * i)
                            kind, t = O_BANKS[o_bank(u)]
                            src = ob[o_bank(u) % 2]
                            if kind == "p":
                                act.activation(o_t[:, t * P:(t + 1) * P], src[:, 0:P], ACT.Copy).then_inc(S.o_read, 1)
                            else:
                                if t == 1:
                                    act.wait_ge(S.tp_done, tpv(i, ("o", 0)))
                                act.activation(o_s[:, :], src[:, 0:P], ACT.Copy).then_inc(S.o_read, 1)

            @block.vector
            def _(dve):
                steps = S.dve_steps

                def pack(i, n):
                    src = stage[n % 2]
                    cols = slice((n % 3) * RBN, (n % 3 + 1) * RBN)
                    dve.wait_ge(S.acc_read_a, b_end(i, n))
                    half = (slice(0, 64), slice(64, P))
                    if n < 3:
                        for h in range(2):
                            m = steps.mark(dve.tensor_copy(q_pack[h][half[h], cols], src[half[h], :]))
                        for h in range(2):
                            dve.wait_ge(steps.sem, steps.value(m - 1 + h))
                            ins = dve.tensor_tensor(q_pack[h][half[1 - h], cols], src[half[h], :],
                                                    q_pack[h][half[h], cols].bitcast(F32), ALU.subtract)
                            if h == 0:
                                steps.mark(ins)
                    else:
                        for h in range(2):
                            m = steps.mark(dve.tensor_copy(k_hi[h][half[h], cols], src[half[h], :]))
                            steps.mark(dve.tensor_copy(k_hi[h][half[1 - h], cols], src[half[h], :]))
                        m = steps.pos - 3
                        for h in range(2):
                            dve.wait_ge(steps.sem, steps.value(m + 2 * h))
                            steps.mark(dve.tensor_tensor(k_lo[h][half[h], cols], src[half[h], :],
                                                         k_hi[h][half[h], cols].bitcast(F32), ALU.subtract))
                            ins = dve.tensor_tensor(k_lo[h][half[1 - h], cols], src[half[h], :],
                                                    k_hi[h][half[h], cols].bitcast(F32), ALU.subtract)
                            if h == 0:
                                steps.mark(ins)
                    ins.then_inc(packed, 1)

                def drain(i, ev):
                    n = TP.index(ev)
                    src = tp[n % 2]
                    dve.wait_ge(S.tp_done, HEAD + NTP * i + n + 1)
                    kind, x = ev
                    if kind in "kv":
                        m = x + (3 if kind == "v" else 0)
                        dve.wait_ge(kv_stored[m % 2], kv_before(i, m))
                        if kind == "v":
                            steps.mark(dve.tensor_copy(v_rows[:, 3 * x:3 * x + 3, :],
                                                       src[:, 0:RBN].rearrange("p (r c) -> p r c", c=P)))
                            dve.wait_ge(steps.sem, steps.value(steps.pos))
                            dve.tensor_copy(kv_out[m % 2][:, :, :], v_rows[:, 3 * x:3 * x + 3, :])\
                               .then_inc(S.tp_drained, 1)
                        else:
                            dve.tensor_copy(kv_out[m % 2][:, :, :], src[:, 0:RBN].rearrange("p (r c) -> p r c", c=P))\
                               .then_inc(S.tp_drained, 1)
                    elif kind == "cache":
                        dve.wait_ge(S.z_done, uv(i, U_OLD0[0]) if x >= 4 else HEAD + NU * i)
                        dve.tensor_copy(kc_t[:, x % 4, :].rearrange("p (m s) -> p s m", s=4),
                                        src[:, :].rearrange("p (s m) -> p s m", s=4)).then_inc(S.tp_drained, 1)
                    elif kind == "w":
                        dve.wait_ge(S.av_done, HEAD + NU * i + x - 3)
                        c = UNITS[x][4] // P
                        dve.tensor_copy(w_t[x % 4][:, 0:c, :], src[:, 0:c * P].rearrange("p (c m) -> p c m", c=c))\
                           .then_inc(S.tp_drained, 1)
                    else:
                        for h in range(2):
                            cols = slice(SEQ + 64 * x, SEQ + 64 * x + 64)
                            ins = dve.tensor_copy(
                                o_t[64 * h:64 * h + 64, cols].rearrange("p (b t) -> p b t", t=TD),
                                src[64 * h:64 * h + 64, 0:P].rearrange("p (b h t) -> p b h t", h=2, t=TD)[:, :, h, :])
                            if h == 1:
                                ins.then_inc(S.tp_drained, 1)

                def split(i, j):
                    S.W.split_lo(dve, u0 + j + 2, PER, i, b_end(i, 3 * j + 2))

                dve.memset(q_diag[:, :, :, :], 0.0).then_inc(zeroed, 1)
                for n in range(2):
                    dve.memset(left[n][:, SEQ:SEQ + 1], 1.0)
                with dve.Fori(0, N) as i:
                    steps.body(i, PAIR_STEPS)
                    for n in range(6):
                        pack(i, n)
                        if n % 3 == 2:
                            split(i, n // 3)
                        if n >= 4:
                            drain(i, TP[n - 4])
                    drain(i, TP[2])
                    drain(i, TP[3])
                    drain(i, TP[4])
                    split(i, 2)
                    drain(i, TP[5])
                    for s in range(STEPS):
                        for b in range(NB):
                            if CACHE_AT[b] == s:
                                drain(i, ("cache", b))
                        if 1 <= s <= NU:
                            u = s - 1
                            kind, t, h, s0, n, first, final, row = UNITS[u]
                            c0, c1 = turn_columns(u)
                            dve.wait_ge(S.kk_done, uv(i, u))
                            if first:
                                prev = [m for m in range(NU) if UNITS[m][7] == row - 2]
                                dve.wait_ge(S.pw_done, uv(i, prev[-1]) if prev else HEAD + NU * i)
                            else:
                                dve.wait_ge(S.p_done, uv(i, u - 1))
                            lf = left[row % 2]
                            k = keep[u % 2]
                            dve.tensor_tensor_scan(rev(lf, c0, c1), rev(k, 0, n), rev(k, 0, n),
                                                   lf[:, c1:c1 + 1], ALU.mult, ALU.bypass).then_inc(S.p_done, 1)
                        if 0 <= s - LAG_T < NU:
                            drain(i, ("w", s - LAG_T))
                        if 0 <= s - LAG_A - 1 < NU and UNITS[s - LAG_A - 1][0] == "old":
                            if UNITS[s - LAG_A - 1][1] == 0:
                                dve.wait_ge(o_stored, 16 * i)
                            drain(i, ("o", UNITS[s - LAG_A - 1][1]))
                        if s in GATE_AT and GATE_AT[s] == 2:
                            split(i, 3)
                    steps.end(0)
                steps.base += N * PAIR_STEPS

            @block.gpsimd
            def _(pool):
                with pool.Fori(0, N) as i:
                    for u in range(NU):
                        n, row = UNITS[u][4], UNITS[u][-1]
                        c0, c1 = turn_columns(u)
                        pool.wait_ge(S.gg_done, uv(i, u))
                        pool.wait_ge(S.p_done, uv(i, u))
                        w = wgt[u % 4]
                        pool.tensor_tensor(w[:, 0:n], w[:, 0:n], left[row % 2][:, c0 + 1:c1 + 1], ALU.mult)\
                            .then_inc(S.pw_done, 1)


def stage_steps(nc, S, A, b0, u0, t0, next_load):
    with ExitStack() as ctx:
        def sb(name, shape, dt=F32):
            return ctx.enter_context(nc.sbuf_tensor(name, shape, dt))

        def bank(name):
            return ctx.enter_context(nc.psum_tensor(name, [P, 512], F32))

        sem = S.sem

        dt_t = sb("dt_t", [P, ROWS])
        raw = sb("dt_raw", [P, RT, NH])
        mag = sb("dt_mag", [P, RT, NH])
        rate = sb("rate", [P, NH])
        acc = [bank("dacc0"), bank("dacc1")]
        tb, sums, ends, batch = bank("dt_rows"), bank("sums"), bank("ends"), bank("batch_ends")
        act_s, dve_s, pe_s = sem("dt_act"), sem("dt_dve"), sem("dt_pe")

        def over_tiles(v):
            return v.unsqueeze(1).to_broadcast([P, RT, NH])

        with nc.Block() as block:
            @block.sync
            def _(sp):
                next_load(sp)

            @block.tensor
            def _(pe):
                for rb in range(NRB):
                    product_block(S, pe, None, u0 % 2, acc[rb % 2], (S.R0_hi, S.R0_lo), rb, HEAD + u0 + 1,
                                  (act_s, rb - 1) if rb >= 1 else (S.acc_done, HEAD + b0))
                pe.wait_ge(act_s, NRB)
                for r in range(RT):
                    last = pe.transpose(tb[:, 32 * r:32 * r + 32], dt_t[0:32, r * P:(r + 1) * P], S.ident[0:32, 0:32])
                last.then_inc(pe_s, 1)
                pe.wait_ge(dve_s, 5)
                n = PT * NH
                flat = S.dta[:, :, :].rearrange("p r h -> p (r h)")
                for out, m, m_s in ((sums, S.tri, S.tri_s), (ends, S.ones, S.same_batch)):
                    pe.matmul(out[:, 0:n], m[:, :], flat[:, 0:n], start=True, stop=True)
                    pe.matmul(out[:, n:n + NH], m_s[:, :], flat[:, n:n + NH], start=True, stop=True)
                for k in range(KT):
                    last = pe.matmul(batch[:, NB * k:NB * k + NB],
                                     dt_t[:, k * P:(k + 1) * P],
                                     S.same_batch[:, 0:P:TD], start=True, stop=True)
                last.then_inc(pe_s, 1)

            @block.scalar
            def _(act):
                for rb in range(NRB):
                    act.wait_ge(S.acc_done, HEAD + b0 + rb + 1)
                    act.activation(dt_t[:, rb * RBN:(rb + 1) * RBN], acc[rb % 2][:, 0:RBN], ACT.Copy).then_inc(act_s, 1)
                S.W.split_hi(act, u0 + 2, 2, 0, HEAD + b0 + NRB)
                act.activation(rate[:, :], S.a_log[:, :], ACT.Exp).then_inc(act_s, 1)
                act.wait_ge(dve_s, 2)
                act.activation(mag[:, :, :], mag[:, :, :], ACT.Exp, scale=-1.0).then_inc(act_s, 1)
                act.wait_ge(act_s, NRB + 2)
                act.activation(mag[:, :, :], mag[:, :, :], ACT.Ln, bias=1.0).then_inc(act_s, 1)
                act.wait_ge(pe_s, 2)
                act.activation(S.chunk_decay[:, :, :].rearrange("p r h -> p (r h)"), ends[:, 0:RT * NH], ACT.Exp)\
                   .then_inc(act_s, 1)
                act.activation(S.batch_decay[:, :, :].rearrange("p k b -> p (k b)"), batch[:, 0:KT * NB], ACT.Exp)\
                   .then_inc(act_s, 1)
                act.wait_ge(dve_s, 7)
                act.activation(S.dt_end[:, :, :], S.dt_end[:, :, :], ACT.Exp).then_inc(act_s, 1)

            @block.vector
            def _(dve):
                S.W.split_lo(dve, u0 + 2, 2, 0, HEAD + b0 + NRB)
                dve.wait_ge(pe_s, 1)
                dve.tensor_tensor(raw[:, :, :], tb[:, 0:32 * RT].rearrange("p (r c) -> p r c", c=32)[:, :, 0:NH],
                                  over_tiles(S.dt_bias[:, :]), ALU.add).then_inc(dve_s, 1)
                dve.wait_ge(dve_s, 1)
                dve.scalar_tensor_tensor(mag[:, :, :], raw[:, :, :], -1.0, raw[:, :, :], ALU.mult, ALU.max)\
                   .then_inc(dve_s, 1)
                dve.wait_ge(act_s, NRB + 3)
                dve.scalar_tensor_tensor(S.dt[:, :, :], raw[:, :, :], 0.0, mag[:, :, :], ALU.max, ALU.add)\
                   .then_inc(dve_s, 1)
                dve.wait_ge(dve_s, 3)
                dve.scalar_tensor_tensor(S.dta[:, :, :], S.dt[:, :, :], -1.0, over_tiles(rate[:, :]),
                                         ALU.mult, ALU.mult).then_inc(dve_s, 1)
                dve.wait_ge(dve_s, 4)
                dve.tensor_copy(dt_t[:, 0:D].rearrange("p (h d) -> p h d", h=NH),
                                S.dta[:, PT, :].unsqueeze(2).to_broadcast([P, NH, HD])).then_inc(dve_s, 1)
                dve.wait_ge(pe_s, 2)
                dve.tensor_copy(S.dsum[:, :, :].rearrange("p r h -> p (r h)"), sums[:, 0:RT * NH]).then_inc(dve_s, 1)
                dve.wait_ge(dve_s, 6)
                dve.wait_ge(act_s, NRB + 4)
                dve.tensor_tensor(S.dt_end[:, :, :].rearrange("p r h -> p (r h)"), ends[:, 0:RT * NH],
                                  S.dsum[:, :, :].rearrange("p r h -> p (r h)"), ALU.subtract).then_inc(dve_s, 1)
                dve.wait_ge(act_s, NRB + 6)
                dve.tensor_tensor(S.dt_end[:, :, :], S.dt_end[:, :, :], S.dt[:, :, :], ALU.mult).then_inc(dve_s, 1)


SSD_TP = ["hist", "tail"] + [("rows", 0)]
for _c in range(RT):
    if _c + 1 < RT:
        SSD_TP.append(("rows", _c + 1))
    if _c == PT:
        SSD_TP += [("h0", _b) for _b in range(NB)]
        SSD_TP.append("state")
NTP2 = len(SSD_TP)
PAD = 3
XW = PAD + SEQ
XP_COLS = XW + NB * (PAD + TD)


def stage_ssd(nc, S, A, b0, ba0, u0, t0, tiles, next_tiles):
    BPI, PER = 24, 8
    HC = HPG * HD
    with ExitStack() as ctx:
        def sb(name, shape, dt=F32):
            return ctx.enter_context(nc.sbuf_tensor(name, shape, dt))

        def bank(name):
            return ctx.enter_context(nc.psum_tensor(name, [P, 512], F32))

        sem = S.sem

        xp = sb("conv_in", [P, 4, XP_COLS])
        y = sb("conv_out", [P, 4, ROWS])
        sg = sb("sig", [P, ROWS])
        zt = sb("z_t", [P, 2, ROWS])
        gb = sb("gb_t", [P, 2, ROWS])
        rs = sb("y_rstd", [P, ROWS])
        seg = [sb(f"seg{n}", [P, HPG, P]) for n in range(2)]
        grow = [sb(f"grow{n}", [P, 2, P]) for n in range(2)]
        dx = [sb(f"dx{n}", [P, HPG, HD]) for n in range(2)]
        dxe = [sb(f"dxe{n}", [P, HPG, HD]) for n in range(2)]
        b_rows = [sb(f"b_rows{n}", [P, NS]) for n in range(2)]
        cbm = sb("cb_masked", [P, P])
        off = sb("y_off", [P, 2, P])
        state = sb("state", [P, HPG, HD])
        state_out = sb("state_out", [P, 2, NS])
        h0 = sb("h0", [P, 2, NB, NS])
        h0_t = [sb(f"h0_t{n}", [P, 2 * P]) for n in range(2)]
        b_blk = sb("b_blocks", [P, NB, NS])
        hist = sb("hist", [P, 4, P])
        tail = sb("tail", [P, 4, PAD * (NB + 1)])
        tail_t = sb("tail_t", [PAD * (NB + 1), 4, P])
        cw, cb = sb("cw", [P, 4, 4]), sb("cbias", [P, 4])
        dtg, dtag, dsg, deg, cdg = [sb(n, [P, RT, HPG]) for n in ("g_dt", "g_dta", "g_dsum", "g_dte", "g_decay")]
        bdg, dg, mn = sb("g_bdecay", [P, 2, NB]), sb("g_d", [P, 2]), sb("g_mn", [P, 2])

        acc = [bank("sacc0"), bank("sacc1")]
        tp = [bank("stp0"), bank("stp1")]
        al, cbb, stb, yy = bank("decay_rows"), bank("cb"), bank("states"), bank("ys")

        hist_clear, hist_in, h0_in = sem("hist_clear"), sem("hist_in"), sem("h0_in")
        tail_st, state_st, h0_st, gb_st, y_st = sem("tail_st"), sem("state_st"), sem("h0_st"), sem("gb_st"), sem("y_st")
        front, yy_done, st_done, norm_done = sem("front_done"), sem("yy_done"), sem("st_done"), sem("norm_sum")
        e_done, sg_done, gb_done, sq_done, rt_done = sem("e_done"), sem("sg_done"), sem("gb_done"), sem("ysq_done"), sem("rt_done")
        seg_done, m_done, y_read, h_done, conv_done, silu_done = (
            sem("seg_done"), sem("m_done"), sem("y_read"), sem("h_done"), sem("conv_done"), sem("silu_done"))
        gate_mul, var_done, y_done, loaded, xl_done, st_read = (
            sem("gate_mul"), sem("var_done"), sem("y_done"), sem("g_loaded"), sem("xl_done"), sem("st_read"))

        def b_end(i, n):
            return HEAD + b0 + BPI * i + n + 1

        def a_end(i, n):
            return HEAD + ba0 + BPI * i + n + 1

        def tpv(i, ev):
            return HEAD + t0 + NTP2 * i + SSD_TP.index(ev) + 1

        def channels(i):
            return ((0, 2, i * HC), (2, 1, D + i * NS), (3, 1, D + NG * NS + i * NS))

        with nc.Block() as block:
            @block.sync
            def _(sp):
                def body(i, last):
                    def weight(j):
                        if j < 4:
                            src = tiles(i, j + 4)
                        else:
                            src = next_tiles[j - 4] if last else tiles(i + 1, j - 4)
                        S.W.load(sp, u0 + 4 + j, PER, i, src)

                    sp.wait_ge(S.tp_done, HEAD + t0 + NTP2 * i)
                    for t, n, c in channels(i):
                        sp.dma_start(hist[0:NB * PAD, t:t + n, :].rearrange("r t c -> r (t c)"),
                                     A.state_conv[0].rearrange("b s c -> (b s) c")[:, ds(c, n * P)]).then_inc(hist_in, 16)
                    sp.wait_ge(h0_st, 32 * i)
                    for q in range(2):
                        sp.dma_start(h0[:, q, :, :], A.state_ssm[0, :, ds(4 * i + 2 * q, 2)]
                                     .rearrange("b h p n -> (h p) b n")).then_inc(h0_in, 16)
                    for j in range(4):
                        weight(j)
                    sp.wait_ge(S.tp_drained, tpv(i, "tail"))
                    for t, n, c in channels(i):
                        src = tail_t[:, t:t + n, :].rearrange("r t c -> r (t c)")
                        sp.dma_start(A.new_conv_prompt[0, 0, :, ds(c, n * P)], src[0:PAD, :]).then_inc(tail_st, 16)
                        sp.dma_start(A.new_conv_sample[0].rearrange("b s c -> (b s) c")[:, ds(c, n * P)],
                                     src[PAD:, :]).then_inc(tail_st, 16)
                    for j in range(4, 8):
                        weight(j)
                    sp.wait_ge(S.tp_drained, tpv(i, "state"))
                    for q in range(2):
                        sp.dma_start(A.new_ssm_prompt[0, 0, ds(4 * i + 2 * q, 2)].rearrange("h p n -> (h p) n"),
                                     state_out[:, q, :]).then_inc(state_st, 16)
                    sp.wait_ge(st_read, 4 * i + 4)
                    for q in range(2):
                        sp.dma_start(A.new_ssm_sample[0, :, ds(4 * i + 2 * q, 2)].rearrange("b h p n -> (h p) b n"),
                                     h0[:, q, :, :]).then_inc(h0_st, 16)
                    sp.wait_ge(gb_done, 2 * i + 2)
                    sp.dma_start(S.d_gate_b[ds(2 * i, 2)].rearrange("k p n -> p k n"), gb[:, :, :]).then_inc(gb_st, 16)
                    sp.wait_ge(y_done, 2 * i + 2)
                    sp.dma_start(S.d_y[ds(2 * i, 2)].rearrange("k p n -> p k n"), y[:, 0:2, :]).then_inc(y_st, 16)

                sp.wait_ge(hist_clear, 1)
                with sp.Fori(0, NG - 1) as i:
                    body(i, False)
                body(NG - 1, True)
                for s, n in ((tail_st, 96), (state_st, 32), (h0_st, 32), (gb_st, 16), (y_st, 16)):
                    sp.wait_ge(s, NG * n)

            @block.tensor
            def _(pe):
                rhs = (S.R0_hi, S.R0_lo)

                def product(i, n):
                    product_block(S, pe, None, (u0 + n // 3) % 2, acc[n % 2], rhs, n % 3,
                                  HEAD + u0 + PER * i + n // 3 + 1,
                                  (S.acc_read_a, HEAD + ba0 + BPI * i + n - 1))

                def open_tp(i, ev):
                    n = SSD_TP.index(ev)
                    pe.wait_ge(S.tp_drained, HEAD + t0 + NTP2 * i + n - 1)
                    return tp[n % 2]

                def begin_front(i, c):
                    rows = slice(c * P, (c + 1) * P)
                    out = open_tp(i, ("rows", c))
                    if c == 0:
                        pe.wait_ge(silu_done, 4 * i + 4)
                        pe.wait_ge(loaded, i + 1)
                    for q in range(3):
                        last = pe.transpose(out[:, q * P:(q + 1) * P], y[:, q, rows], S.ident[:, :])
                    last.then_inc(S.tp_done, 1)
                    if c == 0:
                        pe.wait_ge(var_done, 3 * i)
                    pe.wait_ge(seg_done, RT * i + c)
                    pe.wait_ge(e_done, RT * i + c)
                    tri = S.tri if c < PT else S.tri_s
                    for h in range(HPG):
                        pe.matmul(al[:, h * P:(h + 1) * P], dtag[:, c, h:h + 1].to_broadcast([P, P]), tri[:, :],
                                  start=True, stop=True)
                    pe.matmul(cbb[:, 0:P], y[:, 2, rows], y[:, 3, rows], start=True, stop=True).then_inc(front, 1)

                def back(i, c):
                    rows = slice(c * P, (c + 1) * P)
                    pe.wait_ge(m_done, RT * i + c + 1)
                    pe.wait_ge(y_read, RT * i + c)
                    for h in range(HPG):
                        half = slice(64 * (h % 2), 64 * (h % 2) + 64)
                        pe.matmul(yy[half, (h // 2) * P:(h // 2 + 1) * P], dx[c % 2][:, h, :], seg[c % 2][:, h, :],
                                  start=True, stop=True)
                    if c < PT:
                        pe.wait_ge(h_done, PT * i + i + c + 1)
                        for q in range(2):
                            last = pe.matmul(yy[:, (2 + q) * P:(3 + q) * P],
                                             state[:, 2 * q:2 * q + 2, :].rearrange("p h d -> p (h d)"),
                                             y[:, 3, rows], start=True, stop=True)
                        last.then_inc(yy_done, 1)
                        pe.matmul(stb[:, 0:HC], b_rows[c % 2][:, :],
                                  dxe[c % 2][:, :, :].rearrange("p h d -> p (h d)"),
                                  start=True, stop=True).then_inc(st_done, 1)
                        return
                    pe.wait_ge(h0_in, 32 * i + 32)
                    for b in range(NB):
                        out = open_tp(i, ("h0", b))
                        for q in range(2):
                            last = pe.transpose(out[:, q * P:(q + 1) * P], h0[:, q, b, :], S.ident[:, :])
                        last.then_inc(S.tp_done, 1)
                        if b >= 1:
                            off_rows(i, b - 1)
                    off_rows(i, NB - 1)
                    pe.wait_ge(h_done, PT * i + i + PT + 1)
                    out = open_tp(i, "state")
                    for q in range(2):
                        last = pe.transpose(out[:, q * P:(q + 1) * P],
                                            state[:, 2 * q:2 * q + 2, :].rearrange("p h d -> p (h d)"), S.ident[:, :])
                    last.then_inc(S.tp_done, 1)
                    for n in range(4):
                        pe.wait_ge(st_read, 4 * i + max(n - 1, 0))
                        dst = (stb, cbb)[n % 2]
                        pe.matmul(dst[:, :], dxe[c % 2][:, 2 * (n // 2):2 * (n // 2) + 2, :].rearrange("p h d -> p (h d)"),
                                  b_blk[:, 4 * (n % 2):4 * (n % 2) + 4, :].rearrange("p b n -> p (b n)"),
                                  start=True, stop=True).then_inc(st_done, 1)

                def off_rows(i, b):
                    pe.wait_ge(S.tp_drained, tpv(i, ("h0", b)))
                    for q in range(2):
                        last = pe.matmul(yy[:, (2 + q) * P + TD * b:(2 + q) * P + TD * (b + 1)],
                                         h0_t[b % 2][:, q * P:(q + 1) * P],
                                         y[:, 3, SEQ + TD * b:SEQ + TD * (b + 1)], start=True, stop=True)
                    if b == NB - 1:
                        last.then_inc(yy_done, 1)

                with pe.Fori(0, NG) as i:
                    out = open_tp(i, "hist")
                    pe.wait_ge(hist_in, 48 * i + 48)
                    for q in range(4):
                        last = pe.transpose(out[:, q * P:(q + 1) * P], hist[:, q, :], S.ident[:, :])
                    last.then_inc(S.tp_done, 1)
                    for n in range(15):
                        product(i, n)
                    out = open_tp(i, "tail")
                    pe.wait_ge(xl_done, i + 1)
                    for q in range(4):
                        last = pe.transpose(out[0:PAD * (NB + 1), q * P:(q + 1) * P], tail[:, q, :], S.ident[:, :])
                    last.then_inc(S.tp_done, 1)
                    begin_front(i, 0)
                    for c in range(RT):
                        product(i, 15 + c)
                        if c < PT:
                            begin_front(i, c + 1)
                        back(i, c)
                    for rb in range(NRB):
                        out = (al, cbb, stb)[rb]
                        pe.wait_ge(sq_done, 2 * i + 2)
                        pe.wait_ge(st_read, 4 * i + 4)
                        for q in range(2):
                            last = pe.matmul(out[:, 0:RBN], S.ones[:, :], zt[:, q, rb * RBN:(rb + 1) * RBN],
                                             start=(q == 0), stop=(q == 1))
                        last.then_inc(norm_done, 1)

            @block.scalar
            def _(act):
                def split(i, j):
                    S.W.split_hi(act, u0 + j + 2, PER, i, b_end(i, 3 * j + 2))

                def copy_block(i, n):
                    act.wait_ge(S.acc_done, b_end(i, n))
                    src = acc[n % 2][:, 0:RBN]
                    q, rb = n // 3, n % 3
                    if q < 4:
                        if n == 0:
                            act.wait_ge(conv_done, 4 * i)
                            act.wait_ge(xl_done, i)
                        m = RBN if rb < 2 else SEQ - 2 * RBN
                        ins = act.activation(xp[:, q, PAD + rb * RBN:PAD + rb * RBN + m], src[:, 0:m], ACT.Copy)
                        if rb == 2:
                            ins = act.activation(
                                xp[:, q, XW:].rearrange("p (b s) -> p b s", b=NB)[:, :, PAD:],
                                src[:, m:].rearrange("p (b s) -> p b s", b=NB), ACT.Copy)
                    elif q < 6:
                        if n == 12:
                            act.wait_ge(norm_done, 3 * i)
                        ins = act.activation(zt[:, q - 4, rb * RBN:(rb + 1) * RBN], src, ACT.Copy)
                    else:
                        if n == 18:
                            act.wait_ge(gb_st, 16 * i)
                        ins = act.activation(gb[:, q - 6, rb * RBN:(rb + 1) * RBN], src, ACT.Copy)
                    ins.then_inc(S.acc_read_a, 1)
                    if n % 3 == 2:
                        split(i, q)

                def silu_sig(i, q):
                    act.wait_ge(conv_done, 4 * i + q + 1)
                    act.wait_ge(silu_done, 4 * i + q)
                    if q == 0:
                        act.wait_ge(gate_mul, 2 * i)
                    act.activation(sg[:, :], y[:, q, :], ACT.Sigmoid).then_inc(sg_done, 1)

                def exps(i, c):
                    act.wait_ge(front, RT * i + c + 1)
                    act.wait_ge(y_read, max(c - 1, 0) + RT * i)
                    act.wait_ge(seg_done, RT * i + c + 1)
                    rows = al[:, :].rearrange("p (q h n) -> p q h n", q=2, h=2)
                    for h in range(2):
                        half = slice(64 * h, 64 * h + 64)
                        act.activation(grow[c % 2][half, :, :], rows[half, :, h, :], ACT.Exp)
                    act.activation(seg[c % 2][:, :, :], seg[c % 2][:, :, :], ACT.Exp).then_inc(e_done, 1)

                with act.Fori(0, NG) as i:
                    for n in range(15):
                        copy_block(i, n)
                        if n >= 5 and n % 3 == 2 and n < 15:
                            silu_sig(i, (n - 5) // 3)
                    exps(i, 0)
                    for c in range(RT):
                        copy_block(i, 15 + c)
                        if c + 1 < RT:
                            exps(i, c + 1)
                    for q in range(2):
                        act.wait_ge(silu_done, 4 * i + 4)
                        act.wait_ge(gate_mul, 2 * i + q)
                        act.wait_ge(S.acc_read_a, a_end(i, BPI - 1))
                        act.activation(sg[:, :], zt[:, q, :], ACT.Sigmoid).then_inc(sg_done, 1)
                        act.activation(gb[:, q, :], gb[:, q, :], ACT.Sigmoid).then_inc(gb_done, 1)
                    for q in range(2):
                        act.wait_ge(gate_mul, 2 * i + q + 1)
                        act.activation(zt[:, q, :], y[:, q, :], ACT.Square).then_inc(sq_done, 1)
                    for rb in range(NRB):
                        act.wait_ge(var_done, 3 * i + rb + 1)
                        cols = slice(rb * RBN, (rb + 1) * RBN)
                        act.activation(rs[:, cols], rs[:, cols], ACT.Sqrt).then_inc(rt_done, 1)

            @block.vector
            def _(dve):
                steps = S.dve_steps

                def link(ins):
                    pos = steps.mark(ins)
                    dve.wait_ge(steps.sem, steps.value(pos))

                def drain(i, ev):
                    dve.wait_ge(S.tp_done, tpv(i, ev))
                    return tp[SSD_TP.index(ev) % 2]

                def split(i, j):
                    S.W.split_lo(dve, u0 + j + 2, PER, i, b_end(i, 3 * j + 2))

                def group_vectors(i):
                    tab = S.vec[:, V_CW:V_CB].rearrange("p (t c) -> p t c", t=4)
                    for (t, n, first) in ((0, 2, 2 * i), (2, 1, KT + i), (3, 1, KT + NG + i)):
                        dve.tensor_copy(cw[:, :, t:t + n], tab[:, :, ds(first, n)])
                        dve.tensor_copy(cb[:, t:t + n], S.vec[:, ds(V_CB + first, n)])
                    dve.tensor_copy(mn[:, :], S.vec[:, ds(V_MN + 2 * i, 2)])
                    dve.tensor_copy(dg[:, :], S.d_chan[:, ds(2 * i, 2)])
                    dve.tensor_copy(bdg[:, :, :], S.batch_decay[:, ds(2 * i, 2), :])
                    for dst, src in ((dtg, S.dt), (dtag, S.dta), (dsg, S.dsum), (deg, S.dt_end), (cdg, S.chunk_decay)):
                        last = dve.tensor_copy(dst[:, :, :], src[:, :, ds(4 * i, 4)])
                    last.then_inc(loaded, 1)
                    dve.wait_ge(loaded, i + 1)

                def conv(i, q):
                    dve.wait_ge(S.acc_read_a, a_end(i, 3 * q + 2))
                    if q == 0:
                        dve.wait_ge(y_st, 16 * i)
                    p_in = xp[:, q, :]
                    s_in = xp[:, q, XW:].rearrange("p (b s) -> p b s", b=NB)
                    p_out = y[:, q, 0:SEQ]
                    s_out = y[:, q, SEQ:].rearrange("p (b s) -> p b s", b=NB)
                    for t in range(4):
                        for out, src in ((p_out, p_in[:, t:t + SEQ]), (s_out, s_in[:, :, t:t + TD])):
                            w = cw[:, t, q:q + 1]
                            if t == 0:
                                ins = dve.tensor_scalar(out, src, w, cb[:, q:q + 1], ALU.mult, ALU.add)
                            else:
                                dve.wait_ge(steps.sem, steps.value(steps.pos - 1))
                                ins = dve.scalar_tensor_tensor(out, src, w, out, ALU.mult, ALU.add)
                            if t == 3 and out is s_out:
                                ins.then_inc(conv_done, 1)
                            else:
                                steps.mark(ins)

                def silu(i, q):
                    dve.wait_ge(sg_done, 6 * i + q + 1)
                    dve.tensor_tensor(y[:, q, :], y[:, q, :], sg[:, :], ALU.mult).then_inc(silu_done, 1)

                def tails(i):
                    dve.tensor_copy(tail[:, :, 0:PAD], xp[:, :, XW - PAD:XW])
                    src = xp[:, :, XW:].rearrange("p q (b s) -> p q b s", b=NB)[:, :, :, TD:]
                    dve.tensor_copy(tail[:, :, PAD:].rearrange("p q (b s) -> p q b s", b=NB), src).then_inc(xl_done, 1)
                    n = PAD * (NB + 1)
                    src = drain(i, "tail")
                    dve.wait_ge(tail_st, 96 * i)
                    dve.tensor_copy(tail_t[:, :, :].rearrange("r q c -> r (q c)"), src[0:n, :]).then_inc(S.tp_drained, 1)

                def rows(i, c):
                    src = drain(i, ("rows", c))
                    dve.wait_ge(st_done, 12 * i + max(c - 1, 0))
                    x = src[:, 0:HC].rearrange("p (h d) -> p h d", h=HPG)
                    for dst, s in ((dx, dtg), (dxe, deg)):
                        dve.tensor_tensor(dst[c % 2][:, :, :], x,
                                          s[:, c, :].unsqueeze(2).to_broadcast([P, HPG, HD]), ALU.mult)
                    dve.tensor_copy(b_rows[c % 2][:, :], src[:, HC:HC + NS]).then_inc(S.tp_drained, 1)

                def decays(i, c):
                    dve.wait_ge(front, RT * i + c + 1)
                    if c >= 1:
                        dve.wait_ge(m_done, RT * i + c)
                    if c >= 2:
                        dve.wait_ge(yy_done, RT * i + c - 1)
                    dve.tensor_tensor(cbm[:, :], cbb[:, 0:P], (S.tri if c < PT else S.tri_s)[:, :], ALU.mult)
                    s = seg[c % 2]
                    link(dve.tensor_tensor(s[:, :, :], al[:, :].rearrange("p (h n) -> p h n", h=HPG),
                                           dsg[:, c, :].unsqueeze(2).to_broadcast([P, HPG, P]), ALU.subtract))
                    dve.tensor_scalar(s[:, :, :], s[:, :, :], 0.0, None, ALU.min).then_inc(seg_done, 1)

                def mix(i, c):
                    dve.wait_ge(e_done, RT * i + c + 1)
                    s = seg[c % 2]
                    dve.tensor_tensor(s[:, :, :], s[:, :, :], cbm[:, :].unsqueeze(1).to_broadcast([P, HPG, P]),
                                      ALU.mult).then_inc(m_done, 1)

                def outputs(i, c):
                    rows_ = slice(c * P, (c + 1) * P)
                    dve.wait_ge(yy_done, RT * i + c + 1)
                    for q in range(2):
                        dve.scalar_tensor_tensor(y[:, q, rows_], y[:, q, rows_], dg[:, q:q + 1],
                                                 yy[:, q * P:(q + 1) * P], ALU.mult, ALU.add)
                    link(dve.tensor_tensor(off[:, :, :], yy[:, 2 * P:4 * P].rearrange("p (q n) -> p q n", q=2),
                                           grow[c % 2][:, :, :], ALU.mult))
                    dve.tensor_tensor(y[:, 0:2, rows_], y[:, 0:2, rows_], off[:, :, :], ALU.add).then_inc(y_read, 1)
                    dve.wait_ge(y_read, RT * i + c + 1)

                def advance(i, c):
                    link(dve.tensor_tensor(state[:, :, :], state[:, :, :],
                                           cdg[:, c, :].unsqueeze(2).to_broadcast([P, HPG, HD]), ALU.mult))
                    dve.wait_ge(st_done, 12 * i + c + 1)
                    dve.tensor_tensor(state[:, :, :], state[:, :, :],
                                      stb[:, 0:HC].rearrange("p (h d) -> p h d", h=HPG), ALU.add).then_inc(h_done, 1)

                def sample_states(i):
                    for b in range(NB):
                        src = drain(i, ("h0", b))
                        if b == 0:
                            dve.wait_ge(yy_done, RT * i + PT)
                        dve.tensor_copy(h0_t[b % 2][:, :], src[:, 0:2 * P]).then_inc(S.tp_drained, 1)
                    outputs(i, PT)
                    src = drain(i, "state")
                    dve.wait_ge(state_st, 32 * i)
                    dve.tensor_copy(state_out[:, :, :].rearrange("p q n -> p (q n)"), src[:, 0:2 * P])\
                       .then_inc(S.tp_drained, 1)
                    for n in range(4):
                        q, half = n // 2, n % 2
                        dve.wait_ge(st_done, 12 * i + PT + n + 1)
                        for b in range(4):
                            ins = dve.scalar_tensor_tensor(
                                h0[:, q, 4 * half + b, :], h0[:, q, 4 * half + b, :], bdg[:, q, 4 * half + b:4 * half + b + 1],
                                (stb, cbb)[n % 2][:, b * NS:(b + 1) * NS], ALU.mult, ALU.add)
                        ins.then_inc(st_read, 1)

                dve.memset(xp[:, :, 0:PAD], 0.0)
                dve.memset(hist[:, :, :], 0.0).then_inc(hist_clear, 1)
                with dve.Fori(0, NG) as i:
                    steps.body(i, SSD_STEPS)
                    dve.wait_ge(y_done, 2 * i)
                    group_vectors(i)
                    src = drain(i, "hist")
                    dve.wait_ge(xl_done, i)
                    dve.tensor_copy(xp[:, :, XW:].rearrange("p q (b s) -> p q b s", b=NB)[:, :, :, 0:PAD],
                                    src[:, :].rearrange("p (q n) -> p q n", q=4)[:, :, 0:NB * PAD]
                                    .rearrange("p q (b s) -> p q b s", s=PAD))\
                       .then_inc(S.tp_drained, 1)
                    dve.wait_ge(S.tp_drained, tpv(i, "hist"))
                    for q in range(4):
                        if q >= 1:
                            split(i, q - 1)
                        conv(i, q)
                        if q >= 1:
                            silu(i, q - 1)
                    split(i, 3)
                    silu(i, 3)
                    tails(i)
                    split(i, 4)
                    dve.wait_ge(norm_done, 3 * i)
                    dve.memset(state[:, :, :], 0.0).then_inc(h_done, 1)
                    rows(i, 0)
                    decays(i, 0)
                    for c in range(RT):
                        mix(i, c)
                        if c < PT:
                            rows(i, c + 1)
                            decays(i, c + 1)
                        if c % 3 == 2:
                            split(i, 5 + c // 3)
                        if c < PT:
                            outputs(i, c)
                            advance(i, c)
                        if c == PT - 1:
                            dve.tensor_tensor(b_blk[:, :, :], b_rows[PT % 2][:, :].unsqueeze(1).to_broadcast([P, NB, NS]),
                                              S.same_batch[:, 0:P:TD].unsqueeze(2).to_broadcast([P, NB, NS]), ALU.mult)
                    sample_states(i)
                    for q in range(2):
                        dve.wait_ge(sg_done, 6 * i + 4 + q + 1)
                        link(dve.tensor_tensor(zt[:, q, :], zt[:, q, :], sg[:, :], ALU.mult))
                        dve.tensor_tensor(y[:, q, :], y[:, q, :], zt[:, q, :], ALU.mult).then_inc(gate_mul, 1)
                    for rb in range(NRB):
                        cols = slice(rb * RBN, (rb + 1) * RBN)
                        dve.wait_ge(norm_done, 3 * i + rb + 1)
                        dve.tensor_scalar(rs[:, cols], (al, cbb, stb)[rb][:, 0:RBN], 1.0 / HC, EPS, ALU.mult, ALU.add)\
                           .then_inc(var_done, 1)
                    for rb in range(NRB):
                        cols = slice(rb * RBN, (rb + 1) * RBN)
                        dve.wait_ge(rt_done, 3 * i + rb + 1)
                        link(dve.reciprocal(rs[:, cols], rs[:, cols]))
                    for q in range(2):
                        dve.scalar_tensor_tensor(y[:, q, :], y[:, q, :], mn[:, q:q + 1], rs[:, :],
                                                 ALU.mult, ALU.mult).then_inc(y_done, 1)
                    steps.end(0)
                steps.base += NG * SSD_STEPS


def tools(nc, S, ctx, tag):
    def sb(name, shape, dt=F32):
        return ctx.enter_context(nc.sbuf_tensor(f"{tag}_{name}", shape, dt))

    def bank(name):
        return ctx.enter_context(nc.psum_tensor(f"{tag}_{name}", [P, 512], F32))

    def sem(name):
        return S.sem(f"{tag}_{name}")
    return sb, bank, sem


def tile_of(t, k):
    return t[ds(k, 1)].rearrange("a p n -> (a p) n")


def flat_tile(t, k, cols=slice(0, ROWS)):
    return t[:, ds(k, 1), cols].rearrange("p a n -> p (a n)")


def rb_cols(rb):
    return slice(rb * RBN, (rb + 1) * RBN)


def stream_pairs(S, sp, u0, tiles, next_tiles, work, before=lambda i, j: None):
    n = KT // 2
    with sp.Fori(0, n - 2) as i:
        for j in range(2):
            before(i, j)
            S.W.load(sp, u0 + 4 + j, 2, i, tiles(i + 2, j))
            work(i, j, False)
    for i in range(n - 2, n):
        for j in range(2):
            before(i, j)
            S.W.load(sp, u0 + 4 + j, 2, i, next_tiles[2 * (i - n + 2) + j])
            work(i, j, i == n - 1)


def stage_branch_a(nc, S, A, b0, bv0, u0, tiles, next_tiles):
    with ExitStack() as ctx:
        sb, bank, sem = tools(nc, S, ctx, "a")
        src_t = [sb(f"src{n}", [P, ROWS]) for n in range(2)]
        gate = [sb(f"gate{n}", [P, ROWS]) for n in range(2)]
        out = [sb(f"out{n}", [P, ROWS]) for n in range(2)]
        acc = [bank("acc0"), bank("acc1")]
        src_in = [sem("src_in0"), sem("src_in1")]
        gate_in = [sem("gate_in0"), sem("gate_in1")]
        stored = [sem("st0"), sem("st1")]
        hi_done, lo_done = sem("hi"), sem("lo")

        with nc.Block() as block:
            @block.sync
            def _(sp):
                def source(src, m, j):
                    sp.wait_ge(lo_done, m - 1)
                    sp.dma_start(src_t[j][:, :], src).then_inc(src_in[j], 16)

                def load_gate(i, j):
                    sp.dma_start(gate[j][:, :], tile_of(S.d_gate_a, 2 * i + j)).then_inc(gate_in[j], 16)

                for m in range(KT):
                    if m < 2:
                        sp.dma_start(src_t[m][:, :], S.d_y[m]).then_inc(src_in[m], 16)
                        load_gate(0, m)
                    else:
                        source(S.d_y[m], m, m % 2)

                def before(i, j):
                    source(tile_of(S.d_o, 2 * i + j), 2 * i + KT + j, j)

                def work(i, j, last):
                    sp.wait_ge(S.acc_read_v, HEAD + bv0 + 6 * i + 3 * j + 3)
                    sp.dma_start(tile_of(S.d_ta, 2 * i + j), out[j][:, :]).then_inc(stored[j], 16)
                    if not last:
                        load_gate(i + 1, j)

                stream_pairs(S, sp, u0, tiles, next_tiles, work, before)
                for j in range(2):
                    sp.wait_ge(stored[j], 16 * KT // 2)

            @block.tensor
            def _(pe):
                pe.wait_ge(lo_done, KT)
                pe.wait_ge(hi_done, KT)
                with pe.Fori(0, KT // 2) as i:
                    for n in range(6):
                        product_block(S, pe, None, (u0 + n // 3) % 2, acc[n % 2], (S.R1_hi, S.R1_lo), n % 3,
                                      HEAD + u0 + 2 * i + n // 3 + 1, (S.acc_read_v, HEAD + bv0 + 6 * i + n - 1))

            @block.scalar
            def _(act):
                for m in range(KT):
                    act.wait_ge(src_in[m % 2], 16 * (m // 2 + 1))
                    act.activation(S.R1_hi[:, m, :], src_t[m % 2][:, :], ACT.Copy).then_inc(hi_done, 1)
                with act.Fori(0, KT // 2) as i:
                    for j in range(2):
                        act.wait_ge(src_in[j], 16 * (KT // 2 + 1) + 16 * i)
                        act.activation(flat_tile(S.R0_hi, 2 * i + j), src_t[j][:, :], ACT.Copy).then_inc(hi_done, 1)
                        S.W.split_hi(act, u0 + j + 2, 2, i, HEAD + b0 + 6 * i + 3 * j + 3)

            @block.vector
            def _(dve):
                for m in range(KT):
                    dve.wait_ge(hi_done, m + 1)
                    dve.tensor_tensor(S.R1_lo[:, m, :], src_t[m % 2][:, :], S.R1_hi[:, m, :].bitcast(F32),
                                      ALU.subtract).then_inc(lo_done, 1)
                with dve.Fori(0, KT // 2) as i:
                    for n in range(6):
                        j = n // 3
                        if n % 3 == 0:
                            dve.wait_ge(gate_in[j], 16 * i + 16)
                            dve.wait_ge(stored[j], 16 * i)
                        dve.wait_ge(S.acc_done, HEAD + b0 + 6 * i + n + 1)
                        dve.tensor_tensor(out[j][:, rb_cols(n % 3)], acc[n % 2][:, 0:RBN], gate[j][:, rb_cols(n % 3)],
                                          ALU.mult).then_inc(S.acc_read_v, 1)
                        if n % 3 == 1:
                            dve.wait_ge(hi_done, 2 * i + KT + j + 1)
                            dve.tensor_tensor(flat_tile(S.R0_lo, 2 * i + j), src_t[j][:, :],
                                              flat_tile(S.R0_hi, 2 * i + j).bitcast(F32), ALU.subtract)\
                               .then_inc(lo_done, 1)
                        if n % 3 == 2:
                            S.W.split_lo(dve, u0 + j + 2, 2, i, HEAD + b0 + 6 * i + 3 * j + 3)


def stage_branch_b(nc, S, A, b0, bv0, u0, tiles, next_tiles):
    with ExitStack() as ctx:
        sb, bank, sem = tools(nc, S, ctx, "b")
        gate = [sb(f"gate{n}", [P, ROWS]) for n in range(2)]
        part = [sb(f"part{n}", [P, ROWS]) for n in range(2)]
        prod = [sb(f"prod{n}", [P, RBN]) for n in range(2)]
        acc = [bank("acc0"), bank("acc1")]
        gate_in = [sem("gate_in0"), sem("gate_in1")]
        hi_done, sum_done, mul_done, lo_done = sem("hi"), sem("sum"), sem("mul"), sem("lo")

        with nc.Block() as block:
            @block.sync
            def _(sp):
                def arrive(i, j):
                    for dst, src in ((gate, S.d_gate_b), (part, S.d_ta)):
                        sp.dma_start(dst[j][:, :], tile_of(src, 2 * i + j)).then_inc(gate_in[j], 16)

                def work(i, j, last):
                    if not last:
                        sp.wait_ge(lo_done, 6 * i + 3 * j + 3)
                        arrive(i + 1, j)

                arrive(0, 0)
                arrive(0, 1)
                stream_pairs(S, sp, u0, tiles, next_tiles, work)

            @block.tensor
            def _(pe):
                with pe.Fori(0, KT // 2) as i:
                    for n in range(6):
                        product_block(S, pe, None, (u0 + n // 3) % 2, acc[n % 2], (S.R0_hi, S.R0_lo), n % 3,
                                      HEAD + u0 + 2 * i + n // 3 + 1, (S.acc_read_v, HEAD + bv0 + 6 * i + n - 1))

            @block.scalar
            def _(act):
                with act.Fori(0, KT // 2) as i:
                    for n in range(6):
                        j = n // 3
                        act.wait_ge(sum_done, 6 * i + n + 1)
                        act.activation(S.R1_hi[:, ds(2 * i + j, 1), rb_cols(n % 3)].rearrange("p a n -> p (a n)"),
                                       part[j][:, rb_cols(n % 3)], ACT.Copy).then_inc(hi_done, 1)
                        if n % 3 == 2:
                            S.W.split_hi(act, u0 + j + 2, 2, i, HEAD + b0 + 6 * i + 3 * j + 3)

            @block.vector
            def _(dve):
                def low(i, n):
                    j, cols = n // 3, rb_cols(n % 3)
                    dve.wait_ge(hi_done, 6 * i + n + 1)
                    d = ds(2 * i + j, 1)
                    dve.tensor_tensor(S.R1_lo[:, d, cols].rearrange("p a n -> p (a n)"), part[j][:, cols],
                                      S.R1_hi[:, d, cols].rearrange("p a n -> p (a n)").bitcast(F32),
                                      ALU.subtract).then_inc(lo_done, 1)

                with dve.Fori(0, KT // 2) as i:
                    for n in range(6):
                        j, cols = n // 3, rb_cols(n % 3)
                        if n % 3 == 0:
                            dve.wait_ge(gate_in[j], 32 * i + 32)
                        dve.wait_ge(S.acc_done, HEAD + b0 + 6 * i + n + 1)
                        dve.tensor_tensor(prod[n % 2][:, :], acc[n % 2][:, 0:RBN], gate[j][:, cols], ALU.mult)\
                           .then_inc(S.acc_read_v, 1)
                        dve.wait_ge(S.acc_read_v, HEAD + bv0 + 6 * i + n + 1)
                        dve.tensor_tensor(part[j][:, cols], part[j][:, cols], prod[n % 2][:, :], ALU.add)\
                           .then_inc(sum_done, 1)
                        if n % 3 == 2:
                            S.W.split_lo(dve, u0 + j + 2, 2, i, HEAD + b0 + 6 * i + 3 * j + 3)
                        low(i, n)


def stage_out(nc, S, A, b0, bv0, u0, tiles, next_tiles):
    with ExitStack() as ctx:
        sb, bank, sem = tools(nc, S, ctx, "c")
        xr = [sb(f"xr{n}", [P, RT, P]) for n in range(2)]
        xs = [sb(f"xs{n}", [P, ROWS]) for n in range(2)]
        sq = [sb(f"sq{n}", [P, RBN]) for n in range(2)]
        gcol = sb("gcol", [P, 2])
        acc = [bank("acc0"), bank("acc1")]
        x_in, stored = [sem("x_in0"), sem("x_in1")], [sem("st0"), sem("st1")]
        hi_done, lo_done, sq_done, ss_done, col_done, zeroed = (
            sem("hi"), sem("lo"), sem("sq"), sem("ss"), sem("col"), sem("zeroed"))

        with nc.Block() as block:
            @block.sync
            def _(sp):
                def x_cols(i, j):
                    cols = ds((2 * i + j) * P, P)
                    sp.dma_start(xr[j][:, 0:PT, :], A.x_prompt[0].rearrange("(r p) c -> p r c", p=P)[:, :, cols])\
                      .then_inc(x_in[j], 16)
                    sp.dma_start(xr[j][:, PT, :], A.x_sample.rearrange("b t c -> (b t) c")[:, cols])\
                      .then_inc(x_in[j], 16)

                def work(i, j, last):
                    sp.wait_ge(S.acc_read_v, HEAD + bv0 + 6 * i + 3 * j + 3)
                    sp.dma_start(tile_of(S.d_x, 2 * i + j), xs[j][:, :]).then_inc(stored[j], 16)
                    if not last:
                        x_cols(i + 1, j)

                x_cols(0, 0)
                x_cols(0, 1)
                stream_pairs(S, sp, u0, tiles, next_tiles, work)
                for j in range(2):
                    sp.wait_ge(stored[j], 16 * KT // 2)

            @block.tensor
            def _(pe):
                with pe.Fori(0, KT // 2) as i:
                    for n in range(6):
                        j, rb, a = n // 3, n % 3, acc[n % 2]

                        def add_x():
                            pe.wait_ge(x_in[j], 32 * i + 32)
                            for r in range(3):
                                last = pe.matmul(a[:, r * P:(r + 1) * P], xr[j][:, 3 * rb + r, :], S.ident[:, :],
                                                 start=False, stop=(r == 2))
                            return last
                        product_block(S, pe, None, (u0 + j) % 2, a, (S.R1_hi, S.R1_lo), rb,
                                      HEAD + u0 + 2 * i + j + 1, (S.acc_read_v, HEAD + bv0 + 6 * i + n - 1), more=add_x)

            @block.scalar
            def _(act):
                with act.Fori(0, KT // 2) as i:
                    for n in range(6):
                        j, cols = n // 3, rb_cols(n % 3)
                        act.wait_ge(S.acc_read_v, HEAD + bv0 + 6 * i + n + 1)
                        act.wait_ge(ss_done, 6 * i + max(n - 1, 0))
                        act.activation(sq[n % 2][:, :], xs[j][:, cols], ACT.Square).then_inc(sq_done, 1)
                        act.wait_ge(col_done, i + 1)
                        act.activation(S.R0_hi[:, ds(2 * i + j, 1), cols].rearrange("p a n -> p (a n)"), xs[j][:, cols],
                                       ACT.Copy, scale=gcol[:, j:j + 1]).then_inc(hi_done, 1)
                        if n % 3 == 2:
                            S.W.split_hi(act, u0 + j + 2, 2, i, HEAD + b0 + 6 * i + 3 * j + 3)

            @block.vector
            def _(dve):
                dve.memset(S.ss[:, :], 0.0).then_inc(zeroed, 1)
                with dve.Fori(0, KT // 2) as i:
                    dve.wait_ge(hi_done, 6 * i)
                    dve.wait_ge(lo_done, 6 * i)
                    dve.tensor_copy(gcol[:, :], S.vec[:, ds(V_FFN + 2 * i, 2)]).then_inc(col_done, 1)
                    dve.wait_ge(col_done, i + 1)
                    for n in range(6):
                        j, cols = n // 3, rb_cols(n % 3)
                        if n % 3 == 0:
                            dve.wait_ge(stored[j], 16 * i)
                            dve.wait_ge(sq_done, 6 * i)
                        dve.wait_ge(S.acc_done, HEAD + b0 + 6 * i + n + 1)
                        dve.tensor_copy(xs[j][:, cols], acc[n % 2][:, 0:RBN]).then_inc(S.acc_read_v, 1)
                        dve.wait_ge(hi_done, 6 * i + n + 1)
                        d = ds(2 * i + j, 1)
                        dve.scalar_tensor_tensor(S.R0_lo[:, d, cols].rearrange("p a n -> p (a n)"), xs[j][:, cols],
                                                 gcol[:, j:j + 1],
                                                 S.R0_hi[:, d, cols].rearrange("p a n -> p (a n)").bitcast(F32),
                                                 ALU.mult, ALU.subtract).then_inc(lo_done, 1)
                        if n % 3 == 2:
                            S.W.split_lo(dve, u0 + j + 2, 2, i, HEAD + b0 + 6 * i + 3 * j + 3)

            @block.gpsimd
            def _(pool):
                pool.wait_ge(zeroed, 1)
                with pool.Fori(0, KT // 2) as i:
                    for n in range(6):
                        cols = rb_cols(n % 3)
                        pool.wait_ge(sq_done, 6 * i + n + 1)
                        if n >= 3:
                            pool.wait_ge(ss_done, 6 * i + n - 2)
                        pool.tensor_tensor(S.ss[:, cols], S.ss[:, cols], sq[n % 2][:, :], ALU.add).then_inc(ss_done, 1)


def down_tile(A, i, half):
    return A.w_down[0].rearrange("(f k p) c -> f p k c", k=2, p=P)[ds(i, 1), :, :, half * 512:half * 512 + 512]\
        .rearrange("a p k c -> (a p) k c")


def stage_ffn(nc, S, A, b0, bv0, u0, next_tiles):
    N = FT // 2
    with ExitStack() as ctx:
        sb, bank, sem = tools(nc, S, ctx, "f")
        x = S.x_t
        rstd = sb("rstd", [P, ROWS])
        act_hi, act_lo = sb("act_hi", [P, 2, ROWS], F32R), sb("act_lo", [P, 2, ROWS], F32R)
        hid = [sb(f"hid{n}", [P, ROWS]) for n in range(2)]
        gs = [sb(f"gs{n}", [P, RBN]) for n in range(3)]
        sg = [sb(f"sg{n}", [P, RBN]) for n in range(3)]
        acc = [bank(f"acc{n}") for n in range(6)]
        ssum = bank("ssum")
        x_in = sem("x_in")
        sum_done, var_done, root_done = sem("sum"), sem("var"), sem("root")
        sg_done, hi_done, sq_done, xg_done = sem("sg"), sem("hi"), sem("sq"), sem("xg")
        steps = Steps(sem("steps"))
        steps.base = 0
        hid_done, ss_done = sem("hid"), sem("ss")

        def blk(i, part, n):
            if isinstance(i, int) and i == 0:
                return {"up0": 0, "up1": 6}[part] + n
            return 12 + 36 * (i - 1) + {"up0": 0, "down": 6, "up1": 30}[part] + n

        def blk_last(d, rb):
            return 12 + 36 * (N - 1) + 3 * d + rb + 1

        def slot(part, n):
            return ({"up0": 0, "down": 6, "up1": 30}[part] + n) % 6

        with nc.Block() as block:
            def up_tile(i, j):
                w = A.w_gate[0] if j % 2 == 0 else A.w_up[0]
                return wsrc(w, (2 * i + j // 2) * P)

            @block.sync
            def _(sp):
                for k in range(KT):
                    sp.dma_start(x[:, k, :], S.d_x[k]).then_inc(x_in, 16)
                with sp.Fori(0, N - 1) as i:
                    order = (up_tile(i + 1, 0), up_tile(i + 1, 1), down_tile(A, i, 0), down_tile(A, i, 1),
                             up_tile(i + 1, 2), up_tile(i + 1, 3))
                    for j in range(6):
                        S.W.load(sp, u0 + 4 + j, 6, i, order[j])
                u = u0 + 4 + 6 * (N - 1)
                for j, t in enumerate([down_tile(A, N - 1, 0), down_tile(A, N - 1, 1)] + list(next_tiles)):
                    S.W.load(sp, u + j, 2, 0, t)

            @block.tensor
            def _(pe):
                def up(i, part, n):
                    b = blk(i, part, n)
                    t = (0 if part == "up0" else 2) + n // 3 if isinstance(i, int) and i == 0 else \
                        4 + 6 * (i - 1) + (0 if part == "up0" else 4) + n // 3
                    par = ((0 if part == "up0" else 2) + n // 3) % 2
                    product_block(S, pe, None, (u0 + par) % 2, acc[slot(part, n)], (S.R0_hi, S.R0_lo), n % 3,
                                  HEAD + u0 + t + 1, (S.acc_read_v, HEAD + bv0 + b - 5))

                def down(i):
                    for n in range(24):
                        d, rb = n // 3, n % 3
                        half = d // 4
                        final = isinstance(i, int)
                        b = blk(i, "down", n) - (6 if final else 0)
                        pe.wait_ge(S.lo_done, HEAD + u0 + 4 + 6 * (i - 1) + (0 if final else 2) + half + 1)
                        if n == 0:
                            pe.wait_ge(steps.sem, low_value(i))
                        pe.wait_ge(S.acc_read_v, HEAD + bv0 + b - 5)
                        s = (u0 + half) % 2
                        wh = S.w_hi[s][:, :].rearrange("p (k c) -> p k c", k=2)
                        wl = S.w_lo[s][:, :].rearrange("p (k c) -> p k c", k=2)
                        m = 0
                        a = acc[slot("down", n)]
                        for k in range(2):
                            for w, r in ((wh, act_hi), (wh, act_lo), (wl, act_hi)):
                                last = pe.matmul(a[:, 0:RBN], w[:, k, (d % 4) * P:(d % 4 + 1) * P],
                                                 r[:, k, rb_cols(rb)], start=(m == 0), stop=(m == 5))
                                m += 1
                        last.then_inc(S.acc_done, 1)

                def low_value(i):
                    return F_FIRST + F_PASS * (i - 1)

                for rb in range(NRB):
                    if rb >= 1:
                        pe.wait_ge(var_done, rb)
                    pe.matmul(ssum[:, 0:RBN], S.ones[:, :], S.ss[:, rb_cols(rb)], start=True, stop=True)\
                      .then_inc(sum_done, 1)
                pe.wait_ge(S.acc_read_v, HEAD + bv0)
                for n in range(6):
                    up(0, "up0", n)
                for n in range(6):
                    up(0, "up1", n)
                with pe.Fori(1, N) as i:
                    for n in range(6):
                        up(i, "up0", n)
                    down(i)
                    for n in range(6):
                        up(i, "up1", n)
                down(N)

            @block.scalar
            def _(act):
                def split(u, per, i, last):
                    S.W.split_hi(act, u, per, i, last)

                def gates(i, part):
                    for rb in range(3):
                        act.wait_ge(S.acc_read_v, HEAD + bv0 + blk(i, part, rb) + 1)
                        act.activation(sg[rb][:, :], gs[rb][:, :], ACT.Sigmoid).then_inc(sg_done, 1)

                def highs(i, k):
                    for rb in range(3):
                        act.wait_ge(hid_done, 6 * i + 3 * k + rb + 1)
                        if k == 0 and rb == 0 and not (isinstance(i, int) and i == 0):
                            act.wait_ge(S.acc_done, HEAD + b0 + blk(i, "down", 24))
                        act.activation(act_hi[:, k, rb_cols(rb)], hid[k][:, rb_cols(rb)], ACT.Copy).then_inc(hi_done, 1)

                for rb in range(NRB):
                    act.wait_ge(var_done, rb + 1)
                    act.activation(rstd[:, rb_cols(rb)], rstd[:, rb_cols(rb)], ACT.Sqrt).then_inc(root_done, 1)
                split(u0 + 2, 2, 0, HEAD + b0 + 3)
                gates(0, "up0")
                split(u0 + 3, 2, 0, HEAD + b0 + 6)
                highs(0, 0)
                split(u0 + 4, 2, 0, HEAD + b0 + 9)
                gates(0, "up1")
                split(u0 + 5, 2, 0, HEAD + b0 + 12)
                highs(0, 1)
                with act.Fori(1, N) as i:
                    b = HEAD + b0 + 12 + 36 * (i - 1)
                    u = u0 + 6
                    split(u, 6, i - 1, b + 3)
                    gates(i, "up0")
                    split(u + 1, 6, i - 1, b + 6)
                    split(u + 2, 6, i - 1, b + 18)
                    split(u + 3, 6, i - 1, b + 30)
                    highs(i, 0)
                    split(u + 4, 6, i - 1, b + 33)
                    gates(i, "up1")
                    split(u + 5, 6, i - 1, b + 36)
                    highs(i, 1)
                b = HEAD + b0 + 12 + 36 * (N - 1)
                u = u0 + 4 + 6 * (N - 1) + 2
                for d in range(KT):
                    for rb in range(3):
                        act.wait_ge(S.acc_read_v, HEAD + bv0 + blk_last(d, rb))
                        act.wait_ge(ss_done, max(3 * d + rb - 2, 0))
                        act.activation(gs[rb][:, :], x[:, d, rb_cols(rb)], ACT.Square).then_inc(sq_done, 1)
                        act.activation(S.R0_hi[:, d, rb_cols(rb)], x[:, d, rb_cols(rb)], ACT.Copy,
                                       scale=S.vec[:, V_PLE + d:V_PLE + d + 1]).then_inc(hi_done, 1)
                    if d % 4 == 3:
                        split(u + d // 4, 2, 0, b + 3 * d + 3)

            @block.vector
            def _(dve):
                def gate_up(i, part, k):
                    for rb in range(3):
                        n = blk(i, part, rb)
                        dve.wait_ge(S.acc_done, HEAD + b0 + n + 1)
                        dve.tensor_tensor(gs[rb][:, :], acc[slot(part, rb)][:, 0:RBN], rstd[:, rb_cols(rb)], ALU.mult)\
                           .then_inc(S.acc_read_v, 1)
                    split_after(i, part, 0)
                    for rb in range(3):
                        n = blk(i, part, 3 + rb)
                        dve.wait_ge(sg_done, 6 * i + (0 if part == "up0" else 3) + rb + 1)
                        steps.mark(dve.tensor_tensor(gs[rb][:, :], gs[rb][:, :], sg[rb][:, :], ALU.mult))
                        dve.wait_ge(S.acc_done, HEAD + b0 + n + 1)
                        h = hid[k][:, rb_cols(rb)]
                        dve.tensor_tensor(h, acc[slot(part, 3 + rb)][:, 0:RBN], rstd[:, rb_cols(rb)], ALU.mult)\
                           .then_inc(S.acc_read_v, 1)
                        dve.wait_ge(S.acc_read_v, HEAD + bv0 + n + 1)
                        dve.tensor_tensor(h, h, gs[rb][:, :], ALU.mult).then_inc(hid_done, 1)
                    split_after(i, part, 1)

                def lows(i, k):
                    for rb in range(3):
                        cols = rb_cols(rb)
                        dve.wait_ge(hi_done, 6 * i + 3 * k + rb + 1)
                        steps.mark(dve.tensor_tensor(act_lo[:, k, cols], hid[k][:, cols],
                                                     act_hi[:, k, cols].bitcast(F32), ALU.subtract))

                def split_after(i, part, j):
                    if isinstance(i, int) and i == 0:
                        u, last = {"up0": (2, 3), "up1": (4, 9)}[part]
                        S.W.split_lo(dve, u0 + u + j, 2, 0, HEAD + b0 + last + 3 * j)
                        return
                    b = HEAD + b0 + 12 + 36 * (i - 1)
                    u, last = {"up0": (6, 3), "up1": (10, 33)}[part]
                    S.W.split_lo(dve, u0 + u + j, 6, i - 1, b + last + 3 * j)

                def down(i, final=False):
                    b = HEAD + b0 + 12 + 36 * (i - 1) + (0 if final else 6)
                    for n in range(24):
                        d, rb = n // 3, n % 3
                        dve.wait_ge(S.acc_done, b + n + 1)
                        if n == 0:
                            dve.wait_ge(x_in, 16 * KT)
                        if final and n >= 1:
                            low_last(n - 1)
                        ins = dve.tensor_tensor(x[:, d, rb_cols(rb)], x[:, d, rb_cols(rb)],
                                                acc[slot("down", n)][:, 0:RBN], ALU.add)
                        ins.then_inc(S.acc_read_v, 1)
                        if n % 12 == 11:
                            if not final:
                                S.W.split_lo(dve, u0 + 8 + n // 12, 6, i - 1, b + n + 1)
                            else:
                                S.W.split_lo(dve, u0 + 4 + 6 * (N - 1) + 2 + n // 12, 2, 0, b + n + 1)
                    if final:
                        low_last(23)

                def low_last(n):
                    d, cols = n // 3, rb_cols(n % 3)
                    dve.wait_ge(hi_done, 6 * N + n + 1)
                    dve.scalar_tensor_tensor(S.R0_lo[:, d, cols], x[:, d, cols], S.vec[:, V_PLE + d:V_PLE + d + 1],
                                             S.R0_hi[:, d, cols].bitcast(F32), ALU.mult, ALU.subtract)\
                       .then_inc(xg_done, 1)

                for rb in range(NRB):
                    dve.wait_ge(sum_done, rb + 1)
                    dve.tensor_scalar(rstd[:, rb_cols(rb)], ssum[:, 0:RBN], 1.0 / D, EPS, ALU.mult, ALU.add)\
                       .then_inc(var_done, 1)
                for rb in range(NRB):
                    dve.wait_ge(root_done, rb + 1)
                    steps.i, steps.per = 0, 0
                    steps.pos = rb
                    steps.mark(dve.reciprocal(rstd[:, rb_cols(rb)], rstd[:, rb_cols(rb)]))
                dve.wait_ge(steps.sem, 3)
                steps.base = 3
                steps.body(0, F_PASS)
                gate_up(0, "up0", 0)
                lows(0, 0)
                gate_up(0, "up1", 1)
                lows(0, 1)
                steps.end(1)
                with dve.Fori(1, N) as i:
                    steps.body(i - 1, F_PASS)
                    gate_up(i, "up0", 0)
                    down(i)
                    lows(i, 0)
                    gate_up(i, "up1", 1)
                    lows(i, 1)
                    steps.end(0)
                down(N, final=True)

            @block.gpsimd
            def _(pool):
                for n in range(24):
                    d, rb = n // 3, n % 3
                    pool.wait_ge(sq_done, n + 1)
                    if d == 0:
                        pool.tensor_copy(S.ss[:, rb_cols(rb)], gs[rb][:, :]).then_inc(ss_done, 1)
                    else:
                        pool.wait_ge(ss_done, n - 2)
                        pool.tensor_tensor(S.ss[:, rb_cols(rb)], S.ss[:, rb_cols(rb)], gs[rb][:, :], ALU.add)\
                            .then_inc(ss_done, 1)


F_PASS = 12
F_FIRST = 3 + F_PASS


def ple_tile(A, d, j):
    return wsrc(A.w_ple_gate[0] if j == 0 else A.w_ple[0], d * P)


def stage_ple(nc, S, A, b0, bv0, u0):
    with ExitStack() as ctx:
        sb, bank, sem = tools(nc, S, ctx, "p")
        x = S.x_t
        rstd = sb("rstd", [P, ROWS])
        pr = sb("p_rows", [P, RT, PLE])
        p_hi, p_lo = sb("p_hi", [P, 2, ROWS], F32R), sb("p_lo", [P, 2, ROWS], F32R)
        gs = [sb(f"gs{n}", [P, RBN]) for n in range(3)]
        pe_t = [sb(f"emb{n}", [P, RBN]) for n in range(3)]
        acc = [bank(f"acc{n}") for n in range(6)]
        tp = [bank(f"tp{n}") for n in range(2)]
        p_in, sum_done, var_done, root_done = sem("p_in"), sem("sum"), sem("var"), sem("root")
        pt_done, phi_done, plo_done = sem("pt"), sem("phi"), sem("plo")
        sg_done, rec_done, mul_done = sem("sg"), sem("rec"), sem("mul")
        N = KT

        with nc.Block() as block:
            @block.sync
            def _(sp):
                sp.dma_start(pr[:, 0:PT, :], A.p_prompt[0, 0].rearrange("(r p) c -> p r c", p=P)).then_inc(p_in, 16)
                sp.dma_start(pr[:, PT, :], A.p_sample[0].rearrange("b t c -> (b t) c")).then_inc(p_in, 16)
                with sp.Fori(0, N - 2) as i:
                    for j in range(2):
                        S.W.load(sp, u0 + 4 + j, 2, i, ple_tile(A, i + 2, j))

            @block.tensor
            def _(pe):
                for rb in range(NRB):
                    if rb >= 1:
                        pe.wait_ge(var_done, rb)
                    pe.matmul(tp[0][:, 0:RBN], S.ones[:, :], S.ss[:, rb_cols(rb)], start=True, stop=True)\
                      .then_inc(sum_done, 1)
                pe.wait_ge(var_done, 3)
                pe.wait_ge(p_in, 32)
                for m in range(6):
                    if m >= 2:
                        pe.wait_ge(plo_done, m - 1)
                    for r in range(3):
                        last = pe.transpose(tp[m % 2][:, r * P:(r + 1) * P],
                                            pr[:, 3 * (m // 2) + r, (m % 2) * P:(m % 2 + 1) * P], S.ident[:, :])
                    last.then_inc(pt_done, 1)
                pe.wait_ge(plo_done, 6)
                pe.wait_ge(S.acc_read_v, HEAD + bv0)
                with pe.Fori(0, N) as i:
                    for n in range(6):
                        product_block(S, pe, None, (u0 + n // 3) % 2, acc[n],
                                      (S.R0_hi, S.R0_lo) if n < 3 else (p_hi, p_lo), n % 3,
                                      HEAD + u0 + 2 * i + n // 3 + 1, (S.acc_read_v, HEAD + bv0 + 6 * i + n - 5),
                                      kts=KT if n < 3 else 2)

            @block.scalar
            def _(act):
                for rb in range(NRB):
                    act.wait_ge(var_done, rb + 1)
                    act.activation(rstd[:, rb_cols(rb)], rstd[:, rb_cols(rb)], ACT.Sqrt).then_inc(root_done, 1)
                for m in range(6):
                    act.wait_ge(pt_done, m + 1)
                    act.activation(p_hi[:, m % 2, rb_cols(m // 2)], tp[m % 2][:, 0:RBN], ACT.Copy).then_inc(phi_done, 1)

                def body(i, last):
                    for n in range(3):
                        act.wait_ge(S.acc_read_v, HEAD + bv0 + 6 * i + n + 1)
                        act.activation(gs[n][:, :], gs[n][:, :], ACT.Sigmoid).then_inc(sg_done, 1)
                    if not last:
                        for j in range(2):
                            S.W.split_hi(act, u0 + 2 + j, 2, i, HEAD + b0 + 6 * i + 3 * j + 3)
                with act.Fori(0, N - 1) as i:
                    body(i, False)
                body(N - 1, True)

            @block.vector
            def _(dve):
                for rb in range(NRB):
                    dve.wait_ge(sum_done, rb + 1)
                    dve.tensor_scalar(rstd[:, rb_cols(rb)], tp[0][:, 0:RBN], 1.0 / D, EPS, ALU.mult, ALU.add)\
                       .then_inc(var_done, 1)
                for m in range(6):
                    dve.wait_ge(phi_done, m + 1)
                    cols = rb_cols(m // 2)
                    dve.tensor_tensor(p_lo[:, m % 2, cols], tp[m % 2][:, 0:RBN], p_hi[:, m % 2, cols].bitcast(F32),
                                      ALU.subtract).then_inc(plo_done, 1)
                for rb in range(NRB):
                    dve.wait_ge(root_done, rb + 1)
                    dve.reciprocal(rstd[:, rb_cols(rb)], rstd[:, rb_cols(rb)]).then_inc(rec_done, 1)
                dve.wait_ge(rec_done, 3)

                def body(i, last):
                    for n in range(3):
                        dve.wait_ge(S.acc_done, HEAD + b0 + 6 * i + n + 1)
                        dve.wait_ge(mul_done, 3 * i)
                        dve.tensor_tensor(gs[n][:, :], acc[n][:, 0:RBN], rstd[:, rb_cols(n)], ALU.mult)\
                           .then_inc(S.acc_read_v, 1)
                    if not last:
                        S.W.split_lo(dve, u0 + 2, 2, i, HEAD + b0 + 6 * i + 3)
                    for n in range(3):
                        dve.wait_ge(S.acc_done, HEAD + b0 + 6 * i + 3 + n + 1)
                        dve.wait_ge(sg_done, 3 * i + n + 1)
                        dve.tensor_tensor(pe_t[n][:, :], acc[3 + n][:, 0:RBN], gs[n][:, :], ALU.mult)\
                           .then_inc(S.acc_read_v, 1)
                        dve.wait_ge(S.acc_read_v, HEAD + bv0 + 6 * i + 3 + n + 1)
                        xv = x[:, ds(i, 1), rb_cols(n)].rearrange("p a n -> p (a n)")
                        dve.tensor_tensor(xv, xv, pe_t[n][:, :], ALU.add).then_inc(mul_done, 1)
                    if not last:
                        S.W.split_lo(dve, u0 + 3, 2, i, HEAD + b0 + 6 * i + 6)

                with dve.Fori(0, N - 1) as i:
                    body(i, False)
                body(N - 1, True)


def stage_final(nc, S, A):
    with ExitStack() as ctx:
        sb, bank, sem = tools(nc, S, ctx, "end")
        gain = sb("gain", [P, D])
        junk = sb("squares", [P, D])
        var, root, rstd = sb("var", [P, RT]), sb("root", [P, RT]), sb("rstd", [P, RT])
        out = [sb(f"out{n}", [P, D]) for n in range(3)]
        pt = [ctx.enter_context(nc.psum_tensor(f"y_t{n}", [P, D], F32)) for n in range(3)]
        gain_in, t_done, sq_done, var_done, root_done, rec_done, out_done = (
            sem("gain_in"), sem("t"), sem("sq"), sem("var"), sem("root"), sem("rec"), sem("out"))
        stored = [sem(f"st{n}") for n in range(3)]
        with nc.Block() as block:
            @block.sync
            def _(sp):
                sp.dma_start(gain[:, :], A.final_norm_g.unsqueeze(0).to_broadcast([P, D])).then_inc(gain_in, 16)
                for r in range(RT):
                    sp.wait_ge(out_done, r + 1)
                    dst = A.y_prompt[0, r * P:(r + 1) * P, :] if r < PT else A.y_sample.rearrange("b t d -> (b t) d")
                    sp.dma_start(dst, out[r % 3][:, :]).then_inc(stored[r % 3], 16)
                for n in range(3):
                    sp.wait_ge(stored[n], 16 * (RT // 3))

            @block.tensor
            def _(pe):
                for r in range(RT):
                    if r >= 3:
                        pe.wait_ge(out_done, r - 2)
                    for k in range(KT):
                        last = pe.transpose(pt[r % 3][:, k * P:(k + 1) * P], S.x_t[:, k, r * P:(r + 1) * P], S.ident[:, :])
                    last.then_inc(t_done, 1)

            @block.scalar
            def _(act):
                for r in range(RT):
                    act.wait_ge(t_done, r + 1)
                    if r >= 1:
                        act.wait_ge(sq_done, r)
                    act.activation(junk[:, :], pt[r % 3][:, :], ACT.Square, accum_out=var[:, r:r + 1]).then_inc(sq_done, 1)
                    act.wait_ge(var_done, r + 1)
                    act.activation(root[:, r:r + 1], rstd[:, r:r + 1], ACT.Sqrt).then_inc(root_done, 1)

            @block.vector
            def _(dve):
                dve.wait_ge(gain_in, 16)
                for r in range(RT):
                    dve.wait_ge(sq_done, r + 1)
                    dve.tensor_scalar(rstd[:, r:r + 1], var[:, r:r + 1], 1.0 / D, EPS, ALU.mult, ALU.add)\
                       .then_inc(var_done, 1)
                    dve.wait_ge(root_done, r + 1)
                    dve.reciprocal(rstd[:, r:r + 1], root[:, r:r + 1]).then_inc(rec_done, 1)
                    dve.wait_ge(rec_done, r + 1)
                    if r >= 3:
                        dve.wait_ge(stored[r % 3], 16 * (r // 3))
                    dve.scalar_tensor_tensor(out[r % 3][:, :], pt[r % 3][:, :], rstd[:, r:r + 1], gain[:, :],
                                             ALU.mult, ALU.mult).then_inc(out_done, 1)


PAIR_STEPS = 33
SSD_STEPS = 59


def hybrid_step(nc, A):
    S = Store()
    with ExitStack() as ctx:
        def sb(name, shape, dt=F32):
            return ctx.enter_context(nc.sbuf_tensor(name, shape, dt))

        def sem(name):
            return ctx.enter_context(nc.semaphore(name))

        S.sem = sem
        S.W = WeightStream(S)
        def dram(name):
            return nc.dram_tensor(name, (KT, P, ROWS), F32).ap()
        S.d_gate_a, S.d_gate_b, S.d_o, S.d_y, S.d_ta, S.d_x = [
            dram(n) for n in ("s_gate_a", "s_gate_b", "s_o", "s_y", "s_branch_a", "s_x")]
        S.acc_done, S.acc_read_a, S.acc_read_v = sem("acc_done"), sem("acc_read_a"), sem("acc_read_v")
        S.hi_done, S.lo_done, S.raw_in = sem("w_hi_done"), sem("w_lo_done"), [sem("raw_in0"), sem("raw_in1")]
        S.z_done, S.tp_done, S.av_done = sem("z_done"), sem("tp_done"), sem("av_done")
        S.kk_done, S.gg_done, S.o_read = sem("keep_done"), sem("grab_done"), sem("o_read")
        S.tp_drained, S.p_done, S.pw_done = sem("tp_drained"), sem("left_done"), sem("weights_done")
        S.dve_steps = Steps(sem("dve_steps"))

        S.raw = [sb(f"w_raw{n}", [P, D]) for n in range(2)]
        S.w_hi = [sb(f"w_hi{n}", [P, D], F32R) for n in range(2)]
        S.w_lo = [sb(f"w_lo{n}", [P, D], F32R) for n in range(2)]
        S.R0_hi, S.R0_lo = sb("operand0_hi", [P, KT, ROWS], F32R), sb("operand0_lo", [P, KT, ROWS], F32R)
        S.ident, S.ones = sb("ident", [P, P]), sb("ones", [P, P])
        S.ident_b, S.mask_p = sb("ident_bf16", [P, P], BF16), sb("mask_prompt", [P, P], BF16)
        S.mask_s = [sb(f"mask_sample{n}", [P, P], BF16) for n in range(2)]
        S.tri, S.tri_s, S.same_batch = sb("tri", [P, P]), sb("tri_sample", [P, P]), sb("same_batch", [P, P])
        S.vec = sb("vectors", [P, V_ALL])
        S.dt_bias, S.a_log, S.d_heads, S.d_chan = sb("dt_bias", [P, NH]), sb("a_log", [P, NH]), sb("d_heads", [P, NH]), sb("d_chan", [P, KT])
        S.dt, S.dta, S.dsum, S.dt_end, S.chunk_decay = [
            sb(n, [P, RT, NH]) for n in ("dt", "dt_a", "dt_a_sum", "dt_to_end", "chunk_decay")]
        S.batch_decay = sb("batch_decay", [P, KT, NB])

        w_in, w_a, w_b, w_out = A.w_in[0], A.w_a[0], A.w_b[0], A.w_out[0]

        def pair_tiles(i, j):
            return wsrc(w_in, (OFF_Q, OFF_K, OFF_V, OFF_GA)[j] + i * P)

        def ssd_tiles(i, j):
            at = (OFF_XBC + 2 * i * P, OFF_XBC + (2 * i + 1) * P, OFF_XBC + D + i * P, OFF_XBC + D + NG * NS + i * P,
                  OFF_Z + 2 * i * P, OFF_Z + (2 * i + 1) * P, OFF_GB + 2 * i * P, OFF_GB + (2 * i + 1) * P)
            return wsrc(w_in, at[j])

        def by_two(w):
            return lambda i, j: wsrc(w, (2 * i + j) * P)

        a_t, b_t, c_t = by_two(w_a), by_two(w_b), by_two(w_out)
        first = [pair_tiles(0, j) for j in range(4)]
        ssd_first = [ssd_tiles(0, j) for j in range(4)]
        up_first = [wsrc(w, f * P) for f in range(2) for w in (A.w_gate[0], A.w_up[0])]

        def four(t):
            return [t(0, 0), t(0, 1), t(1, 0), t(1, 1)]

        with ExitStack() as tmp:
            S.tmp = tmp.enter_context(nc.sbuf_tensor("mask_tmp", [P, P], F32))
            stage_prologue(nc, S, A, first)
        dt_tile = wsrc(w_in, OFF_DT)
        stage_pairs(nc, S, A, 0, 0, pair_tiles, [dt_tile] + ssd_first[0:3])
        t0 = NTP * (NH // 2)
        stage_steps(nc, S, A, 96, 32, t0, lambda sp: S.W.load(sp, 36, 2, 0, ssd_first[3]))
        stage_ssd(nc, S, A, 99, 96, 33, t0, ssd_tiles, four(a_t))
        S.ss = ctx.enter_context(nc.sbuf_tensor("sq_sums", [P, ROWS], F32))
        with ExitStack() as two:
            S.R1_hi = two.enter_context(nc.sbuf_tensor("operand1_hi", [P, KT, ROWS], F32R))
            S.R1_lo = two.enter_context(nc.sbuf_tensor("operand1_lo", [P, KT, ROWS], F32R))
            stage_branch_a(nc, S, A, 195, 0, 65, a_t, four(b_t))
            stage_branch_b(nc, S, A, 219, 24, 73, b_t, four(c_t))
            stage_out(nc, S, A, 243, 48, 81, c_t, up_first)
        with ExitStack() as late:
            S.x_t = late.enter_context(nc.sbuf_tensor("x_t", [P, KT, ROWS], F32))
            stage_ffn(nc, S, A, 267, 72, 89, [ple_tile(A, d, j) for d in range(2) for j in range(2)])
            stage_ple(nc, S, A, 663, 468, 155)
            stage_final(nc, S, A)


_INS = ["x_prompt", "x_sample", "cache_k", "cache_v", "state_conv", "state_ssm", "p_prompt", "p_sample",
        "norm_mix_g", "w_in", "conv_w", "conv_b", "dt_bias", "a_log", "d_skip", "mnorm_g", "w_a", "w_b", "w_out",
        "norm_ffn_g", "w_gate", "w_up", "w_down", "norm_ple_g", "w_ple_gate", "w_ple", "final_norm_g"]

_OUTS = [((1, SEQ, D), "y_prompt"), ((NB, TD, D), "y_sample"),
         ((1, 1, NH, SEQ, HD), "new_k_prompt"), ((1, 1, NH, SEQ, HD), "new_v_prompt"),
         ((1, 1, 3, XBC), "new_conv_prompt"), ((1, 1, NH, HD, NS), "new_ssm_prompt"),
         ((1, NB, NH, TD, HD), "new_k_sample"), ((1, NB, NH, TD, HD), "new_v_sample"),
         ((1, NB, 3, XBC), "new_conv_sample"), ((1, NB, NH, HD, NS), "new_ssm_sample")]


def kernel(**inputs):
    import numpy as _np
    import concourse.bacc as _bacc
    from concourse import mybir as _mybir
    from concourse.bass_utils import run_bass_kernel_spmd as _run

    nc = _bacc.Bacc("TRN2", target_bir_lowering=False, num_devices=1)
    arrays, A = {}, Store()
    for name in _INS:
        a = _np.ascontiguousarray(inputs[name])
        arrays[f"in_{name}"] = a
        A.__dict__[name] = nc.dram_tensor(f"in_{name}", a.shape, _mybir.dt.from_np(a.dtype), kind="ExternalInput").ap()
    for shape, name in _OUTS:
        A.__dict__[name] = nc.dram_tensor(f"out_{name}", shape, _mybir.dt.float32, kind="ExternalOutput").ap()
    hybrid_step(nc, A)
    r = _run(nc, [arrays], core_ids=[0])
    return tuple(r.results[0][f"out_{name}"] for _, name in _OUTS)
```

```python
import numpy as np
from contextlib import ExitStack

import concourse.bass as bass
from concourse import mybir
from concourse.alu_op_type import AluOpType as ALU

F32 = mybir.dt.float32
F32R = mybir.dt.float32r
BF16 = mybir.dt.bfloat16
ACT = mybir.ActivationFunctionType
ds = bass.ds

D, SEQ, NB, TD, PAST = 1024, 1024, 8, 16, 512
EPS = 1e-6
NEG = -1e30
P = 128
KT = D // P
ROWS = SEQ + NB * TD
RT = ROWS // P
RBN = 384
NRB = ROWS // RBN
PT = SEQ // P
HD, NH, NG, HPG, NS = 64, 16, 4, 4, 128
XBC = D + 2 * NG * NS
DFF = 2816
FT = DFF // P
PLE = 256
OFF_Z = 0
OFF_XBC = OFF_Z + D
OFF_DT = OFF_XBC + XBC
OFF_Q = OFF_DT + NH
OFF_K = OFF_Q + D
OFF_V = OFF_K + D
OFF_GA = OFF_V + D
OFF_GB = OFF_GA + D
SB_SCALE = HD ** -0.5
CT = XBC // P
HEAD = 4
START, DMA_HEAD = 1, 16

V_MIX, V_CW, V_CB, V_MN, V_FFN, V_PLE, V_ALL = 0, 8, 72, 88, 96, 104, 112


class Store:
    pass


class Steps:

    def __init__(self, sem):
        self.sem, self.base = sem, HEAD

    def body(self, i, per):
        self.i, self.per, self.pos = i, per, 0

    def mark(self, ins):
        ins.then_inc(self.sem, 1)
        self.pos += 1
        return self.pos

    def value(self, pos):
        return self.base + self.i * self.per + pos

    def end(self, passes):
        assert self.pos == self.per, (self.pos, self.per)
        self.base += passes * self.per


def rev(t, c0, c1):
    return t[:, c1 - 1::-1] if c0 == 0 else t[:, c1 - 1:c0 - 1:-1]


def turn_columns(u):
    kind, t, h, s0, n, first = UNITS[u][:6]
    end = SEQ
    if not first:
        end -= P if kind == "old" else (t + 1) * P - n
    return end - n, end


def wsrc(w, col, n=P):
    return w.rearrange("(k p) c -> p k c", p=P)[:, :, ds(col, n)]


class WeightStream:

    def __init__(self, S):
        self.S = S

    def load(self, sp, u0, per, i, src):
        S = self.S
        sp.wait_ge(S.lo_done, HEAD + u0 - 1 + i * per)
        dst = S.raw[u0 % 2][:, 0:src.shape[1] * src.shape[2]].rearrange("p (k c) -> p k c", k=src.shape[1])
        sp.dma_start(dst, src).then_inc(S.raw_in[u0 % 2], 16)

    def split_hi(self, act, u0, per, i, last_block):
        S = self.S
        act.wait_ge(S.raw_in[u0 % 2], (u0 // 2 + 1) * 16 + i * (per // 2 * 16))
        act.wait_ge(S.acc_done, last_block)
        act.activation(S.w_hi[u0 % 2][:, :], S.raw[u0 % 2][:, :], ACT.Copy).then_inc(S.hi_done, 1)

    def split_lo(self, dve, u0, per, i, last_block):
        S = self.S
        dve.wait_ge(S.hi_done, HEAD + u0 + 1 + i * per)
        dve.wait_ge(S.acc_done, last_block)
        dve.tensor_tensor(S.w_lo[u0 % 2][:, :], S.raw[u0 % 2][:, :], S.w_hi[u0 % 2][:, :].bitcast(F32),
                          ALU.subtract).then_inc(S.lo_done, 1)


def product_block(S, pe, slot, acc, rhs, rb, ready, free, kts=KT, more=None):
    if ready is not None:
        pe.wait_ge(S.lo_done, ready)
    pe.wait_ge(*free)
    hi = S.w_hi[slot][:, 0:kts * P].rearrange("p (k c) -> p k c", k=kts)
    lo = S.w_lo[slot][:, 0:kts * P].rearrange("p (k c) -> p k c", k=kts)
    a_hi, a_lo = rhs
    rows = slice(rb * RBN, (rb + 1) * RBN)
    n = 0
    for k in range(kts):
        for w, a in ((hi, a_hi), (hi, a_lo), (lo, a_hi)):
            last = pe.matmul(acc[:, 0:RBN], w[:, k, :], a[:, k, rows],
                             start=(n == 0), stop=(n == 3 * kts - 1 and more is None))
            n += 1
    if more is not None:
        last = more()
    last.then_inc(S.acc_done, 1)


def inverse_root(dve, var, root, t, out, sem, base):
    dve.reciprocal(out, root).then_inc(sem, 1)
    dve.wait_ge(sem, base + 1)
    dve.tensor_tensor(t, var, out, ALU.mult).then_inc(sem, 1)
    dve.wait_ge(sem, base + 2)
    dve.tensor_tensor(t, t, out, ALU.mult).then_inc(sem, 1)
    dve.wait_ge(sem, base + 3)
    dve.tensor_scalar(t, t, -0.5, 1.5, ALU.mult, ALU.add).then_inc(sem, 1)
    dve.wait_ge(sem, base + 4)
    dve.tensor_tensor(out, out, t, ALU.mult).then_inc(sem, 1)
    dve.wait_ge(sem, base + 5)


def stage_prologue(nc, S, A, first_tiles):
    with ExitStack() as ctx:
        def sb(name, shape, dt=F32):
            return ctx.enter_context(nc.sbuf_tensor(name, shape, dt))

        sem = S.sem

        x_rows = [sb(f"x_rows{n}", [P, D]) for n in range(RT)]
        x_sq = sb("x_sq", [P, D])
        gain = sb("mix_gain", [P, D])
        vec_rows = sb("vec_rows", [V_ALL, P])
        mean_sq = sb("mean_sq", [P, RT])
        var, root, newton, rstd = [sb(f"mix_{n}", [P, RT]) for n in ("var", "root", "newton", "rstd")]
        mask_f = sb("mask_f", [P, 64])
        mask_g = sb("mask_g", [P, 64])
        pt = [ctx.enter_context(nc.psum_tensor(f"x_t{n}", [P, KT, P], F32)) for n in range(3)]
        pv = ctx.enter_context(nc.psum_tensor("vec_t", [P, V_ALL], F32))
        vec_in, par_in, gain_in = sem("vec_in"), sem("par_in"), sem("gain_in")
        x_in = [sem(f"x_in{n}") for n in range(RT)]
        made, sq_done, root_done, h_done = sem("made"), sem("sq_done"), sem("root_done"), sem("h_rows_done")
        x_t, vec_t, hi_ev, lo_ev = sem("x_tdone"), sem("vec_tdone"), sem("h_hi_done"), sem("h_lo_done")
        var_done, newton_done = sem("mix_var_done"), sem("newton_done")

        groups = ((0, 2), (2, 5), (5, RT))

        with nc.Block() as block:
            @block.sync
            def _(sp):
                def rows_in(r):
                    src = A.x_prompt[0, r * P:(r + 1) * P, :] if r < PT else A.x_sample.rearrange("b t d -> (b t) d")
                    sp.dma_start(x_rows[r][:, :], src).then_inc(x_in[r], 16)

                for r in range(2):
                    rows_in(r)
                sp.dma_start(gain[:, :], A.norm_mix_g[0:1, :].to_broadcast([P, D])).then_inc(gain_in, 16)
                for r in range(2, RT):
                    rows_in(r)
                table = [(A.norm_mix_g[0], V_MIX), (A.conv_b[0], V_CB), (A.mnorm_g[0], V_MN),
                         (A.norm_ffn_g[0], V_FFN), (A.norm_ple_g[0], V_PLE)]
                for v, at in table:
                    n = v.shape[0] // P
                    sp.dma_start(vec_rows[at:at + n, :], v.rearrange("(k p) -> k p", p=P)).then_inc(vec_in, 16)
                sp.dma_start(vec_rows[V_CW:V_CB, :],
                             A.conv_w[0].rearrange("t (c p) -> (t c) p", p=P)).then_inc(vec_in, 16)
                for v, dst in ((A.dt_bias, S.dt_bias), (A.a_log, S.a_log), (A.d_skip, S.d_heads)):
                    sp.dma_start(dst[:, :], v[0:1, :].to_broadcast([P, NH])).then_inc(par_in, 16)
                S.W.load(sp, 0, 2, 0, first_tiles[0])
                S.W.load(sp, 1, 2, 0, first_tiles[1])
                S.W.load(sp, 2, 2, 0, first_tiles[2])
                S.W.load(sp, 3, 2, 0, first_tiles[3])

            @block.gpsimd
            def _(pool):
                count = [0]

                def link(ins):
                    count[0] += 1
                    ins.then_inc(made, 1)
                    pool.wait_ge(made, count[0])

                def fill(t, v):
                    link(pool.memset(t, v))

                def sel(out, in_, op, fill_, base, pattern, cm):
                    link(pool.affine_select(out=out, in_=in_, compare_op=op, fill=fill_, base=base,
                                            pattern=pattern, channel_multiplier=cm))

                fill(S.ident[:, :], 0.0)
                sel(S.ident[:, :], S.ident[:, :], ALU.not_equal, 1.0, 0, [[-1, P]], 1)
                fill(S.ones[:, :], 1.0)
                sel(S.tri[:, :], S.ones[:, :], ALU.is_ge, 0.0, 0, [[1, P]], -1)
                blocks = S.same_batch[:, :].rearrange("p (b t) -> p b t", t=TD)
                sel(blocks, S.ones[:, :].rearrange("p (b t) -> p b t", t=TD), ALU.is_ge, 0.0, 0,
                    [[-TD, NB], [0, TD]], 1)
                sel(blocks, blocks, ALU.is_ge, 0.0, TD - 1, [[TD, NB], [0, TD]], -1)
                link(pool.tensor_tensor(S.tri_s[:, :], S.tri[:, :], S.same_batch[:, :], ALU.mult))
                fill(S.tmp[:, :], 0.0)
                sel(S.tmp[:, :], S.tmp[:, :], ALU.is_gt, NEG, 0, [[-1, P]], 1)
                link(pool.tensor_copy(S.mask_p[:, :], S.tmp[:, :]))
                link(pool.tensor_copy(S.ident_b[:, :], S.ident[:, :]))
                for h, m in ((0, mask_f), (1, mask_g)):
                    v = m[:, :].rearrange("p (b s) -> p b s", s=TD)
                    fill(m[:, :], 1.0)
                    sel(v, v, ALU.is_gt, 0.0, -TD * h, [[-2 * TD, 4], [-1, TD]], 1)
                    sel(v, v, ALU.is_ge, 0.0, TD * h + TD - 1, [[2 * TD, 4], [0, TD]], -1)
                link(pool.tensor_tensor(mask_f[:, :], mask_f[:, :], mask_g[:, :], ALU.add))
                link(pool.tensor_scalar(mask_f[:, :], mask_f[:, :], 1.0, -NEG, ALU.subtract, ALU.mult))
                for j in range(2):
                    fill(S.mask_s[j][:, :], NEG)
                    link(pool.tensor_copy(S.mask_s[j][:, 64 * j:64 * j + 64], mask_f[:, :]))
                pool.nop().then_inc(S.pw_done, HEAD)

            @block.scalar
            def _(act):
                act.nop().then_inc(S.hi_done, HEAD)
                act.nop().then_inc(S.acc_read_a, HEAD)
                act.nop().then_inc(S.kk_done, HEAD)
                act.nop().then_inc(S.gg_done, HEAD)
                act.nop().then_inc(S.o_read, HEAD)
                def square(r):
                    act.wait_ge(x_in[r], 16)
                    if r >= 1:
                        act.wait_ge(sq_done, r)
                    act.activation(x_sq[:, :], x_rows[r][:, :], ACT.Square,
                                   accum_out=mean_sq[:, r:r + 1]).then_inc(sq_done, 1)

                def roots(g):
                    cols = slice(*groups[g])
                    act.wait_ge(var_done, g + 1)
                    act.activation(root[:, cols], var[:, cols], ACT.Sqrt).then_inc(root_done, 1)

                def high(r):
                    act.wait_ge(x_t, r + 1)
                    act.activation(S.R0_hi[:, :, r * P:(r + 1) * P], pt[r % 3][:, :, :], ACT.Copy).then_inc(hi_ev, 1)

                square(0)
                square(1)
                roots(0)
                for r in range(2, 5):
                    square(r)
                roots(1)
                for r, later in enumerate(((5,), (6, 7), (8,))):
                    high(r)
                    for m in later:
                        square(m)
                roots(2)
                for r in range(3, RT):
                    high(r)
                S.W.split_hi(act, 0, 2, 0, HEAD)
                S.W.split_hi(act, 1, 2, 0, HEAD)

            @block.vector
            def _(dve):
                for s in (S.lo_done, S.acc_read_v, S.tp_drained, S.p_done, S.dve_steps.sem):
                    dve.nop().then_inc(s, HEAD)
                dve.wait_ge(gain_in, 16)
                def factors(g):
                    r0, r1 = groups[g]
                    cols = slice(r0, r1)
                    dve.wait_ge(sq_done, r1)
                    dve.tensor_scalar(var[:, cols], mean_sq[:, cols], 1.0 / D, EPS,
                                      ALU.mult, ALU.add).then_inc(var_done, 1)
                    dve.wait_ge(root_done, g + 1)
                    inverse_root(dve, var[:, cols], root[:, cols], newton[:, cols], rstd[:, cols], newton_done, 5 * g)

                def low(r):
                    dve.wait_ge(hi_ev, r + 1)
                    cols = slice(r * P, (r + 1) * P)
                    dve.tensor_tensor(S.R0_lo[:, :, cols], pt[r % 3][:, :, :],
                                      S.R0_hi[:, :, cols].bitcast(F32), ALU.subtract).then_inc(lo_ev, 1)

                for g, (r0, r1) in enumerate(groups):
                    factors(g)
                    for r in range(r0, r1):
                        dve.scalar_tensor_tensor(x_rows[r][:, :], x_rows[r][:, :], rstd[:, r:r + 1],
                                                 gain[:, :], ALU.mult, ALU.mult).then_inc(h_done, 1)
                        if r >= 2:
                            low(r - 2)
                low(RT - 2)
                low(RT - 1)
                S.W.split_lo(dve, 0, 2, 0, HEAD)
                S.W.split_lo(dve, 1, 2, 0, HEAD)
                dve.wait_ge(vec_t, 1)
                dve.tensor_copy(S.vec[:, :], pv[:, :])
                dve.wait_ge(par_in, 48)
                for h in range(2):
                    dve.tensor_copy(S.d_chan[64 * h:64 * h + 64, :],
                                    S.d_heads[64 * h:64 * h + 64, :].rearrange("p (k h) -> p k h", h=2)[:, :, h])

            @block.tensor
            def _(pe):
                for s in (S.acc_done, S.z_done, S.tp_done, S.av_done):
                    pe.nop().then_inc(s, HEAD)
                pe.wait_ge(made, 2)
                for r in range(RT):
                    pe.wait_ge(h_done, r + 1)
                    if r >= 3:
                        pe.wait_ge(lo_ev, r - 2)
                    for k in range(KT):
                        last = pe.transpose(pt[r % 3][:, k, :], x_rows[r][:, k * P:(k + 1) * P], S.ident[:, :])
                    last.then_inc(x_t, 1)
                pe.wait_ge(vec_in, 6 * 16)
                pe.transpose(pv[:, :], vec_rows[:, :], S.ident[0:V_ALL, 0:V_ALL]).then_inc(vec_t, 1)


def score_units():
    rows = []
    for t in range(PT):
        for h in range(2):
            n = (t + 1) * P
            top = max(0, n - n % 512 if n % 512 else n - 512)
            row = [("p", t, h, top, n - top)]
            if top:
                row.append(("p", t, h, 0, top))
            rows.append([u + (m == 0, m == len(row) - 1) for m, u in enumerate(row)])
    sample = [[("new", j, 0, 0, P, True, False), ("old", j, 0, 0, PAST, False, True)] for j in range(2)]
    rows = rows[:10] + [sample[0]] + rows[10:] + [sample[1]]
    return [u + (n,) for n, row in enumerate(rows) for u in row]


UNITS = score_units()
NU = len(UNITS)
LAG_T, LAG_A = 3, 5
STEPS = NU + LAG_A + 1
U_OLD0 = [n for n, u in enumerate(UNITS) if u[0] == "old"]
CACHE_AT = {0: 2, 1: 4, 2: 6, 3: 8, 4: 15, 5: 17, 6: 19, 7: 21}
GATE_AT = {1: 0, 9: 1, 19: 2}
O_BANKS = [("p", t) for t in range(5)] + [("s", 0)] + [("p", t) for t in range(5, PT)] + [("s", 1)]


def o_bank(u):
    kind, n = ("p" if UNITS[u][0] == "p" else "s"), UNITS[u][1]
    return O_BANKS.index((kind, n))


def o_last(u):
    return u == max(m for m in range(NU) if o_bank(m) == o_bank(u))


def o_first(u):
    return u == min(m for m in range(NU) if o_bank(m) == o_bank(u))


def tp_events():
    ev = [("k", 0), ("k", 1), ("k", 2), ("v", 0), ("v", 1), ("v", 2)]
    for s in range(STEPS):
        ev += [("cache", b) for b in range(NB) if CACHE_AT[b] == s]
        if 0 <= s - LAG_T < NU:
            ev.append(("w", s - LAG_T))
        if 0 <= s - LAG_A - 1 < NU and UNITS[s - LAG_A - 1][0] == "old":
            ev.append(("o", UNITS[s - LAG_A - 1][1]))
    return ev


TP = tp_events()
NTP = len(TP)
NO = len(O_BANKS)


def stage_pairs(nc, S, A, b0, u0, tiles, next_tiles):
    N = NH // 2
    BPI, PER = 12, 4
    assert NTP % 2 == 0 and NO % 2 == 0 and NU % 2 == 0 and NU % 4 == 0, (NTP, NO, NU)
    with ExitStack() as ctx:
        def sb(name, shape, dt=F32):
            return ctx.enter_context(nc.sbuf_tensor(name, shape, dt))

        sem = S.sem

        q_pack = [sb(f"q_pack{h}", [P, ROWS], F32R) for h in range(2)]
        k_hi = [sb(f"k_hi{h}", [P, ROWS], F32R) for h in range(2)]
        k_lo = [sb(f"k_lo{h}", [P, ROWS], F32R) for h in range(2)]
        k_new = sb("k_new", [P, P])
        q_diag = sb("q_diag", [P, NB, 2, TD])
        stage = [sb(f"qkv_stage{n}", [P, RBN]) for n in range(2)]
        kv_out = [sb(f"kv_out{n}", [P, 3, P]) for n in range(2)]
        v_rows = sb("v_rows", [P, RT, P])
        keep = [sb(f"keep{n}", [P, 512]) for n in range(2)]
        wgt = [sb(f"wgt{n}", [P, 512]) for n in range(4)]
        left = [sb(f"left{n}", [P, SEQ + 1]) for n in range(2)]
        w_t = [sb(f"w_t{n}", [P, 4, P]) for n in range(4)]
        kc = sb("k_cache", [P, 4, 4, 2, HD])
        vc = sb("v_cache", [P, 4, 2, 4, HD])
        kc_t = sb("k_cache_t", [P, 4, PAST])
        o_t = sb("o_t", [P, ROWS])
        o_s = sb("o_sample", [P, P])
        gate = [sb(f"gate{n}", [P, RBN]) for n in range(2)]

        def bank(name):
            return ctx.enter_context(nc.psum_tensor(name, [P, 512], F32))

        acc = [bank("acc0"), bank("acc1")]
        zb = [bank("z0"), bank("z1")]
        tp = [bank("tp0"), bank("tp1")]
        ob = [bank("o0"), bank("o1")]

        kc_in, vc_in, o_stored = sem("kc_in"), sem("vc_in"), sem("o_st")
        kv_stored = [sem(f"kv_st{n}") for n in range(2)]
        gate_stored = [sem(f"gt_st{n}") for n in range(3)]
        q_diag_done, packed, zeroed = sem("q_diag_done"), sem("packed"), sem("zeroed")
        k_out = A.new_k_prompt[0, 0], A.new_k_sample[0]
        v_out = A.new_v_prompt[0, 0], A.new_v_sample[0]

        def b_end(i, n):
            return HEAD + b0 + BPI * i + n + 1

        def tpv(i, ev):
            return HEAD + NTP * i + TP.index(ev) + 1

        def uv(i, u):
            return HEAD + NU * i + u + 1

        per_m = [3, 3, 2 + NB] * 2
        KV0 = 16 * sum(per_m[m] for m in range(6) if m % 2 == 0)
        KV1 = 16 * sum(per_m[m] for m in range(6) if m % 2 == 1)

        def kv_before(i, m):
            return (KV1 if m % 2 else KV0) * i + 16 * sum(per_m[n] for n in range(m) if n % 2 == m % 2)

        with nc.Block() as block:
            @block.sync
            def _(sp):
                for s in (o_stored, *kv_stored, *gate_stored):
                    sp.nop().then_inc(s, DMA_HEAD)
                def body(i, last):
                    def weight(j):
                        src = next_tiles[j] if last else tiles(i + 1, j)
                        S.W.load(sp, u0 + PER + j, PER, i, src)


                    def cache_k(j):
                        sp.wait_ge(S.tp_done, tpv(i, ("cache", 3)) if j else HEAD + NTP * i)
                        for n in range(4):
                            for s in range(4):
                                src = A.cache_k[0, 4 * j + n, ds(2 * i, 2)].rearrange("h (p s) d -> s p h d", s=4)[s]
                                sp.dma_start(kc[:, n, s, :, :], src).then_inc(kc_in, 16)

                    def cache_v(j):
                        sp.wait_ge(S.av_done, uv(i, U_OLD0[0]) if j else HEAD + NU * i)
                        for n in range(4):
                            sp.dma_start(vc[:, n, :, :, :].rearrange("p h s d -> p h (s d)"),
                                         A.cache_v[0, 4 * j + n, ds(2 * i, 2)].rearrange("h (p s) d -> p h (s d)", s=4))\
                              .then_inc(vc_in, 16)

                    def store_rows(out, m):
                        sp.wait_ge(S.tp_drained, tpv(i, ("kv"[m // 3], m % 3)))
                        src = kv_out[m % 2]
                        prompt, sample = out
                        n = 3 if m % 3 < 2 else 2
                        for r in range(n):
                            s0 = (m % 3) * RBN + r * P
                            sp.dma_start(prompt[ds(2 * i, 2), s0:s0 + P, :].rearrange("h p d -> p h d"),
                                         src[:, r, :].rearrange("p (h d) -> p h d", h=2)).then_inc(kv_stored[m % 2], 16)
                        if n == 2:
                            for b in range(NB):
                                sp.dma_start(sample[b, ds(2 * i, 2)].rearrange("h p d -> p h d"),
                                             src[TD * b:TD * (b + 1), 2, :].rearrange("p (h d) -> p h d", h=2))\
                                  .then_inc(kv_stored[m % 2], 16)

                    cache_k(0)
                    cache_v(0)
                    weight(0)
                    for m in range(3):
                        store_rows(k_out, m)
                    weight(1)
                    for m in range(3, 6):
                        store_rows(v_out, m)
                    weight(2)

                    def store_gate(rb):
                        sp.wait_ge(S.acc_read_a, b_end(i, 9 + rb))
                        sp.dma_start(S.d_gate_a[ds(i, 1), :, rb * RBN:(rb + 1) * RBN].rearrange("a p n -> (a p) n"),
                                     gate[rb % 2][:, :]).then_inc(gate_stored[rb], 16)
                    store_gate(0)
                    cache_k(1)
                    store_gate(1)
                    cache_v(1)
                    store_gate(2)
                    weight(3)
                    sp.wait_ge(S.tp_drained, tpv(i, ("o", 1)))
                    sp.dma_start(S.d_o[ds(i, 1)].rearrange("a p n -> (a p) n"), o_t[:, :]).then_inc(o_stored, 16)

                with sp.Fori(0, N - 1) as i:
                    body(i, False)
                body(N - 1, True)
                for s, n in ((kv_stored[0], KV0), (kv_stored[1], KV1), (o_stored, 16), *((g, 16) for g in gate_stored)):
                    sp.wait_ge(s, DMA_HEAD + N * n)

            @block.tensor
            def _(pe):
                rhs = (S.R0_hi, S.R0_lo)

                def product(i, n):
                    b = b0 + n
                    product_block(S, pe, (u0 + n // 3) % 2, acc[b % 2], rhs, n % 3,
                                  HEAD + u0 + PER * i + n // 3 + 1,
                                  (S.acc_read_a, HEAD + b0 - 1 + BPI * i + n))

                def open_tp(i, ev):
                    n = TP.index(ev)
                    pe.wait_ge(S.tp_drained, HEAD + NTP * i + n - 1)
                    return tp[n % 2]

                def rows_of(i, ev):
                    kind, rb = ev
                    n = (3 if kind == "k" else 6) + rb
                    pe.wait_ge(S.acc_read_a, b_end(i, n))
                    out = open_tp(i, ev)
                    for r in range(3):
                        last = pe.transpose(out[:, r * P:(r + 1) * P], stage[n % 2][:, r * P:(r + 1) * P], S.ident[:, :])
                    last.then_inc(S.tp_done, 1)

                def cache_t(i, b):
                    pe.wait_ge(kc_in, 512 * i + 256 * (b // 4 + 1))
                    out = open_tp(i, ("cache", b))
                    for s in range(4):
                        last = pe.transpose(out[:, s * P:(s + 1) * P], kc[:, b % 4, s, :, :].rearrange("p h d -> p (h d)"), S.ident[:, :])
                    last.then_inc(S.tp_done, 1)

                def scores(i, u):
                    kind, t, h, s0, n = UNITS[u][:5]
                    z = zb[u % 2]
                    pe.wait_ge(S.gg_done, HEAD + NU * i + u - 1)
                    if u == 0:
                        pe.wait_ge(packed, 6 * i + 6)
                    if kind == "p":
                        q = q_pack[h][:, t * P:(t + 1) * P]
                        pe.matmul(z[:, 0:n], q, k_hi[h][:, s0:s0 + n], start=True, stop=False)
                        last = pe.matmul(z[:, 0:n], q, k_lo[h][:, s0:s0 + n], start=False, stop=(s0 + n <= t * P))
                        if s0 + n > t * P:
                            last = pe.matmul(z[:, n - P:n], S.ident_b[:, :], S.mask_p[:, :], start=False, stop=True)
                    elif kind == "new":
                        if t == 0:
                            pe.wait_ge(q_diag_done, 3 * i + 3)
                        q = q_diag[:, 4 * t:4 * t + 4, :, :].rearrange("p b h t -> p (b h t)")
                        pe.matmul(z[:, 0:P], q, k_new[:, :], start=True, stop=False)
                        last = pe.matmul(z[:, 0:P], S.ident_b[:, :], S.mask_s[t][:, :], start=False, stop=True)
                    else:
                        pe.wait_ge(S.tp_drained, tpv(i, ("cache", 4 * t + 3)))
                        for b in range(4):
                            last = pe.matmul(z[32 * b:32 * b + 32, :],
                                             q_diag[:, 4 * t + b, :, :].rearrange("p h t -> p (h t)"),
                                             kc_t[:, b, :], start=True, stop=True)
                    last.then_inc(S.z_done, 1)

                def transposes(i, u):
                    kind, t, h, s0, n = UNITS[u][:5]
                    pe.wait_ge(S.pw_done, uv(i, u))
                    out = open_tp(i, ("w", u))
                    w = wgt[u % 4]
                    for c in range(n // P):
                        src = w[:, c:PAST:4] if kind == "old" else w[:, c * P:(c + 1) * P]
                        last = pe.transpose(out[:, c * P:(c + 1) * P], src, S.ident[:, :])
                    last.then_inc(S.tp_done, 1)

                def values(i, u):
                    kind, t, h, s0, n, first, final = UNITS[u][:7]
                    pe.wait_ge(S.tp_drained, tpv(i, ("w", u)))
                    o = ob[o_bank(u) % 2]
                    if o_first(u):
                        pe.wait_ge(S.o_read, HEAD + NO * i + o_bank(u) - 1)
                    wt = w_t[u % 4]
                    if kind == "p":
                        for c in range(n // P):
                            last = pe.matmul(o[64 * h:64 * h + 64, 0:P], v_rows[:, s0 // P + c, 64 * h:64 * h + 64],
                                             wt[:, c, :], start=(first and c == 0), stop=(final and c == n // P - 1))
                    elif kind == "new":
                        last = pe.matmul(o[:, 0:P], wt[:, 0, :], v_rows[:, PT, :], start=True, stop=False)
                    else:
                        pe.wait_ge(vc_in, 128 * i + 64 * (t + 1))
                        for c in range(4):
                            for b in range(4):
                                last = pe.matmul(o[32 * b:32 * b + 32, 0:P], wt[:, c, 32 * b:32 * b + 32],
                                                 vc[:, b, :, c, :], start=False, stop=(c == 3))
                    last.then_inc(S.av_done, 1)

                def turn_o(i, j):
                    pe.wait_ge(S.o_read, HEAD + NO * i + O_BANKS.index(("s", j)) + 1)
                    out = open_tp(i, ("o", j))
                    pe.transpose(out[:, 0:P], o_s[:, :], S.ident[:, :]).then_inc(S.tp_done, 1)

                with pe.Fori(0, N) as i:
                    for n in range(9):
                        product(i, n)
                        if n >= 4:
                            rows_of(i, TP[n - 4])
                    rows_of(i, ("v", 2))
                    for s in range(STEPS):
                        if s in GATE_AT:
                            product(i, 9 + GATE_AT[s])
                        for b in range(NB):
                            if CACHE_AT[b] == s:
                                cache_t(i, b)
                        if s < NU:
                            scores(i, s)
                        if 0 <= s - LAG_T < NU:
                            transposes(i, s - LAG_T)
                        if 0 <= s - LAG_A < NU:
                            values(i, s - LAG_A)
                        if 0 <= s - LAG_A - 1 < NU and UNITS[s - LAG_A - 1][0] == "old":
                            turn_o(i, UNITS[s - LAG_A - 1][1])

            @block.scalar
            def _(act):
                def copy_block(i, n):
                    act.wait_ge(S.acc_done, b_end(i, n))
                    if n < 2:
                        act.wait_ge(S.tp_done, HEAD + NTP * i)
                    elif n < 8:
                        m = n - 2
                        act.wait_ge(packed, 6 * i + min(m, 5) + 1)
                        if n == 4 or n == 7:
                            act.wait_ge(q_diag_done, 3 * i + (2 if n == 4 else 3))
                        if m >= 3:
                            act.wait_ge(S.tp_done, tpv(i, ("k", m - 3)))
                    else:
                        act.wait_ge(S.tp_done, tpv(i, ("v", 0)))
                    act.activation(stage[n % 2][:, :], acc[(b0 + n) % 2][:, 0:RBN], ACT.Copy)\
                       .then_inc(S.acc_read_a, 1)

                def diag(i, h):
                    act.wait_ge(S.acc_read_a, b_end(i, 2))
                    act.wait_ge(zeroed, 1)
                    act.activation(q_diag[64 * h:64 * h + 64, :, h, :],
                                   stage[0][64 * h:64 * h + 64, 2 * P:3 * P].rearrange("p (b t) -> p b t", t=TD),
                                   ACT.Copy).then_inc(q_diag_done, 1)

                def split(i, j):
                    S.W.split_hi(act, u0 + j + 2, PER, i, b_end(i, 3 * j + 2))

                with act.Fori(0, N) as i:
                    for n in range(9):
                        copy_block(i, n)
                        if n == 2:
                            diag(i, 0)
                            diag(i, 1)
                        if n == 5:
                            act.wait_ge(S.acc_read_a, b_end(i, 5))
                            act.activation(k_new[:, :], stage[1][:, 2 * P:3 * P], ACT.Copy).then_inc(q_diag_done, 1)
                        if n % 3 == 2:
                            split(i, n // 3)
                    for s in range(STEPS):
                        if s in GATE_AT:
                            rb = GATE_AT[s]
                            act.wait_ge(S.acc_done, b_end(i, 9 + rb))
                            if rb == 2:
                                act.wait_ge(gate_stored[0], DMA_HEAD + 16 * i + 16)
                            else:
                                act.wait_ge(gate_stored[rb], DMA_HEAD + 16 * i)
                                if rb == 0:
                                    act.wait_ge(gate_stored[2], DMA_HEAD + 16 * i)
                            act.activation(gate[rb % 2][:, :], acc[(b0 + 9 + rb) % 2][:, 0:RBN], ACT.Sigmoid)\
                               .then_inc(S.acc_read_a, 1)
                            if rb == 2:
                                split(i, 3)
                        if s < NU:
                            n = UNITS[s][4]
                            act.wait_ge(S.z_done, uv(i, s))
                            act.wait_ge(S.p_done, HEAD + NU * i + s - 1)
                            act.activation(keep[s % 2][:, 0:n], zb[s % 2][:, 0:n], ACT.Sigmoid, scale=-SB_SCALE)\
                               .then_inc(S.kk_done, 1)
                            if s >= 4:
                                act.wait_ge(S.tp_done, tpv(i, ("w", s - 4)))
                            act.activation(wgt[s % 4][:, 0:n], zb[s % 2][:, 0:n], ACT.Sigmoid, scale=SB_SCALE)\
                               .then_inc(S.gg_done, 1)
                        u = s - LAG_A
                        if 0 <= u < NU and o_last(u):
                            act.wait_ge(S.av_done, uv(i, u))
                            if u == min(m for m in range(NU) if o_last(m)):
                                act.wait_ge(o_stored, DMA_HEAD + 16 * i)
                            kind, t = O_BANKS[o_bank(u)]
                            src = ob[o_bank(u) % 2]
                            if kind == "p":
                                act.activation(o_t[:, t * P:(t + 1) * P], src[:, 0:P], ACT.Copy).then_inc(S.o_read, 1)
                            else:
                                if t == 1:
                                    act.wait_ge(S.tp_done, tpv(i, ("o", 0)))
                                act.activation(o_s[:, :], src[:, 0:P], ACT.Copy).then_inc(S.o_read, 1)

            @block.vector
            def _(dve):
                steps = S.dve_steps

                def pack(i, n):
                    src = stage[n % 2]
                    cols = slice((n % 3) * RBN, (n % 3 + 1) * RBN)
                    dve.wait_ge(S.acc_read_a, b_end(i, n))
                    half = (slice(0, 64), slice(64, P))
                    if n < 3:
                        for h in range(2):
                            m = steps.mark(dve.tensor_copy(q_pack[h][half[h], cols], src[half[h], :]))
                        for h in range(2):
                            dve.wait_ge(steps.sem, steps.value(m - 1 + h))
                            ins = dve.tensor_tensor(q_pack[h][half[1 - h], cols], src[half[h], :],
                                                    q_pack[h][half[h], cols].bitcast(F32), ALU.subtract)
                            if h == 0:
                                steps.mark(ins)
                    else:
                        for h in range(2):
                            m = steps.mark(dve.tensor_copy(k_hi[h][half[h], cols], src[half[h], :]))
                            steps.mark(dve.tensor_copy(k_hi[h][half[1 - h], cols], src[half[h], :]))
                        m = steps.pos - 3
                        for h in range(2):
                            dve.wait_ge(steps.sem, steps.value(m + 2 * h))
                            steps.mark(dve.tensor_tensor(k_lo[h][half[h], cols], src[half[h], :],
                                                         k_hi[h][half[h], cols].bitcast(F32), ALU.subtract))
                            ins = dve.tensor_tensor(k_lo[h][half[1 - h], cols], src[half[h], :],
                                                    k_hi[h][half[h], cols].bitcast(F32), ALU.subtract)
                            if h == 0:
                                steps.mark(ins)
                    ins.then_inc(packed, 1)

                def drain(i, ev):
                    n = TP.index(ev)
                    src = tp[n % 2]
                    dve.wait_ge(S.tp_done, HEAD + NTP * i + n + 1)
                    kind, x = ev
                    if kind in "kv":
                        m = x + (3 if kind == "v" else 0)
                        dve.wait_ge(kv_stored[m % 2], DMA_HEAD + kv_before(i, m))
                        if kind == "v":
                            steps.mark(dve.tensor_copy(v_rows[:, 3 * x:3 * x + 3, :],
                                                       src[:, 0:RBN].rearrange("p (r c) -> p r c", c=P)))
                            dve.wait_ge(steps.sem, steps.value(steps.pos))
                            dve.tensor_copy(kv_out[m % 2][:, :, :], v_rows[:, 3 * x:3 * x + 3, :])\
                               .then_inc(S.tp_drained, 1)
                        else:
                            dve.tensor_copy(kv_out[m % 2][:, :, :], src[:, 0:RBN].rearrange("p (r c) -> p r c", c=P))\
                               .then_inc(S.tp_drained, 1)
                    elif kind == "cache":
                        dve.wait_ge(S.z_done, uv(i, U_OLD0[0]) if x >= 4 else HEAD + NU * i)
                        dve.tensor_copy(kc_t[:, x % 4, :].rearrange("p (m s) -> p s m", s=4),
                                        src[:, :].rearrange("p (s m) -> p s m", s=4)).then_inc(S.tp_drained, 1)
                    elif kind == "w":
                        dve.wait_ge(S.av_done, HEAD + NU * i + x - 3)
                        c = UNITS[x][4] // P
                        dve.tensor_copy(w_t[x % 4][:, 0:c, :], src[:, 0:c * P].rearrange("p (c m) -> p c m", c=c))\
                           .then_inc(S.tp_drained, 1)
                    else:
                        for h in range(2):
                            cols = slice(SEQ + 64 * x, SEQ + 64 * x + 64)
                            ins = dve.tensor_copy(
                                o_t[64 * h:64 * h + 64, cols].rearrange("p (b t) -> p b t", t=TD),
                                src[64 * h:64 * h + 64, 0:P].rearrange("p (b h t) -> p b h t", h=2, t=TD)[:, :, h, :])
                            if h == 1:
                                ins.then_inc(S.tp_drained, 1)

                def split(i, j):
                    S.W.split_lo(dve, u0 + j + 2, PER, i, b_end(i, 3 * j + 2))

                dve.memset(q_diag[:, :, :, :], 0.0).then_inc(zeroed, 1)
                for n in range(2):
                    dve.memset(left[n][:, SEQ:SEQ + 1], 1.0)
                with dve.Fori(0, N) as i:
                    steps.body(i, PAIR_STEPS)
                    for n in range(6):
                        pack(i, n)
                        if n % 3 == 2:
                            split(i, n // 3)
                        if n >= 4:
                            drain(i, TP[n - 4])
                    drain(i, TP[2])
                    drain(i, TP[3])
                    drain(i, TP[4])
                    split(i, 2)
                    drain(i, TP[5])
                    for s in range(STEPS):
                        for b in range(NB):
                            if CACHE_AT[b] == s:
                                drain(i, ("cache", b))
                        if 1 <= s <= NU:
                            u = s - 1
                            kind, t, h, s0, n, first, final, row = UNITS[u]
                            c0, c1 = turn_columns(u)
                            dve.wait_ge(S.kk_done, uv(i, u))
                            if first:
                                prev = [m for m in range(NU) if UNITS[m][7] == row - 2]
                                dve.wait_ge(S.pw_done, uv(i, prev[-1]) if prev else HEAD + NU * i)
                            else:
                                dve.wait_ge(S.p_done, uv(i, u - 1))
                            lf = left[row % 2]
                            k = keep[u % 2]
                            dve.tensor_tensor_scan(rev(lf, c0, c1), rev(k, 0, n), rev(k, 0, n),
                                                   lf[:, c1:c1 + 1], ALU.mult, ALU.bypass).then_inc(S.p_done, 1)
                        if 0 <= s - LAG_T < NU:
                            drain(i, ("w", s - LAG_T))
                        if 0 <= s - LAG_A - 1 < NU and UNITS[s - LAG_A - 1][0] == "old":
                            if UNITS[s - LAG_A - 1][1] == 0:
                                dve.wait_ge(o_stored, DMA_HEAD + 16 * i)
                            drain(i, ("o", UNITS[s - LAG_A - 1][1]))
                        if s in GATE_AT and GATE_AT[s] == 2:
                            split(i, 3)
                    steps.end(0)
                steps.base += N * PAIR_STEPS

            @block.gpsimd
            def _(pool):
                with pool.Fori(0, N) as i:
                    for u in range(NU):
                        n, row = UNITS[u][4], UNITS[u][-1]
                        c0, c1 = turn_columns(u)
                        pool.wait_ge(S.gg_done, uv(i, u))
                        pool.wait_ge(S.p_done, uv(i, u))
                        w = wgt[u % 4]
                        pool.tensor_tensor(w[:, 0:n], w[:, 0:n], left[row % 2][:, c0 + 1:c1 + 1], ALU.mult)\
                            .then_inc(S.pw_done, 1)


def stage_steps(nc, S, A, b0, u0, t0, next_load):
    with ExitStack() as ctx:
        def sb(name, shape, dt=F32):
            return ctx.enter_context(nc.sbuf_tensor(name, shape, dt))

        def bank(name):
            return ctx.enter_context(nc.psum_tensor(name, [P, 512], F32))

        sem = S.sem

        dt_t = sb("dt_t", [P, ROWS])
        raw = sb("dt_raw", [P, RT, NH])
        mag = sb("dt_mag", [P, RT, NH])
        rate = sb("rate", [P, NH])
        acc = [bank("dacc0"), bank("dacc1")]
        tb, sums, ends, batch = bank("dt_rows"), bank("sums"), bank("ends"), bank("batch_ends")
        act_s, dve_s, pe_s = sem("dt_act"), sem("dt_dve"), sem("dt_pe")

        def over_tiles(v):
            return v.unsqueeze(1).to_broadcast([P, RT, NH])

        with nc.Block() as block:
            @block.sync
            def _(sp):
                next_load(sp)

            @block.tensor
            def _(pe):
                for rb in range(NRB):
                    product_block(S, pe, u0 % 2, acc[rb % 2], (S.R0_hi, S.R0_lo), rb, HEAD + u0 + 1,
                                  (act_s, rb - 1) if rb >= 1 else (S.acc_done, HEAD + b0))
                pe.wait_ge(act_s, NRB)
                for r in range(RT):
                    last = pe.transpose(tb[:, 32 * r:32 * r + 32], dt_t[0:32, r * P:(r + 1) * P], S.ident[0:32, 0:32])
                last.then_inc(pe_s, 1)
                pe.wait_ge(dve_s, 5)
                n = PT * NH
                flat = S.dta[:, :, :].rearrange("p r h -> p (r h)")
                for out, m, m_s in ((sums, S.tri, S.tri_s), (ends, S.ones, S.same_batch)):
                    pe.matmul(out[:, 0:n], m[:, :], flat[:, 0:n], start=True, stop=True)
                    pe.matmul(out[:, n:n + NH], m_s[:, :], flat[:, n:n + NH], start=True, stop=True)
                for k in range(KT):
                    last = pe.matmul(batch[:, NB * k:NB * k + NB],
                                     dt_t[:, k * P:(k + 1) * P],
                                     S.same_batch[:, 0:P:TD], start=True, stop=True)
                last.then_inc(pe_s, 1)

            @block.scalar
            def _(act):
                for rb in range(NRB):
                    act.wait_ge(S.acc_done, HEAD + b0 + rb + 1)
                    act.activation(dt_t[:, rb * RBN:(rb + 1) * RBN], acc[rb % 2][:, 0:RBN], ACT.Copy).then_inc(act_s, 1)
                S.W.split_hi(act, u0 + 2, 2, 0, HEAD + b0 + NRB)
                act.activation(rate[:, :], S.a_log[:, :], ACT.Exp).then_inc(act_s, 1)
                act.wait_ge(dve_s, 2)
                act.activation(mag[:, :, :], mag[:, :, :], ACT.Exp, scale=-1.0).then_inc(act_s, 1)
                act.wait_ge(act_s, NRB + 2)
                act.activation(mag[:, :, :], mag[:, :, :], ACT.Ln, bias=1.0).then_inc(act_s, 1)
                act.wait_ge(pe_s, 2)
                act.activation(S.chunk_decay[:, :, :].rearrange("p r h -> p (r h)"), ends[:, 0:RT * NH], ACT.Exp)\
                   .then_inc(act_s, 1)
                act.activation(S.batch_decay[:, :, :].rearrange("p k b -> p (k b)"), batch[:, 0:KT * NB], ACT.Exp)\
                   .then_inc(act_s, 1)
                act.wait_ge(dve_s, 7)
                act.activation(S.dt_end[:, :, :], S.dt_end[:, :, :], ACT.Exp).then_inc(act_s, 1)

            @block.vector
            def _(dve):
                S.W.split_lo(dve, u0 + 2, 2, 0, HEAD + b0 + NRB)
                dve.wait_ge(pe_s, 1)
                dve.tensor_tensor(raw[:, :, :], tb[:, 0:32 * RT].rearrange("p (r c) -> p r c", c=32)[:, :, 0:NH],
                                  over_tiles(S.dt_bias[:, :]), ALU.add).then_inc(dve_s, 1)
                dve.wait_ge(dve_s, 1)
                dve.scalar_tensor_tensor(mag[:, :, :], raw[:, :, :], -1.0, raw[:, :, :], ALU.mult, ALU.max)\
                   .then_inc(dve_s, 1)
                dve.wait_ge(act_s, NRB + 3)
                dve.scalar_tensor_tensor(S.dt[:, :, :], raw[:, :, :], 0.0, mag[:, :, :], ALU.max, ALU.add)\
                   .then_inc(dve_s, 1)
                dve.wait_ge(dve_s, 3)
                dve.scalar_tensor_tensor(S.dta[:, :, :], S.dt[:, :, :], -1.0, over_tiles(rate[:, :]),
                                         ALU.mult, ALU.mult).then_inc(dve_s, 1)
                dve.wait_ge(dve_s, 4)
                dve.tensor_copy(dt_t[:, 0:D].rearrange("p (h d) -> p h d", h=NH),
                                S.dta[:, PT, :].unsqueeze(2).to_broadcast([P, NH, HD])).then_inc(dve_s, 1)
                dve.wait_ge(pe_s, 2)
                dve.tensor_copy(S.dsum[:, :, :].rearrange("p r h -> p (r h)"), sums[:, 0:RT * NH]).then_inc(dve_s, 1)
                dve.wait_ge(dve_s, 6)
                dve.wait_ge(act_s, NRB + 4)
                dve.tensor_tensor(S.dt_end[:, :, :].rearrange("p r h -> p (r h)"), ends[:, 0:RT * NH],
                                  S.dsum[:, :, :].rearrange("p r h -> p (r h)"), ALU.subtract).then_inc(dve_s, 1)
                dve.wait_ge(act_s, NRB + 6)
                dve.tensor_tensor(S.dt_end[:, :, :], S.dt_end[:, :, :], S.dt[:, :, :], ALU.mult).then_inc(dve_s, 1)


SSD_TP = ["hist", "tail", ("rows", 0)]
for _c in range(PT):
    SSD_TP += [("rows", _c + 1), ("h0", _c)]
SSD_TP.append("state")
SSD_ORDER = (2, 3, 0, 1)
SILU_AT = (6, 8, 10, 12)
NTP2 = len(SSD_TP)
PAD = 3
XW = PAD + SEQ
XP_COLS = XW + NB * (PAD + TD)


def stage_ssd(nc, S, A, b0, ba0, u0, t0, tiles, next_tiles):
    BPI, PER = 24, 8
    HC = HPG * HD
    with ExitStack() as ctx:
        def sb(name, shape, dt=F32):
            return ctx.enter_context(nc.sbuf_tensor(name, shape, dt))

        def bank(name):
            return ctx.enter_context(nc.psum_tensor(name, [P, 512], F32))

        sem = S.sem

        xp = S.stream
        sg = sb("sig", [P, ROWS])
        zt = sb("z_t", [P, 2, ROWS])
        gb = sb("gb_t", [P, 2, ROWS])
        var, root, newton, rs = [sb(f"y_{n}", [P, RT]) for n in ("var", "root", "newton", "rstd")]
        seg = [sb(f"seg{n}", [P, HPG, P]) for n in range(2)]
        grow = [sb(f"grow{n}", [P, 2, P]) for n in range(2)]
        dx = [sb(f"dx{n}", [P, HPG, HD]) for n in range(2)]
        dxe = [sb(f"dxe{n}", [P, HPG, HD]) for n in range(2)]
        b_rows = [sb(f"b_rows{n}", [P, NS]) for n in range(2)]
        cbm = sb("cb_masked", [P, P])
        off = sb("y_off", [P, 2, P])
        state = sb("state", [P, HPG, HD])
        state_out = sb("state_out", [P, 2, NS])
        h0 = sb("h0", [P, 2, NB, NS])
        h0_t = [sb(f"h0_t{n}", [P, 2 * P]) for n in range(NB)]
        b_blk = sb("b_blocks", [P, NB, NS])
        hist = sb("hist", [P, 4, P])
        tail = sb("tail", [P, 4, PAD * (NB + 1)])
        tail_t = sb("tail_t", [PAD * (NB + 1), 4, P])
        cw = sb("taps_and_bias", [P, 5, 4])
        heads = sb("group_head_values", [P, 5, RT, HPG])
        dtg, dtag, dsg, deg, cdg = [heads[:, n, :, :] for n in range(5)]
        bdg, dg, mn = sb("g_bdecay", [P, 2, NB]), sb("g_d", [P, 2]), sb("g_mn", [P, 2])

        y = sb("conv_out", [P, 4, ROWS])

        acc = [bank("sacc0"), bank("sacc1")]
        tp = [bank("stp0"), bank("stp1")]
        al, cbb, stb, yy = bank("decay_rows"), bank("cb"), bank("states"), bank("ys")

        hist_clear, hist_in, h0_in = sem("hist_clear"), sem("hist_in"), sem("h0_in")
        tail_st, state_st, h0_st, gb_st, y_st = sem("tail_st"), sem("state_st"), sem("h0_st"), sem("gb_st"), sem("y_st")
        front, yy_done, st_done, norm_done = sem("front_done"), sem("yy_done"), sem("st_done"), sem("norm_sum")
        e_done, sg_done, gb_done, sq_done, rt_done = sem("e_done"), sem("sg_done"), sem("gb_done"), sem("ysq_done"), sem("rt_done")
        seg_done, m_done, y_read, h_done, conv_done, silu_done = (
            sem("seg_done"), sem("m_done"), sem("y_read"), sem("h_done"), sem("conv_done"), sem("silu_done"))
        gate_mul, var_done, y_done, loaded, xl_done, st_read = (
            sem("gate_mul"), sem("var_done"), sem("y_done"), sem("g_loaded"), sem("xl_done"), sem("st_read"))
        silu_z, rec_done, spread_done = sem("silu_z"), sem("yrec_done"), sem("spread_done")
        sq_added = sem("ysq_added")
        S.y_stored = y_st

        def b_end(i, n):
            return HEAD + b0 + BPI * i + n + 1

        def a_end(i, n):
            return HEAD + ba0 + BPI * i + n + 1

        def tpv(i, ev):
            return HEAD + t0 + NTP2 * i + SSD_TP.index(ev) + 1

        def channels(i):
            return ((0, 2, i * HC), (2, 1, D + i * NS), (3, 1, D + NG * NS + i * NS))

        with nc.Block() as block:
            @block.sync
            def _(sp):
                for s in (gb_st, state_st, tail_st, y_st, h0_st):
                    sp.nop().then_inc(s, DMA_HEAD)
                def load_hist(i):
                    for t, n, c in channels(i):
                        sp.dma_start(hist[0:NB * PAD, t:t + n, :].rearrange("r t c -> r (t c)"),
                                     A.state_conv[0].rearrange("b s c -> (b s) c")[:, ds(c, n * P)]).then_inc(hist_in, 16)

                def load_h0(i):
                    sp.wait_ge(h0_st, DMA_HEAD + 32 * i)
                    for q in range(2):
                        sp.dma_start(h0[:, q, :, :], A.state_ssm[0, :, ds(4 * i + 2 * q, 2)]
                                     .rearrange("b h p n -> (h p) b n")).then_inc(h0_in, 16)

                def store_y(i):
                    sp.wait_ge(y_done, START + 2 * i + 2)
                    sp.dma_start(S.d_y[ds(2 * i, 2)].rearrange("k p n -> p k n"), y[:, 0:2, :]).then_inc(y_st, 16)

                def body(i, first, last):
                    def weight(j):
                        if j < 4:
                            src = tiles(i, j + 4)
                        else:
                            src = next_tiles[j - 4] if last else tiles(i + 1, j - 4)
                        S.W.load(sp, u0 + 4 + j, PER, i, src)

                    for j in range(2):
                        weight(j)
                    if not first:
                        store_y(i - 1)
                    for j in range(2, 4):
                        weight(j)
                    if not last:
                        sp.wait_ge(S.tp_done, tpv(i, "hist"))
                        load_hist(i + 1)
                    sp.wait_ge(S.tp_drained, tpv(i, "tail"))
                    for t, n, c in channels(i):
                        src = tail_t[:, t:t + n, :].rearrange("r t c -> r (t c)")
                        sp.dma_start(A.new_conv_prompt[0, 0, :, ds(c, n * P)], src[0:PAD, :]).then_inc(tail_st, 16)
                        sp.dma_start(A.new_conv_sample[0].rearrange("b s c -> (b s) c")[:, ds(c, n * P)],
                                     src[PAD:, :]).then_inc(tail_st, 16)
                    for j in range(4, 8):
                        weight(j)
                    sp.wait_ge(S.tp_drained, tpv(i, "state"))
                    for q in range(2):
                        sp.dma_start(A.new_ssm_prompt[0, 0, ds(4 * i + 2 * q, 2)].rearrange("h p n -> (h p) n"),
                                     state_out[:, q, :]).then_inc(state_st, 16)
                    sp.wait_ge(st_read, START + 4 * i + 4)
                    for q in range(2):
                        sp.dma_start(A.new_ssm_sample[0, :, ds(4 * i + 2 * q, 2)].rearrange("b h p n -> (h p) b n"),
                                     h0[:, q, :, :]).then_inc(h0_st, 16)
                    sp.wait_ge(gb_done, 2 * i + 2)
                    sp.dma_start(S.d_gate_b[ds(2 * i, 2)].rearrange("k p n -> p k n"), gb[:, :, :]).then_inc(gb_st, 16)
                    if not last:
                        load_h0(i + 1)

                sp.wait_ge(hist_clear, 1)
                load_hist(0)
                load_h0(0)
                body(0, True, False)
                with sp.Fori(1, NG - 1) as i:
                    body(i, False, False)
                body(NG - 1, False, True)
                sp.wait_ge(S.tp_drained, tpv(NG - 1, "tail"))
                for m in range(4):
                    sp.dma_start(xp[:, m, 0:ROWS], S.d_o[m]).then_inc(S.o_in[m], 16)
                store_y(NG - 1)
                for s, n in ((tail_st, 96), (state_st, 32), (h0_st, 32), (gb_st, 16)):
                    sp.wait_ge(s, DMA_HEAD + NG * n)

            @block.tensor
            def _(pe):
                for s in (norm_done, st_done):
                    pe.nop().then_inc(s, START)
                rhs = (S.R0_hi, S.R0_lo)

                def product(i, n):
                    product_block(S, pe, (u0 + n // 3) % 2, acc[n % 2], rhs, n % 3,
                                  HEAD + u0 + PER * i + n // 3 + 1,
                                  (S.acc_read_a, HEAD + ba0 + BPI * i + n - 1))

                def open_tp(i, ev):
                    n = SSD_TP.index(ev)
                    pe.wait_ge(S.tp_drained, HEAD + t0 + NTP2 * i + n - 1)
                    return tp[n % 2]

                def begin_front(i, c):
                    rows = slice(c * P, (c + 1) * P)
                    out = open_tp(i, ("rows", c))
                    if c == 0:
                        pe.wait_ge(silu_done, START + 4 * i + 4)
                        pe.wait_ge(loaded, i + 1)
                    for q in range(3):
                        last = pe.transpose(out[:, q * P:(q + 1) * P], y[:, q, rows], S.ident[:, :])
                    last.then_inc(S.tp_done, 1)
                    if c == 0:
                        pe.wait_ge(y_done, START + 2 * i)
                    pe.wait_ge(seg_done, START + RT * i + c)
                    pe.wait_ge(e_done, START + RT * i + c)
                    tri = S.tri if c < PT else S.tri_s
                    for h in range(HPG):
                        pe.matmul(al[:, h * P:(h + 1) * P], dtag[:, c, h:h + 1].to_broadcast([P, P]), tri[:, :],
                                  start=True, stop=True)
                    pe.matmul(cbb[:, 0:P], y[:, 2, rows], y[:, 3, rows], start=True, stop=True).then_inc(front, 1)

                def back(i, c):
                    rows = slice(c * P, (c + 1) * P)
                    pe.wait_ge(m_done, RT * i + c + 1)
                    pe.wait_ge(y_read, START + RT * i + c)
                    for h in range(HPG):
                        half = slice(64 * (h % 2), 64 * (h % 2) + 64)
                        pe.matmul(yy[half, (h // 2) * P:(h // 2 + 1) * P], dx[c % 2][:, h, :], seg[c % 2][:, h, :],
                                  start=True, stop=True)
                    if c < PT:
                        pe.wait_ge(h_done, PT * i + i + c + 1)
                        for q in range(2):
                            last = pe.matmul(yy[:, (2 + q) * P:(3 + q) * P],
                                             state[:, 2 * q:2 * q + 2, :].rearrange("p h d -> p (h d)"),
                                             y[:, 3, rows], start=True, stop=True)
                        last.then_inc(yy_done, 1)
                        pe.matmul(stb[:, 0:HC], b_rows[c % 2][:, :],
                                  dxe[c % 2][:, :, :].rearrange("p h d -> p (h d)"),
                                  start=True, stop=True).then_inc(st_done, 1)
                        return
                    pe.wait_ge(S.tp_drained, tpv(i, ("h0", NB - 1)))
                    for b in range(NB):
                        for q in range(2):
                            last = pe.matmul(yy[:, (2 + q) * P + TD * b:(2 + q) * P + TD * (b + 1)],
                                             h0_t[b][:, q * P:(q + 1) * P],
                                             y[:, 3, SEQ + TD * b:SEQ + TD * (b + 1)], start=True, stop=True)
                    last.then_inc(yy_done, 1)
                    pe.wait_ge(h_done, PT * i + i + PT + 1)
                    out = open_tp(i, "state")
                    for q in range(2):
                        last = pe.transpose(out[:, q * P:(q + 1) * P],
                                            state[:, 2 * q:2 * q + 2, :].rearrange("p h d -> p (h d)"), S.ident[:, :])
                    last.then_inc(S.tp_done, 1)
                    for n in range(4):
                        if n == 3:
                            pe.wait_ge(y_read, START + RT * i + RT)
                        pe.matmul((stb, cbb, al, yy)[n][:, :],
                                  dxe[c % 2][:, 2 * (n // 2):2 * (n // 2) + 2, :].rearrange("p h d -> p (h d)"),
                                  b_blk[:, 4 * (n % 2):4 * (n % 2) + 4, :].rearrange("p b n -> p (b n)"),
                                  start=True, stop=True).then_inc(st_done, 1)

                def turn_h0(i, b):
                    if b == 0:
                        pe.wait_ge(h0_in, 32 * i + 32)
                    out = open_tp(i, ("h0", b))
                    for q in range(2):
                        last = pe.transpose(out[:, q * P:(q + 1) * P], h0[:, q, b, :], S.ident[:, :])
                    last.then_inc(S.tp_done, 1)

                def norm_sums(i):
                    pe.wait_ge(sq_added, i + 1)
                    pe.wait_ge(st_read, START + 4 * i + 4)
                    for r in range(RT):
                        last = pe.matmul(yy[:, r:r + 1], zt[:, 0, r * P:(r + 1) * P], S.ones[:, 0:1],
                                         start=True, stop=True)
                    last.then_inc(norm_done, 1)

                def spread(i):
                    pe.wait_ge(rec_done, 5 * i + 5)
                    for r in range(RT):
                        last = pe.matmul((al, cbb, stb)[r // 3][:, (r % 3) * P:(r % 3 + 1) * P],
                                         rs[:, r:r + 1].to_broadcast([P, P]), S.ident[:, :], start=True, stop=True)
                    last.then_inc(spread_done, 1)

                def body(i, first):
                    out = open_tp(i, "hist")
                    pe.wait_ge(hist_in, 48 * i + 48)
                    for q in range(4):
                        last = pe.transpose(out[:, q * P:(q + 1) * P], hist[:, q, :], S.ident[:, :])
                    last.then_inc(S.tp_done, 1)
                    for n in range(15):
                        product(i, n)
                        if n == 2 and not first:
                            norm_sums(i - 1)
                        if n == 3 and not first:
                            spread(i - 1)
                    out = open_tp(i, "tail")
                    pe.wait_ge(xl_done, START + i + 1)
                    for q in range(4):
                        last = pe.transpose(out[0:PAD * (NB + 1), q * P:(q + 1) * P], tail[:, q, :], S.ident[:, :])
                    last.then_inc(S.tp_done, 1)
                    begin_front(i, 0)
                    for c in range(RT):
                        product(i, 15 + c)
                        if c < PT:
                            begin_front(i, c + 1)
                            turn_h0(i, c)
                        back(i, c)

                body(0, True)
                with pe.Fori(1, NG) as i:
                    body(i, False)
                norm_sums(NG - 1)
                spread(NG - 1)

            @block.scalar
            def _(act):
                act.nop().then_inc(e_done, START)
                def split(i, j):
                    S.W.split_hi(act, u0 + j + 2, PER, i, b_end(i, 3 * j + 2))

                def copy_block(i, n):
                    act.wait_ge(S.acc_done, b_end(i, n))
                    src = acc[n % 2][:, 0:RBN]
                    q, rb = n // 3, n % 3
                    if q < 4:
                        q = SSD_ORDER[q]
                        if n == 0:
                            act.wait_ge(conv_done, START + 4 * i)
                            act.wait_ge(xl_done, START + i)
                        m = RBN if rb < 2 else SEQ - 2 * RBN
                        ins = act.activation(xp[:, q, PAD + rb * RBN:PAD + rb * RBN + m], src[:, 0:m], ACT.Copy)
                        if rb == 2:
                            ins = act.activation(
                                xp[:, q, XW:].rearrange("p (b s) -> p b s", b=NB)[:, :, PAD:],
                                src[:, m:].rearrange("p (b s) -> p b s", b=NB), ACT.Copy)
                    elif q < 6:
                        if n == 12:
                            act.wait_ge(norm_done, START + i)
                        ins = act.activation(zt[:, q - 4, rb * RBN:(rb + 1) * RBN], src, ACT.Copy)
                    else:
                        if n == 18:
                            act.wait_ge(gb_st, DMA_HEAD + 16 * i)
                        ins = act.activation(gb[:, q - 6, rb * RBN:(rb + 1) * RBN], src, ACT.Copy)
                    ins.then_inc(S.acc_read_a, 1)
                    if n % 3 == 2:
                        split(i, n // 3)

                def silu_sig(i, m):
                    act.wait_ge(conv_done, START + 4 * i + m + 1)
                    act.wait_ge(silu_done, START + 4 * i + m)
                    if m == 0:
                        act.wait_ge(silu_z, START + 2 * i)
                    act.activation(sg[:, :], y[:, SSD_ORDER[m], :], ACT.Sigmoid).then_inc(sg_done, 1)

                def z_sig(i, q):
                    act.wait_ge(silu_done, START + 4 * i + 4)
                    act.wait_ge(silu_z, START + 2 * i + q)
                    act.wait_ge(S.acc_read_a, a_end(i, 14 + 3 * q))
                    act.activation(sg[:, :], zt[:, q, :], ACT.Sigmoid).then_inc(sg_done, 1)

                def gb_sig(i, q):
                    act.wait_ge(S.acc_read_a, a_end(i, 20 + 3 * q))
                    act.activation(gb[:, q, :], gb[:, q, :], ACT.Sigmoid).then_inc(gb_done, 1)

                def squares(i, q):
                    act.wait_ge(gate_mul, START + 2 * i + q + 1)
                    act.activation(zt[:, q, :], y[:, q, :], ACT.Square).then_inc(sq_done, 1)

                def roots(i):
                    act.wait_ge(var_done, START + i + 1)
                    act.activation(root[:, :], var[:, :], ACT.Sqrt).then_inc(rt_done, 1)

                def exps(i, c):
                    act.wait_ge(front, RT * i + c + 1)
                    act.wait_ge(y_read, START + max(c - 1, 0) + RT * i)
                    act.wait_ge(seg_done, START + RT * i + c + 1)
                    rows = al[:, :].rearrange("p (q h n) -> p q h n", q=2, h=2)
                    for h in range(2):
                        half = slice(64 * h, 64 * h + 64)
                        act.activation(grow[c % 2][half, :, :], rows[half, :, h, :], ACT.Exp)
                    act.activation(seg[c % 2][:, :, :], seg[c % 2][:, :, :], ACT.Exp).then_inc(e_done, 1)

                def body(i, first):
                    for n in range(15):
                        copy_block(i, n)
                        if n < 2 and not first:
                            squares(i - 1, n)
                        if n == 2 and not first:
                            roots(i - 1)
                        if n in SILU_AT:
                            silu_sig(i, SILU_AT.index(n))
                    exps(i, 0)
                    for c in range(RT):
                        copy_block(i, 15 + c)
                        if c + 1 < RT:
                            exps(i, c + 1)
                        if c in (3, 5):
                            z_sig(i, c // 2 - 1)
                        if c in (6, 8):
                            gb_sig(i, c // 2 - 3)

                body(0, True)
                with act.Fori(1, NG) as i:
                    body(i, False)
                squares(NG - 1, 0)
                squares(NG - 1, 1)
                roots(NG - 1)

            @block.vector
            def _(dve):
                for s in (conv_done, gate_mul, xl_done, y_read, y_done, seg_done, st_read, var_done):
                    dve.nop().then_inc(s, START)
                steps = S.dve_steps

                def link(ins):
                    pos = steps.mark(ins)
                    dve.wait_ge(steps.sem, steps.value(pos))

                def drain(i, ev):
                    dve.wait_ge(S.tp_done, tpv(i, ev))
                    return tp[SSD_TP.index(ev) % 2]

                def split(i, j):
                    S.W.split_lo(dve, u0 + j + 2, PER, i, b_end(i, 3 * j + 2))

                def group_vectors(i):
                    table = S.vec[:, V_CW:V_MN].rearrange("p (t c) -> p t c", t=5)
                    dve.tensor_copy(cw[:, :, 0:2], table[:, :, ds(2 * i, 2)])
                    dve.tensor_copy(cw[:, :, 2:4], table[:, :, KT:].rearrange("p t (m g) -> p t m g", m=2)[:, :, :, ds(i, 1)]
                                    .rearrange("p t m g -> p t (m g)"))
                    dve.tensor_copy(mn[:, :], S.vec[:, ds(V_MN + 2 * i, 2)])
                    dve.tensor_copy(dg[:, :], S.d_chan[:, ds(2 * i, 2)])
                    dve.tensor_copy(bdg[:, :, :], S.batch_decay[:, ds(2 * i, 2), :])
                    dve.tensor_copy(heads[:, :, :, :], S.heads[:, :, :, ds(4 * i, 4)]).then_inc(loaded, 1)
                    dve.wait_ge(loaded, i + 1)

                def conv(i, m):
                    q = SSD_ORDER[m]
                    dve.wait_ge(S.acc_read_a, a_end(i, 3 * m + 2))
                    if q == 0:
                        dve.wait_ge(y_st, DMA_HEAD + 16 * i)
                    p_in = xp[:, q, :]
                    s_in = xp[:, q, XW:].rearrange("p (b s) -> p b s", b=NB)
                    p_out = y[:, q, 0:SEQ]
                    s_out = y[:, q, SEQ:].rearrange("p (b s) -> p b s", b=NB)
                    for t in range(4):
                        for out, src in ((p_out, p_in[:, t:t + SEQ]), (s_out, s_in[:, :, t:t + TD])):
                            w = cw[:, t, q:q + 1]
                            if t == 0:
                                ins = dve.tensor_scalar(out, src, w, cw[:, 4, q:q + 1], ALU.mult, ALU.add)
                            else:
                                dve.wait_ge(steps.sem, steps.value(steps.pos - 1))
                                ins = dve.scalar_tensor_tensor(out, src, w, out, ALU.mult, ALU.add)
                            if t == 3 and out is s_out:
                                ins.then_inc(conv_done, 1)
                            else:
                                steps.mark(ins)

                def tails(i):
                    dve.tensor_copy(tail[:, :, 0:PAD], xp[:, :, XW - PAD:XW])
                    src = xp[:, :, XW:].rearrange("p q (b s) -> p q b s", b=NB)[:, :, :, TD:]
                    dve.tensor_copy(tail[:, :, PAD:].rearrange("p q (b s) -> p q b s", b=NB), src).then_inc(xl_done, 1)
                    n = PAD * (NB + 1)
                    src = drain(i, "tail")
                    dve.wait_ge(tail_st, DMA_HEAD + 96 * i)
                    dve.tensor_copy(tail_t[:, :, :].rearrange("r q c -> r (q c)"), src[0:n, :]).then_inc(S.tp_drained, 1)

                def rows(i, c):
                    src = drain(i, ("rows", c))
                    dve.wait_ge(st_done, START + 12 * i + max(c - 1, 0))
                    x = src[:, 0:HC].rearrange("p (h d) -> p h d", h=HPG)
                    for dst, s in ((dx, dtg), (dxe, deg)):
                        dve.tensor_tensor(dst[c % 2][:, :, :], x,
                                          s[:, c, :].unsqueeze(2).to_broadcast([P, HPG, HD]), ALU.mult)
                    dve.tensor_copy(b_rows[c % 2][:, :], src[:, HC:HC + NS]).then_inc(S.tp_drained, 1)

                def decays(i, c):
                    dve.wait_ge(front, RT * i + c + 1)
                    if c >= 1:
                        dve.wait_ge(m_done, RT * i + c)
                    if c >= 2:
                        dve.wait_ge(yy_done, RT * i + c - 1)
                    dve.tensor_tensor(cbm[:, :], cbb[:, 0:P], (S.tri if c < PT else S.tri_s)[:, :], ALU.mult)
                    s = seg[c % 2]
                    link(dve.tensor_tensor(s[:, :, :], al[:, :].rearrange("p (h n) -> p h n", h=HPG),
                                           dsg[:, c, :].unsqueeze(2).to_broadcast([P, HPG, P]), ALU.subtract))
                    dve.tensor_scalar(s[:, :, :], s[:, :, :], 0.0, None, ALU.min).then_inc(seg_done, 1)

                def mix(i, c):
                    dve.wait_ge(e_done, START + RT * i + c + 1)
                    s = seg[c % 2]
                    dve.tensor_tensor(s[:, :, :], s[:, :, :], cbm[:, :].unsqueeze(1).to_broadcast([P, HPG, P]),
                                      ALU.mult).then_inc(m_done, 1)

                def outputs(i, c):
                    rows_ = slice(c * P, (c + 1) * P)
                    dve.wait_ge(yy_done, RT * i + c + 1)
                    for q in range(2):
                        dve.scalar_tensor_tensor(y[:, q, rows_], y[:, q, rows_], dg[:, q:q + 1],
                                                 yy[:, q * P:(q + 1) * P], ALU.mult, ALU.add)
                    link(dve.tensor_tensor(off[:, :, :], yy[:, 2 * P:4 * P].rearrange("p (q n) -> p q n", q=2),
                                           grow[c % 2][:, :, :], ALU.mult))
                    dve.tensor_tensor(y[:, 0:2, rows_], y[:, 0:2, rows_], off[:, :, :], ALU.add).then_inc(y_read, 1)
                    dve.wait_ge(y_read, START + RT * i + c + 1)

                def advance(i, c):
                    link(dve.tensor_tensor(state[:, :, :], state[:, :, :],
                                           cdg[:, c, :].unsqueeze(2).to_broadcast([P, HPG, HD]), ALU.mult))
                    dve.wait_ge(st_done, START + 12 * i + c + 1)
                    dve.tensor_tensor(state[:, :, :], state[:, :, :],
                                      stb[:, 0:HC].rearrange("p (h d) -> p h d", h=HPG), ALU.add).then_inc(h_done, 1)

                def keep_h0(i, b):
                    src = drain(i, ("h0", b))
                    if b == 0:
                        dve.wait_ge(y_read, START + RT * i)
                    dve.tensor_copy(h0_t[b][:, :], src[:, 0:2 * P]).then_inc(S.tp_drained, 1)

                def norm_factors(i):
                    dve.wait_ge(norm_done, START + i + 1)
                    dve.tensor_scalar(var[:, :], yy[:, 0:RT], 1.0 / HC, EPS, ALU.mult, ALU.add).then_inc(var_done, 1)
                    dve.wait_ge(rt_done, i + 1)
                    inverse_root(dve, var[:, :], root[:, :], newton[:, :], rs[:, :], rec_done, 5 * i)

                def norm(i):
                    dve.wait_ge(spread_done, i + 1)
                    for rb in range(NRB):
                        cols = slice(rb * RBN, (rb + 1) * RBN)
                        for q in range(2):
                            ins = dve.scalar_tensor_tensor(y[:, q, cols], y[:, q, cols], mn[:, q:q + 1],
                                                           (al, cbb, stb)[rb][:, 0:RBN], ALU.mult, ALU.mult)
                    ins.then_inc(y_done, 2)

                def sample_states(i):
                    outputs(i, PT)
                    for q in range(2):
                        dve.wait_ge(silu_z, START + 2 * i + q + 1)
                        dve.tensor_tensor(y[:, q, :], y[:, q, :], zt[:, q, :], ALU.mult).then_inc(gate_mul, 1)
                    src = drain(i, "state")
                    dve.wait_ge(state_st, DMA_HEAD + 32 * i)
                    dve.tensor_copy(state_out[:, :, :].rearrange("p q n -> p (q n)"), src[:, 0:2 * P])\
                       .then_inc(S.tp_drained, 1)
                    for n in range(4):
                        q, half = n // 2, n % 2
                        dve.wait_ge(st_done, START + 12 * i + PT + n + 1)
                        for b in range(4):
                            ins = dve.scalar_tensor_tensor(
                                h0[:, q, 4 * half + b, :], h0[:, q, 4 * half + b, :], bdg[:, q, 4 * half + b:4 * half + b + 1],
                                (stb, cbb, al, yy)[n][:, b * NS:(b + 1) * NS], ALU.mult, ALU.add)
                        ins.then_inc(st_read, 1)

                dve.memset(xp[:, :, 0:PAD], 0.0)
                dve.memset(hist[:, :, :], 0.0).then_inc(hist_clear, 1)
                def body(i, first):
                    steps.body(i, SSD_STEPS)
                    src = drain(i, "hist")
                    dve.wait_ge(xl_done, START + i)
                    dve.tensor_copy(xp[:, :, XW:].rearrange("p q (b s) -> p q b s", b=NB)[:, :, :, 0:PAD],
                                    src[:, :].rearrange("p (q n) -> p q n", q=4)[:, :, 0:NB * PAD]
                                    .rearrange("p q (b s) -> p q b s", s=PAD))\
                       .then_inc(S.tp_drained, 1)
                    if not first:
                        norm_factors(i - 1)
                    split(i, 0)
                    if not first:
                        norm(i - 1)
                        dve.wait_ge(y_done, START + 2 * i)
                    group_vectors(i)
                    dve.wait_ge(S.tp_drained, tpv(i, "hist"))
                    for m in range(4):
                        if m >= 1:
                            split(i, m)
                        conv(i, m)
                    tails(i)
                    split(i, 4)
                    dve.memset(state[:, :, :], 0.0).then_inc(h_done, 1)
                    rows(i, 0)
                    decays(i, 0)
                    for c in range(RT):
                        mix(i, c)
                        if c < PT:
                            rows(i, c + 1)
                            decays(i, c + 1)
                            keep_h0(i, c)
                        if c % 3 == 2:
                            split(i, 5 + c // 3)
                        if c < PT:
                            outputs(i, c)
                            advance(i, c)
                        if c == PT - 1:
                            dve.tensor_tensor(b_blk[:, :, :], b_rows[PT % 2][:, :].unsqueeze(1).to_broadcast([P, NB, NS]),
                                              S.same_batch[:, 0:P:TD].unsqueeze(2).to_broadcast([P, NB, NS]), ALU.mult)
                    sample_states(i)
                    steps.end(0)

                body(0, True)
                with dve.Fori(1, NG) as i:
                    body(i, False)
                norm_factors(NG - 1)
                norm(NG - 1)
                steps.base += NG * SSD_STEPS

            @block.gpsimd
            def _(pool):
                pool.nop().then_inc(silu_z, START)
                pool.nop().then_inc(silu_done, START)
                with pool.Fori(0, NG) as i:
                    for m, q in enumerate(SSD_ORDER):
                        pool.wait_ge(sg_done, 6 * i + m + 1)
                        pool.tensor_tensor(y[:, q, :], y[:, q, :], sg[:, :], ALU.mult).then_inc(silu_done, 1)
                    for q in range(2):
                        pool.wait_ge(sg_done, 6 * i + 4 + q + 1)
                        pool.tensor_tensor(zt[:, q, :], zt[:, q, :], sg[:, :], ALU.mult).then_inc(silu_z, 1)
                    pool.wait_ge(sq_done, 2 * i + 2)
                    pool.tensor_tensor(zt[:, 0, :], zt[:, 0, :], zt[:, 1, :], ALU.add).then_inc(sq_added, 1)


def tools(nc, S, ctx, tag):
    def sb(name, shape, dt=F32):
        return ctx.enter_context(nc.sbuf_tensor(f"{tag}_{name}", shape, dt))

    def bank(name):
        return ctx.enter_context(nc.psum_tensor(f"{tag}_{name}", [P, 512], F32))

    def sem(name):
        return S.sem(f"{tag}_{name}")
    return sb, bank, sem


def tile_of(t, k):
    return t[ds(k, 1)].rearrange("a p n -> (a p) n")


def flat_tile(t, k, cols=slice(0, ROWS)):
    return t[:, ds(k, 1), cols].rearrange("p a n -> p (a n)")


def rb_cols(rb):
    return slice(rb * RBN, (rb + 1) * RBN)


def stream_pairs(S, sp, u0, tiles, next_tiles, work):
    n = KT // 2
    with sp.Fori(0, n - 2) as i:
        for j in range(2):
            S.W.load(sp, u0 + 4 + j, 2, i, tiles(i + 2, j))
            work(i, j, False)
    for i in range(n - 2, n):
        for j in range(2):
            S.W.load(sp, u0 + 4 + j, 2, i, next_tiles[2 * (i - n + 2) + j])
            work(i, j, i == n - 1)


def stage_attention_out(nc, S, A, b0, bv0, u0, tiles, next_tiles):
    with ExitStack() as ctx:
        sb, bank, sem = tools(nc, S, ctx, "a")
        src_t = [S.stream[:, n, 0:ROWS] for n in range(2)]
        gate = [sb(f"gate{n}", [P, ROWS]) for n in range(2)]
        out = [S.stream[:, 2 + n, 0:ROWS] for n in range(2)]
        first_src = src_t + out
        acc = [bank(f"acc{n}") for n in range(6)]
        src_in = S.o_in
        gate_in = [sem("gate_in0"), sem("gate_in1")]
        stored = [sem("st0"), sem("st1")]
        hi_done, lo_done = sem("hi"), sem("lo")
        S.part_stored = stored

        with nc.Block() as block:
            @block.sync
            def _(sp):
                for s in stored:
                    sp.nop().then_inc(s, DMA_HEAD)
                def source(src, m, j):
                    sp.wait_ge(lo_done, m - 1)
                    sp.dma_start(src_t[j][:, :], src).then_inc(src_in[j], 16)

                def load_gate(i, j):
                    sp.dma_start(gate[j][:, :], tile_of(S.d_gate_b, 2 * i + j)).then_inc(gate_in[j], 16)

                for m in range(KT):
                    if m >= 4:
                        sp.wait_ge(lo_done, m - 3)
                        sp.dma_start(first_src[m % 4][:, :], S.d_o[m]).then_inc(src_in[m % 4], 16)
                    if m in (3, 4):
                        load_gate(0, m - 3)

                sp.wait_ge(S.y_stored, DMA_HEAD + 16 * NG)
                source(S.d_y[0], KT, 0)
                source(S.d_y[1], KT + 1, 1)

                def work(i, j, last):
                    if not last:
                        source(tile_of(S.d_y, 2 * i + j + 2), 2 * i + KT + j + 2, j)
                    sp.wait_ge(S.acc_read_v, HEAD + bv0 + 6 * i + 3 * j + 3)
                    sp.dma_start(tile_of(S.d_part, 2 * i + j), out[j][:, :]).then_inc(stored[j], 16)
                    if not last:
                        load_gate(i + 1, j)

                stream_pairs(S, sp, u0, tiles, next_tiles, work)
            @block.tensor
            def _(pe):
                for j in range(2):
                    pe.wait_ge(S.lo_done, HEAD + u0 + j + 1)
                parts = [[w[(u0 + j) % 2][:, :].rearrange("p (k c) -> p k c", k=KT) for w in (S.w_hi, S.w_lo)]
                         for j in range(2)]
                for k in range(KT):
                    pe.wait_ge(lo_done, k + 1)
                    for n in range(6):
                        hi, lo = parts[n // 3]
                        for m, (w, a) in enumerate(((hi, S.R1_hi), (hi, S.R1_lo), (lo, S.R1_hi))):
                            last = pe.matmul(acc[n][:, 0:RBN], w[:, k, :], a[:, k, rb_cols(n % 3)],
                                             start=(k == 0 and m == 0), stop=(k == KT - 1 and m == 2))
                        if k == KT - 1:
                            last.then_inc(S.acc_done, 1)
                with pe.Fori(1, KT // 2) as i:
                    for n in range(6):
                        product_block(S, pe, (u0 + n // 3) % 2, acc[n], (S.R1_hi, S.R1_lo), n % 3,
                                      HEAD + u0 + 2 * i + n // 3 + 1, (S.acc_read_v, HEAD + bv0 + 6 * i + n - 5))

            @block.scalar
            def _(act):
                for m in range(KT):
                    act.wait_ge(src_in[m % 4], 16 * (m // 4 + 1))
                    act.activation(S.R1_hi[:, m, :], first_src[m % 4][:, :], ACT.Copy).then_inc(hi_done, 1)
                with act.Fori(0, KT // 2) as i:
                    for j in range(2):
                        act.wait_ge(src_in[j], 16 * (KT // 4 + 1) + 16 * i)
                        act.activation(flat_tile(S.R0_hi, 2 * i + j), src_t[j][:, :], ACT.Copy).then_inc(hi_done, 1)
                        S.W.split_hi(act, u0 + j + 2, 2, i, HEAD + b0 + 6 * i + 3 * j + 3)

            @block.vector
            def _(dve):
                for m in range(KT):
                    dve.wait_ge(hi_done, m + 1)
                    if m == 3:
                        dve.wait_ge(S.y_stored, DMA_HEAD + 16 * NG)
                    dve.tensor_tensor(S.R1_lo[:, m, :], first_src[m % 4][:, :], S.R1_hi[:, m, :].bitcast(F32),
                                      ALU.subtract).then_inc(lo_done, 1)
                with dve.Fori(0, KT // 2) as i:
                    for n in range(6):
                        j = n // 3
                        if n % 3 == 0:
                            dve.wait_ge(gate_in[j], 16 * i + 16)
                            dve.wait_ge(stored[j], DMA_HEAD + 16 * i)
                        dve.wait_ge(S.acc_done, HEAD + b0 + 6 * i + n + 1)
                        dve.tensor_tensor(out[j][:, rb_cols(n % 3)], acc[n][:, 0:RBN], gate[j][:, rb_cols(n % 3)],
                                          ALU.mult).then_inc(S.acc_read_v, 1)
                        if n % 3 == 1:
                            dve.wait_ge(hi_done, 2 * i + KT + j + 1)
                            dve.tensor_tensor(flat_tile(S.R0_lo, 2 * i + j), src_t[j][:, :],
                                              flat_tile(S.R0_hi, 2 * i + j).bitcast(F32), ALU.subtract)\
                               .then_inc(lo_done, 1)
                        if n % 3 == 2:
                            S.W.split_lo(dve, u0 + j + 2, 2, i, HEAD + b0 + 6 * i + 3 * j + 3)


def stage_merge(nc, S, A, b0, bv0, u0, tiles, next_tiles):
    with ExitStack() as ctx:
        sb, bank, sem = tools(nc, S, ctx, "b")
        gate = [S.stream[:, n, 0:ROWS] for n in range(2)]
        part = [S.stream[:, 2 + n, 0:ROWS] for n in range(2)]
        prod = [sb(f"prod{n}", [P, RBN]) for n in range(2)]
        acc = [bank(f"acc{n}") for n in range(6)]
        gate_in = [sem("gate_in0"), sem("gate_in1")]
        hi_done, sum_done, lo_done = sem("hi"), sem("sum"), sem("lo")

        with nc.Block() as block:
            @block.sync
            def _(sp):
                def arrive(i, j):
                    for dst, src in ((gate, S.d_gate_a), (part, S.d_part)):
                        sp.dma_start(dst[j][:, :], tile_of(src, 2 * i + j)).then_inc(gate_in[j], 16)

                def work(i, j, last):
                    if not last:
                        sp.wait_ge(lo_done, 6 * i + 3 * j + 3)
                        arrive(i + 1, j)

                for s in S.part_stored:
                    sp.wait_ge(s, DMA_HEAD + 16 * KT // 2)
                arrive(0, 0)
                arrive(0, 1)
                stream_pairs(S, sp, u0, tiles, next_tiles, work)

            @block.tensor
            def _(pe):
                pe.wait_ge(S.acc_read_v, HEAD + bv0)
                with pe.Fori(0, KT // 2) as i:
                    for n in range(6):
                        product_block(S, pe, (u0 + n // 3) % 2, acc[n], (S.R0_hi, S.R0_lo), n % 3,
                                      HEAD + u0 + 2 * i + n // 3 + 1, (S.acc_read_v, HEAD + bv0 + 6 * i + n - 5))

            @block.scalar
            def _(act):
                with act.Fori(0, KT // 2) as i:
                    for n in range(6):
                        j = n // 3
                        act.wait_ge(sum_done, 6 * i + n + 1)
                        act.activation(S.R1_hi[:, ds(2 * i + j, 1), rb_cols(n % 3)].rearrange("p a n -> p (a n)"),
                                       part[j][:, rb_cols(n % 3)], ACT.Copy).then_inc(hi_done, 1)
                        if n % 3 == 2:
                            S.W.split_hi(act, u0 + j + 2, 2, i, HEAD + b0 + 6 * i + 3 * j + 3)

            @block.vector
            def _(dve):
                def low(i, n):
                    j, cols = n // 3, rb_cols(n % 3)
                    dve.wait_ge(hi_done, 6 * i + n + 1)
                    d = ds(2 * i + j, 1)
                    dve.tensor_tensor(S.R1_lo[:, d, cols].rearrange("p a n -> p (a n)"), part[j][:, cols],
                                      S.R1_hi[:, d, cols].rearrange("p a n -> p (a n)").bitcast(F32),
                                      ALU.subtract).then_inc(lo_done, 1)

                with dve.Fori(0, KT // 2) as i:
                    for n in range(6):
                        j, cols = n // 3, rb_cols(n % 3)
                        if n % 3 == 0:
                            dve.wait_ge(gate_in[j], 32 * i + 32)
                        dve.wait_ge(S.acc_done, HEAD + b0 + 6 * i + n + 1)
                        dve.tensor_tensor(prod[n % 2][:, :], acc[n][:, 0:RBN], gate[j][:, cols], ALU.mult)\
                           .then_inc(S.acc_read_v, 1)
                        dve.wait_ge(S.acc_read_v, HEAD + bv0 + 6 * i + n + 1)
                        dve.tensor_tensor(part[j][:, cols], part[j][:, cols], prod[n % 2][:, :], ALU.add)\
                           .then_inc(sum_done, 1)
                        if n % 3 == 2:
                            S.W.split_lo(dve, u0 + j + 2, 2, i, HEAD + b0 + 6 * i + 3 * j + 3)
                        low(i, n)


def stage_out(nc, S, A, b0, bv0, u0, tiles, next_tiles):
    with ExitStack() as ctx:
        sb, bank, sem = tools(nc, S, ctx, "c")
        xr = [S.stream[:, n, 0:ROWS].rearrange("p (r c) -> p r c", c=P) for n in range(2)]
        xs = [S.stream[:, 2 + n, 0:ROWS] for n in range(2)]
        sq = [sb(f"sq{n}", [P, RBN]) for n in range(2)]
        gcol = sb("gcol", [P, 2])
        acc = [bank("acc0"), bank("acc1")]
        x_in, stored = [sem("x_in0"), sem("x_in1")], [sem("st0"), sem("st1")]
        S.x_stored = stored
        hi_done, lo_done, sq_done, ss_done, col_done, zeroed = (
            sem("hi"), sem("lo"), sem("sq"), sem("ss"), sem("col"), sem("zeroed"))

        with nc.Block() as block:
            @block.sync
            def _(sp):
                for s in stored:
                    sp.nop().then_inc(s, DMA_HEAD)
                def x_cols(i, j):
                    cols = ds((2 * i + j) * P, P)
                    sp.dma_start(xr[j][:, 0:PT, :], A.x_prompt[0].rearrange("(r p) c -> p r c", p=P)[:, :, cols])\
                      .then_inc(x_in[j], 16)
                    sp.dma_start(xr[j][:, PT, :], A.x_sample.rearrange("b t c -> (b t) c")[:, cols])\
                      .then_inc(x_in[j], 16)

                def work(i, j, last):
                    sp.wait_ge(S.acc_read_v, HEAD + bv0 + 6 * i + 3 * j + 3)
                    sp.dma_start(tile_of(S.d_x, 2 * i + j), xs[j][:, :]).then_inc(stored[j], 16)
                    if not last:
                        x_cols(i + 1, j)

                x_cols(0, 0)
                x_cols(0, 1)
                stream_pairs(S, sp, u0, tiles, next_tiles, work)

            @block.tensor
            def _(pe):
                with pe.Fori(0, KT // 2) as i:
                    for n in range(6):
                        j, rb, a = n // 3, n % 3, acc[n % 2]

                        def add_x():
                            pe.wait_ge(x_in[j], 32 * i + 32)
                            for r in range(3):
                                last = pe.matmul(a[:, r * P:(r + 1) * P], xr[j][:, 3 * rb + r, :], S.ident[:, :],
                                                 start=False, stop=(r == 2))
                            return last
                        product_block(S, pe, (u0 + j) % 2, a, (S.R1_hi, S.R1_lo), rb,
                                      HEAD + u0 + 2 * i + j + 1, (S.acc_read_v, HEAD + bv0 + 6 * i + n - 1), more=add_x)

            @block.scalar
            def _(act):
                for s in (hi_done, sq_done):
                    act.nop().then_inc(s, START)
                with act.Fori(0, KT // 2) as i:
                    for n in range(6):
                        j, cols = n // 3, rb_cols(n % 3)
                        act.wait_ge(S.acc_read_v, HEAD + bv0 + 6 * i + n + 1)
                        act.wait_ge(ss_done, START + 6 * i + max(n - 1, 0))
                        act.activation(sq[n % 2][:, :], xs[j][:, cols], ACT.Square).then_inc(sq_done, 1)
                        act.wait_ge(col_done, i + 1)
                        act.activation(S.R0_hi[:, ds(2 * i + j, 1), cols].rearrange("p a n -> p (a n)"), xs[j][:, cols],
                                       ACT.Copy, scale=gcol[:, j:j + 1]).then_inc(hi_done, 1)
                        if n % 3 == 2:
                            S.W.split_hi(act, u0 + j + 2, 2, i, HEAD + b0 + 6 * i + 3 * j + 3)

            @block.vector
            def _(dve):
                dve.nop().then_inc(lo_done, START)
                dve.memset(S.ss[:, :], 0.0).then_inc(zeroed, 1)
                with dve.Fori(0, KT // 2) as i:
                    dve.wait_ge(hi_done, START + 6 * i)
                    dve.wait_ge(lo_done, START + 6 * i)
                    dve.tensor_copy(gcol[:, :], S.vec[:, ds(V_FFN + 2 * i, 2)]).then_inc(col_done, 1)
                    dve.wait_ge(col_done, i + 1)
                    for n in range(6):
                        j, cols = n // 3, rb_cols(n % 3)
                        if n % 3 == 0:
                            dve.wait_ge(stored[j], DMA_HEAD + 16 * i)
                            dve.wait_ge(sq_done, START + 6 * i)
                        dve.wait_ge(S.acc_done, HEAD + b0 + 6 * i + n + 1)
                        dve.tensor_copy(xs[j][:, cols], acc[n % 2][:, 0:RBN]).then_inc(S.acc_read_v, 1)
                        dve.wait_ge(hi_done, START + 6 * i + n + 1)
                        d = ds(2 * i + j, 1)
                        dve.scalar_tensor_tensor(S.R0_lo[:, d, cols].rearrange("p a n -> p (a n)"), xs[j][:, cols],
                                                 gcol[:, j:j + 1],
                                                 S.R0_hi[:, d, cols].rearrange("p a n -> p (a n)").bitcast(F32),
                                                 ALU.mult, ALU.subtract).then_inc(lo_done, 1)
                        if n % 3 == 2:
                            S.W.split_lo(dve, u0 + j + 2, 2, i, HEAD + b0 + 6 * i + 3 * j + 3)

            @block.gpsimd
            def _(pool):
                pool.nop().then_inc(ss_done, START)
                pool.wait_ge(zeroed, 1)
                with pool.Fori(0, KT // 2) as i:
                    for n in range(6):
                        cols = rb_cols(n % 3)
                        pool.wait_ge(sq_done, START + 6 * i + n + 1)
                        if n >= 3:
                            pool.wait_ge(ss_done, START + 6 * i + n - 2)
                        pool.tensor_tensor(S.ss[:, cols], S.ss[:, cols], sq[n % 2][:, :], ALU.add).then_inc(ss_done, 1)


def down_tile(A, i, half):
    return A.w_down[0].rearrange("(f k p) c -> f p k c", k=2, p=P)[ds(i, 1), :, :, half * 512:half * 512 + 512]\
        .rearrange("a p k c -> (a p) k c")


def stage_ffn(nc, S, A, b0, bv0, u0, next_tiles):
    N = FT // 2
    with ExitStack() as ctx:
        sb, bank, sem = tools(nc, S, ctx, "f")
        x = S.x_t
        rstd = sb("rstd", [P, ROWS])
        act_hi, act_lo = sb("act_hi", [P, 2, ROWS], F32R), sb("act_lo", [P, 2, ROWS], F32R)
        hid = [sb(f"hid{n}", [P, ROWS]) for n in range(2)]
        gs = [sb(f"gs{n}", [P, RBN]) for n in range(3)]
        sg = [sb(f"sg{n}", [P, RBN]) for n in range(3)]
        squares = gs + sg
        acc = [bank(f"acc{n}") for n in range(6)]
        ssum = bank("ssum")
        x_in = sem("x_in")
        sum_done, var_done, root_done = sem("sum"), sem("var"), sem("root")
        sg_done, hi_done, sq_done, xg_done = sem("sg"), sem("hi"), sem("sq"), sem("xg")
        steps = Steps(sem("steps"))
        steps.base = 0
        hid_done, ss_done = sem("hid"), sem("ss")

        def blk(i, part, n):
            if isinstance(i, int) and i == 0:
                return {"up0": 0, "up1": 6}[part] + n
            return 12 + 36 * (i - 1) + {"up0": 0, "down": 6, "up1": 30}[part] + n

        def blk_last(d, rb):
            return 12 + 36 * (N - 1) + 3 * d + rb + 1

        def slot(part, n):
            return ({"up0": 0, "down": 6, "up1": 30}[part] + n) % 6

        with nc.Block() as block:
            def up_tile(i, j):
                w = A.w_gate[0] if j % 2 == 0 else A.w_up[0]
                return wsrc(w, (2 * i + j // 2) * P)

            @block.sync
            def _(sp):
                for s in S.x_stored:
                    sp.wait_ge(s, DMA_HEAD + 16 * KT // 2)
                for k in range(KT):
                    sp.dma_start(x[:, k, :], S.d_x[k]).then_inc(x_in, 16)
                with sp.Fori(0, N - 1) as i:
                    order = (up_tile(i + 1, 0), up_tile(i + 1, 1), down_tile(A, i, 0), down_tile(A, i, 1),
                             up_tile(i + 1, 2), up_tile(i + 1, 3))
                    for j in range(6):
                        S.W.load(sp, u0 + 4 + j, 6, i, order[j])
                u = u0 + 4 + 6 * (N - 1)
                for j, t in enumerate([down_tile(A, N - 1, 0), down_tile(A, N - 1, 1)] + list(next_tiles)):
                    S.W.load(sp, u + j, 2, 0, t)

            @block.tensor
            def _(pe):
                def up(i, part, n):
                    b = blk(i, part, n)
                    t = (0 if part == "up0" else 2) + n // 3 if isinstance(i, int) and i == 0 else \
                        4 + 6 * (i - 1) + (0 if part == "up0" else 4) + n // 3
                    par = ((0 if part == "up0" else 2) + n // 3) % 2
                    product_block(S, pe, (u0 + par) % 2, acc[slot(part, n)], (S.R0_hi, S.R0_lo), n % 3,
                                  HEAD + u0 + t + 1, (S.acc_read_v, HEAD + bv0 + b - 5))

                def down(i):
                    for n in range(24):
                        d, rb = n // 3, n % 3
                        half = d // 4
                        final = isinstance(i, int)
                        b = blk(i, "down", n) - (6 if final else 0)
                        pe.wait_ge(S.lo_done, HEAD + u0 + 4 + 6 * (i - 1) + (0 if final else 2) + half + 1)
                        if n == 0:
                            pe.wait_ge(steps.sem, low_value(i))
                        pe.wait_ge(S.acc_read_v, HEAD + bv0 + b - 5)
                        s = (u0 + half) % 2
                        wh = S.w_hi[s][:, :].rearrange("p (k c) -> p k c", k=2)
                        wl = S.w_lo[s][:, :].rearrange("p (k c) -> p k c", k=2)
                        m = 0
                        a = acc[slot("down", n)]
                        for k in range(2):
                            for w, r in ((wh, act_hi), (wh, act_lo), (wl, act_hi)):
                                last = pe.matmul(a[:, 0:RBN], w[:, k, (d % 4) * P:(d % 4 + 1) * P],
                                                 r[:, k, rb_cols(rb)], start=(m == 0), stop=(m == 5))
                                m += 1
                        last.then_inc(S.acc_done, 1)

                def low_value(i):
                    return F_FIRST + F_PASS * (i - 1)

                for rb in range(NRB):
                    if rb >= 1:
                        pe.wait_ge(var_done, rb)
                    pe.matmul(ssum[:, 0:RBN], S.ones[:, :], S.ss[:, rb_cols(rb)], start=True, stop=True)\
                      .then_inc(sum_done, 1)
                pe.wait_ge(S.acc_read_v, HEAD + bv0)
                for n in range(6):
                    up(0, "up0", n)
                for n in range(6):
                    up(0, "up1", n)
                with pe.Fori(1, N) as i:
                    for n in range(6):
                        up(i, "up0", n)
                    down(i)
                    for n in range(6):
                        up(i, "up1", n)
                down(N)

            @block.scalar
            def _(act):
                def split(u, per, i, last):
                    S.W.split_hi(act, u, per, i, last)

                def gates(i, part):
                    for rb in range(3):
                        act.wait_ge(S.acc_read_v, HEAD + bv0 + blk(i, part, rb) + 1)
                        act.activation(sg[rb][:, :], gs[rb][:, :], ACT.Sigmoid).then_inc(sg_done, 1)

                def highs(i, k):
                    for rb in range(3):
                        act.wait_ge(hid_done, 6 * i + 3 * k + rb + 1)
                        if k == 0 and rb == 0 and not (isinstance(i, int) and i == 0):
                            act.wait_ge(S.acc_done, HEAD + b0 + blk(i, "down", 24))
                        act.activation(act_hi[:, k, rb_cols(rb)], hid[k][:, rb_cols(rb)], ACT.Copy).then_inc(hi_done, 1)

                for rb in range(NRB):
                    act.wait_ge(var_done, rb + 1)
                    act.activation(rstd[:, rb_cols(rb)], rstd[:, rb_cols(rb)], ACT.Sqrt).then_inc(root_done, 1)
                split(u0 + 2, 2, 0, HEAD + b0 + 3)
                gates(0, "up0")
                split(u0 + 3, 2, 0, HEAD + b0 + 6)
                highs(0, 0)
                split(u0 + 4, 2, 0, HEAD + b0 + 9)
                gates(0, "up1")
                split(u0 + 5, 2, 0, HEAD + b0 + 12)
                highs(0, 1)
                with act.Fori(1, N) as i:
                    b = HEAD + b0 + 12 + 36 * (i - 1)
                    u = u0 + 6
                    split(u, 6, i - 1, b + 3)
                    gates(i, "up0")
                    split(u + 1, 6, i - 1, b + 6)
                    split(u + 2, 6, i - 1, b + 18)
                    split(u + 3, 6, i - 1, b + 30)
                    highs(i, 0)
                    split(u + 4, 6, i - 1, b + 33)
                    gates(i, "up1")
                    split(u + 5, 6, i - 1, b + 36)
                    highs(i, 1)
                b = HEAD + b0 + 12 + 36 * (N - 1)
                u = u0 + 4 + 6 * (N - 1) + 2
                for d in range(KT):
                    for rb in range(3):
                        act.wait_ge(S.acc_read_v, HEAD + bv0 + blk_last(d, rb))
                        m = 3 * d + rb
                        if m >= 6:
                            act.wait_ge(ss_done, m - 5)
                        act.activation(S.R0_hi[:, d, rb_cols(rb)], x[:, d, rb_cols(rb)], ACT.Copy,
                                       scale=S.vec[:, V_PLE + d:V_PLE + d + 1]).then_inc(hi_done, 1)
                        act.activation(squares[m % 6][:, :], x[:, d, rb_cols(rb)], ACT.Square).then_inc(sq_done, 1)
                    if d % 4 == 3:
                        split(u + d // 4, 2, 0, b + 3 * d + 3)

            @block.vector
            def _(dve):
                def gate_up(i, part, k):
                    for rb in range(3):
                        n = blk(i, part, rb)
                        dve.wait_ge(S.acc_done, HEAD + b0 + n + 1)
                        dve.tensor_tensor(gs[rb][:, :], acc[slot(part, rb)][:, 0:RBN], rstd[:, rb_cols(rb)], ALU.mult)\
                           .then_inc(S.acc_read_v, 1)
                    split_after(i, part, 0)
                    for rb in range(3):
                        n = blk(i, part, 3 + rb)
                        dve.wait_ge(sg_done, 6 * i + (0 if part == "up0" else 3) + rb + 1)
                        steps.mark(dve.tensor_tensor(gs[rb][:, :], gs[rb][:, :], sg[rb][:, :], ALU.mult))
                        dve.wait_ge(S.acc_done, HEAD + b0 + n + 1)
                        h = hid[k][:, rb_cols(rb)]
                        dve.tensor_tensor(h, acc[slot(part, 3 + rb)][:, 0:RBN], rstd[:, rb_cols(rb)], ALU.mult)\
                           .then_inc(S.acc_read_v, 1)
                        dve.wait_ge(S.acc_read_v, HEAD + bv0 + n + 1)
                        dve.tensor_tensor(h, h, gs[rb][:, :], ALU.mult).then_inc(hid_done, 1)
                    split_after(i, part, 1)

                def lows(i, k):
                    for rb in range(3):
                        cols = rb_cols(rb)
                        dve.wait_ge(hi_done, 6 * i + 3 * k + rb + 1)
                        steps.mark(dve.tensor_tensor(act_lo[:, k, cols], hid[k][:, cols],
                                                     act_hi[:, k, cols].bitcast(F32), ALU.subtract))

                def split_after(i, part, j):
                    if isinstance(i, int) and i == 0:
                        u, last = {"up0": (2, 3), "up1": (4, 9)}[part]
                        S.W.split_lo(dve, u0 + u + j, 2, 0, HEAD + b0 + last + 3 * j)
                        return
                    b = HEAD + b0 + 12 + 36 * (i - 1)
                    u, last = {"up0": (6, 3), "up1": (10, 33)}[part]
                    S.W.split_lo(dve, u0 + u + j, 6, i - 1, b + last + 3 * j)

                def down(i, final=False):
                    b = HEAD + b0 + 12 + 36 * (i - 1) + (0 if final else 6)
                    for n in range(24):
                        d, rb = n // 3, n % 3
                        dve.wait_ge(S.acc_done, b + n + 1)
                        if n == 0:
                            dve.wait_ge(x_in, 16 * KT)
                        if final and n >= LAG:
                            low_last(n - LAG)
                        ins = dve.tensor_tensor(x[:, d, rb_cols(rb)], x[:, d, rb_cols(rb)],
                                                acc[slot("down", n)][:, 0:RBN], ALU.add)
                        ins.then_inc(S.acc_read_v, 1)
                        if n % 12 == 11:
                            if not final:
                                S.W.split_lo(dve, u0 + 8 + n // 12, 6, i - 1, b + n + 1)
                            else:
                                if n == 23:
                                    for m in range(24 - LAG, 24):
                                        low_last(m)
                                S.W.split_lo(dve, u0 + 4 + 6 * (N - 1) + 2 + n // 12, 2, 0, b + n + 1)

                LAG = 3

                def low_last(n):
                    d, cols = n // 3, rb_cols(n % 3)
                    dve.wait_ge(hi_done, 6 * N + n + 1)
                    dve.scalar_tensor_tensor(S.R0_lo[:, d, cols], x[:, d, cols], S.vec[:, V_PLE + d:V_PLE + d + 1],
                                             S.R0_hi[:, d, cols].bitcast(F32), ALU.mult, ALU.subtract)\
                       .then_inc(xg_done, 1)

                for rb in range(NRB):
                    dve.wait_ge(sum_done, rb + 1)
                    dve.tensor_scalar(rstd[:, rb_cols(rb)], ssum[:, 0:RBN], 1.0 / D, EPS, ALU.mult, ALU.add)\
                       .then_inc(var_done, 1)
                for rb in range(NRB):
                    dve.wait_ge(root_done, rb + 1)
                    steps.i, steps.per = 0, 0
                    steps.pos = rb
                    steps.mark(dve.reciprocal(rstd[:, rb_cols(rb)], rstd[:, rb_cols(rb)]))
                dve.wait_ge(steps.sem, 3)
                steps.base = 3
                steps.body(0, F_PASS)
                gate_up(0, "up0", 0)
                lows(0, 0)
                gate_up(0, "up1", 1)
                lows(0, 1)
                steps.end(1)
                with dve.Fori(1, N) as i:
                    steps.body(i - 1, F_PASS)
                    gate_up(i, "up0", 0)
                    down(i)
                    lows(i, 0)
                    gate_up(i, "up1", 1)
                    lows(i, 1)
                    steps.end(0)
                down(N, final=True)

            @block.gpsimd
            def _(pool):
                for n in range(24):
                    d, rb = n // 3, n % 3
                    pool.wait_ge(sq_done, n + 1)
                    if d == 0:
                        pool.tensor_copy(S.ss[:, rb_cols(rb)], squares[n % 6][:, :]).then_inc(ss_done, 1)
                    else:
                        pool.wait_ge(ss_done, n - 2)
                        pool.tensor_tensor(S.ss[:, rb_cols(rb)], S.ss[:, rb_cols(rb)], squares[n % 6][:, :], ALU.add)\
                            .then_inc(ss_done, 1)


F_PASS = 12
F_FIRST = 3 + F_PASS


def ple_tile(A, d, j):
    return wsrc(A.w_ple_gate[0] if j == 0 else A.w_ple[0], d * P)


def stage_ple(nc, S, A, b0, bv0, u0):
    with ExitStack() as ctx:
        sb, bank, sem = tools(nc, S, ctx, "p")
        x = S.x_t
        rstd = sb("rstd", [P, ROWS])
        pr = sb("p_rows", [P, RT, PLE])
        p_hi, p_lo = sb("p_hi", [P, 2, ROWS], F32R), sb("p_lo", [P, 2, ROWS], F32R)
        gs = [sb(f"gs{n}", [P, RBN]) for n in range(3)]
        pe_t = [sb(f"emb{n}", [P, RBN]) for n in range(3)]
        acc = [bank(f"acc{n}") for n in range(6)]
        tp = [bank(f"tp{n}") for n in range(2)]
        p_in, sum_done, var_done, root_done = sem("p_in"), sem("sum"), sem("var"), sem("root")
        pt_done, phi_done, plo_done = sem("pt"), sem("phi"), sem("plo")
        sg_done, rec_done, mul_done = sem("sg"), sem("rec"), sem("mul")
        N = KT

        with nc.Block() as block:
            @block.sync
            def _(sp):
                sp.dma_start(pr[:, 0:PT, :], A.p_prompt[0, 0].rearrange("(r p) c -> p r c", p=P)).then_inc(p_in, 16)
                sp.dma_start(pr[:, PT, :], A.p_sample[0].rearrange("b t c -> (b t) c")).then_inc(p_in, 16)
                with sp.Fori(0, N - 2) as i:
                    for j in range(2):
                        S.W.load(sp, u0 + 4 + j, 2, i, ple_tile(A, i + 2, j))

            @block.tensor
            def _(pe):
                for rb in range(NRB):
                    if rb >= 1:
                        pe.wait_ge(var_done, rb)
                    pe.matmul(tp[0][:, 0:RBN], S.ones[:, :], S.ss[:, rb_cols(rb)], start=True, stop=True)\
                      .then_inc(sum_done, 1)
                pe.wait_ge(var_done, 3)
                pe.wait_ge(p_in, 32)
                for m in range(6):
                    if m >= 2:
                        pe.wait_ge(plo_done, m - 1)
                    for r in range(3):
                        last = pe.transpose(tp[m % 2][:, r * P:(r + 1) * P],
                                            pr[:, 3 * (m // 2) + r, (m % 2) * P:(m % 2 + 1) * P], S.ident[:, :])
                    last.then_inc(pt_done, 1)
                pe.wait_ge(plo_done, 6)
                pe.wait_ge(S.acc_read_v, HEAD + bv0)
                with pe.Fori(0, N) as i:
                    for n in range(6):
                        product_block(S, pe, (u0 + n // 3) % 2, acc[n],
                                      (S.R0_hi, S.R0_lo) if n < 3 else (p_hi, p_lo), n % 3,
                                      HEAD + u0 + 2 * i + n // 3 + 1, (S.acc_read_v, HEAD + bv0 + 6 * i + n - 5),
                                      kts=KT if n < 3 else 2)

            @block.scalar
            def _(act):
                for rb in range(NRB):
                    act.wait_ge(var_done, rb + 1)
                    act.activation(rstd[:, rb_cols(rb)], rstd[:, rb_cols(rb)], ACT.Sqrt).then_inc(root_done, 1)
                for m in range(6):
                    act.wait_ge(pt_done, m + 1)
                    act.activation(p_hi[:, m % 2, rb_cols(m // 2)], tp[m % 2][:, 0:RBN], ACT.Copy).then_inc(phi_done, 1)

                def body(i, last):
                    if not last:
                        S.W.split_hi(act, u0 + 2, 2, i, HEAD + b0 + 6 * i + 3)
                    for n in range(3):
                        act.wait_ge(S.acc_read_v, HEAD + bv0 + 6 * i + n + 1)
                        act.activation(gs[n][:, :], gs[n][:, :], ACT.Sigmoid).then_inc(sg_done, 1)
                    if not last:
                        S.W.split_hi(act, u0 + 3, 2, i, HEAD + b0 + 6 * i + 6)
                with act.Fori(0, N - 1) as i:
                    body(i, False)
                body(N - 1, True)

            @block.vector
            def _(dve):
                dve.nop().then_inc(mul_done, START)
                for rb in range(NRB):
                    dve.wait_ge(sum_done, rb + 1)
                    dve.tensor_scalar(rstd[:, rb_cols(rb)], tp[0][:, 0:RBN], 1.0 / D, EPS, ALU.mult, ALU.add)\
                       .then_inc(var_done, 1)
                for m in range(6):
                    dve.wait_ge(phi_done, m + 1)
                    cols = rb_cols(m // 2)
                    dve.tensor_tensor(p_lo[:, m % 2, cols], tp[m % 2][:, 0:RBN], p_hi[:, m % 2, cols].bitcast(F32),
                                      ALU.subtract).then_inc(plo_done, 1)
                for rb in range(NRB):
                    dve.wait_ge(root_done, rb + 1)
                    dve.reciprocal(rstd[:, rb_cols(rb)], rstd[:, rb_cols(rb)]).then_inc(rec_done, 1)
                dve.wait_ge(rec_done, 3)

                def body(i, last):
                    for n in range(3):
                        dve.wait_ge(S.acc_done, HEAD + b0 + 6 * i + n + 1)
                        dve.wait_ge(mul_done, START + 3 * i)
                        dve.tensor_tensor(gs[n][:, :], acc[n][:, 0:RBN], rstd[:, rb_cols(n)], ALU.mult)\
                           .then_inc(S.acc_read_v, 1)
                    if not last:
                        S.W.split_lo(dve, u0 + 2, 2, i, HEAD + b0 + 6 * i + 3)
                    for n in range(3):
                        dve.wait_ge(S.acc_done, HEAD + b0 + 6 * i + 3 + n + 1)
                        dve.wait_ge(sg_done, 3 * i + n + 1)
                        dve.tensor_tensor(pe_t[n][:, :], acc[3 + n][:, 0:RBN], gs[n][:, :], ALU.mult)\
                           .then_inc(S.acc_read_v, 1)
                        dve.wait_ge(S.acc_read_v, HEAD + bv0 + 6 * i + 3 + n + 1)
                        xv = x[:, ds(i, 1), rb_cols(n)].rearrange("p a n -> p (a n)")
                        dve.tensor_tensor(xv, xv, pe_t[n][:, :], ALU.add).then_inc(mul_done, 1)
                    if not last:
                        S.W.split_lo(dve, u0 + 3, 2, i, HEAD + b0 + 6 * i + 6)

                with dve.Fori(0, N - 1) as i:
                    body(i, False)
                body(N - 1, True)


def stage_final(nc, S, A):
    with ExitStack() as ctx:
        sb, bank, sem = tools(nc, S, ctx, "end")
        gain = sb("gain", [P, D])
        junk = sb("squares", [P, D])
        var, root, rstd = sb("var", [P, RT]), sb("root", [P, RT]), sb("rstd", [P, RT])
        out = [sb(f"out{n}", [P, D]) for n in range(3)]
        pt = [ctx.enter_context(nc.psum_tensor(f"y_t{n}", [P, D], F32)) for n in range(4)]
        gain_in, t_done, sq_done, var_done, root_done, rec_done, out_done = (
            sem("gain_in"), sem("t"), sem("sq"), sem("var"), sem("root"), sem("rec"), sem("out"))
        stored = [sem(f"st{n}") for n in range(3)]
        with nc.Block() as block:
            @block.sync
            def _(sp):
                sp.dma_start(gain[:, :], A.final_norm_g.unsqueeze(0).to_broadcast([P, D])).then_inc(gain_in, 16)
                for r in range(RT):
                    sp.wait_ge(out_done, r + 1)
                    dst = A.y_prompt[0, r * P:(r + 1) * P, :] if r < PT else A.y_sample.rearrange("b t d -> (b t) d")
                    sp.dma_start(dst, out[r % 3][:, :]).then_inc(stored[r % 3], 16)
                for n in range(3):
                    sp.wait_ge(stored[n], 16 * (RT // 3))

            @block.tensor
            def _(pe):
                for r in range(RT):
                    if r >= 4:
                        pe.wait_ge(out_done, r - 3)
                    for k in range(KT):
                        last = pe.transpose(pt[r % 4][:, k * P:(k + 1) * P], S.x_t[:, k, r * P:(r + 1) * P], S.ident[:, :])
                    last.then_inc(t_done, 1)

            @block.scalar
            def _(act):
                for r in range(RT + 1):
                    if r < RT:
                        act.wait_ge(t_done, r + 1)
                        if r >= 1:
                            act.wait_ge(sq_done, r)
                        act.activation(junk[:, :], pt[r % 4][:, :], ACT.Square, accum_out=var[:, r:r + 1])\
                           .then_inc(sq_done, 1)
                    if r >= 1:
                        act.wait_ge(var_done, r)
                        act.activation(root[:, r - 1:r], rstd[:, r - 1:r], ACT.Sqrt).then_inc(root_done, 1)

            @block.vector
            def _(dve):
                dve.wait_ge(gain_in, 16)
                for m in range(RT + 1):
                    if m < RT:
                        dve.wait_ge(sq_done, m + 1)
                        dve.tensor_scalar(rstd[:, m:m + 1], var[:, m:m + 1], 1.0 / D, EPS, ALU.mult, ALU.add)\
                           .then_inc(var_done, 1)
                    if m >= 1:
                        r = m - 1
                        dve.wait_ge(root_done, r + 1)
                        dve.reciprocal(rstd[:, r:r + 1], root[:, r:r + 1]).then_inc(rec_done, 1)
                        dve.wait_ge(rec_done, r + 1)
                        if r >= 3:
                            dve.wait_ge(stored[r % 3], 16 * (r // 3))
                        dve.scalar_tensor_tensor(out[r % 3][:, :], pt[r % 4][:, :], rstd[:, r:r + 1], gain[:, :],
                                                 ALU.mult, ALU.mult).then_inc(out_done, 1)


PAIR_STEPS = 33
SSD_STEPS = 54


def hybrid_step(nc, A):
    S = Store()
    with ExitStack() as ctx:
        def sb(name, shape, dt=F32):
            return ctx.enter_context(nc.sbuf_tensor(name, shape, dt))

        def sem(name):
            return ctx.enter_context(nc.semaphore(name))

        S.sem = sem
        S.W = WeightStream(S)
        def dram(name):
            return nc.dram_tensor(name, (KT, P, ROWS), F32).ap()
        S.d_gate_a, S.d_gate_b, S.d_o, S.d_y, S.d_part, S.d_x = [
            dram(n) for n in ("s_gate_a", "s_gate_b", "s_o", "s_y", "s_attention_part", "s_x")]
        S.acc_done, S.acc_read_a, S.acc_read_v = sem("acc_done"), sem("acc_read_a"), sem("acc_read_v")
        S.hi_done, S.lo_done, S.raw_in = sem("w_hi_done"), sem("w_lo_done"), [sem("raw_in0"), sem("raw_in1")]
        S.z_done, S.tp_done, S.av_done = sem("z_done"), sem("tp_done"), sem("av_done")
        S.kk_done, S.gg_done, S.o_read = sem("keep_done"), sem("grab_done"), sem("o_read")
        S.tp_drained, S.p_done, S.pw_done = sem("tp_drained"), sem("left_done"), sem("weights_done")
        S.dve_steps = Steps(sem("dve_steps"))

        S.raw = [sb(f"w_raw{n}", [P, D]) for n in range(2)]
        S.w_hi = [sb(f"w_hi{n}", [P, D], F32R) for n in range(2)]
        S.w_lo = [sb(f"w_lo{n}", [P, D], F32R) for n in range(2)]
        S.R0_hi, S.R0_lo = sb("operand0_hi", [P, KT, ROWS], F32R), sb("operand0_lo", [P, KT, ROWS], F32R)
        S.ident, S.ones = sb("ident", [P, P]), sb("ones", [P, P])
        S.ident_b, S.mask_p = sb("ident_bf16", [P, P], BF16), sb("mask_prompt", [P, P], BF16)
        S.mask_s = [sb(f"mask_sample{n}", [P, P], BF16) for n in range(2)]
        S.tri, S.tri_s, S.same_batch = sb("tri", [P, P]), sb("tri_sample", [P, P]), sb("same_batch", [P, P])
        S.vec = sb("vectors", [P, V_ALL])
        S.dt_bias, S.a_log, S.d_heads, S.d_chan = sb("dt_bias", [P, NH]), sb("a_log", [P, NH]), sb("d_heads", [P, NH]), sb("d_chan", [P, KT])
        S.heads = sb("head_values", [P, 5, RT, NH])
        S.dt, S.dta, S.dsum, S.dt_end, S.chunk_decay = [S.heads[:, n, :, :] for n in range(5)]
        S.batch_decay = sb("batch_decay", [P, KT, NB])

        w_in, w_a, w_b, w_out = A.w_in[0], A.w_a[0], A.w_b[0], A.w_out[0]

        def pair_tiles(i, j):
            return wsrc(w_in, (OFF_Q, OFF_K, OFF_V, OFF_GA)[j] + i * P)

        def ssd_tiles(i, j):
            at = (OFF_XBC + D + i * P, OFF_XBC + D + NG * NS + i * P, OFF_XBC + 2 * i * P, OFF_XBC + (2 * i + 1) * P,
                  OFF_Z + 2 * i * P, OFF_Z + (2 * i + 1) * P, OFF_GB + 2 * i * P, OFF_GB + (2 * i + 1) * P)
            return wsrc(w_in, at[j])

        def by_two(w):
            return lambda i, j: wsrc(w, (2 * i + j) * P)

        a_t, b_t, c_t = by_two(w_a), by_two(w_b), by_two(w_out)
        first = [pair_tiles(0, j) for j in range(4)]
        ssd_first = [ssd_tiles(0, j) for j in range(4)]
        up_first = [wsrc(w, f * P) for f in range(2) for w in (A.w_gate[0], A.w_up[0])]

        def four(t):
            return [t(0, 0), t(0, 1), t(1, 0), t(1, 1)]

        with ExitStack() as tmp:
            S.tmp = tmp.enter_context(nc.sbuf_tensor("mask_tmp", [P, P], F32))
            stage_prologue(nc, S, A, first)
        dt_tile = wsrc(w_in, OFF_DT)
        u = b = ba = bv = 0
        stage_pairs(nc, S, A, b, u, pair_tiles, [dt_tile] + ssd_first[0:3])
        u, b, ba, t0 = u + 4 * NH // 2, b + 4 * NRB * NH // 2, ba + 4 * NRB * NH // 2, NTP * NH // 2
        stage_steps(nc, S, A, b, u, t0, lambda sp: S.W.load(sp, u + 4, 2, 0, ssd_first[3]))
        u, b = u + 1, b + NRB
        S.o_in = [sem(f"o_in{n}") for n in range(4)]
        S.stream = ctx.enter_context(nc.sbuf_tensor("stream", [P, 4, XP_COLS], F32))
        stage_ssd(nc, S, A, b, ba, u, t0, ssd_tiles, four(b_t))
        u, b = u + 8 * NG, b + 8 * NRB * NG
        S.ss = ctx.enter_context(nc.sbuf_tensor("sq_sums", [P, ROWS], F32))
        with ExitStack() as two:
            S.R1_hi = two.enter_context(nc.sbuf_tensor("operand1_hi", [P, KT, ROWS], F32R))
            S.R1_lo = two.enter_context(nc.sbuf_tensor("operand1_lo", [P, KT, ROWS], F32R))
            tiles, blocks = KT, KT * NRB
            stage_attention_out(nc, S, A, b, bv, u, b_t, four(a_t))
            stage_merge(nc, S, A, b + blocks, bv + blocks, u + tiles, a_t, four(c_t))
            stage_out(nc, S, A, b + 2 * blocks, bv + 2 * blocks, u + 2 * tiles, c_t, up_first)
            u, b, bv = u + 3 * tiles, b + 3 * blocks, bv + 3 * blocks
        with ExitStack() as late:
            S.x_t = late.enter_context(nc.sbuf_tensor("x_t", [P, KT, ROWS], F32))
            stage_ffn(nc, S, A, b, bv, u, [ple_tile(A, d, j) for d in range(2) for j in range(2)])
            blocks = (2 * FT + KT * FT // 2) * NRB
            stage_ple(nc, S, A, b + blocks, bv + blocks, u + 3 * FT)
            stage_final(nc, S, A)


_INS = ["x_prompt", "x_sample", "cache_k", "cache_v", "state_conv", "state_ssm", "p_prompt", "p_sample",
        "norm_mix_g", "w_in", "conv_w", "conv_b", "dt_bias", "a_log", "d_skip", "mnorm_g", "w_a", "w_b", "w_out",
        "norm_ffn_g", "w_gate", "w_up", "w_down", "norm_ple_g", "w_ple_gate", "w_ple", "final_norm_g"]

_OUTS = [((1, SEQ, D), "y_prompt"), ((NB, TD, D), "y_sample"),
         ((1, 1, NH, SEQ, HD), "new_k_prompt"), ((1, 1, NH, SEQ, HD), "new_v_prompt"),
         ((1, 1, 3, XBC), "new_conv_prompt"), ((1, 1, NH, HD, NS), "new_ssm_prompt"),
         ((1, NB, NH, TD, HD), "new_k_sample"), ((1, NB, NH, TD, HD), "new_v_sample"),
         ((1, NB, 3, XBC), "new_conv_sample"), ((1, NB, NH, HD, NS), "new_ssm_sample")]


def kernel(**inputs):
    import numpy as _np
    import concourse.bacc as _bacc
    from concourse import mybir as _mybir
    from concourse.bass_utils import run_bass_kernel_spmd as _run

    nc = _bacc.Bacc("TRN2", target_bir_lowering=False, num_devices=1)
    arrays, A = {}, Store()
    for name in _INS:
        a = _np.ascontiguousarray(inputs[name])
        arrays[f"in_{name}"] = a
        A.__dict__[name] = nc.dram_tensor(f"in_{name}", a.shape, _mybir.dt.from_np(a.dtype), kind="ExternalInput").ap()
    for shape, name in _OUTS:
        A.__dict__[name] = nc.dram_tensor(f"out_{name}", shape, _mybir.dt.float32, kind="ExternalOutput").ap()
    hybrid_step(nc, A)
    r = _run(nc, [arrays], core_ids=[0])
    return tuple(r.results[0][f"out_{name}"] for _, name in _OUTS)
```
